# Optimizing a Trainium2 kernel written in Bass

```python
import math
import jax, jax.numpy as jnp
from jax import lax
import numpy as np

D_MODEL = 1024
BATCH = 1
SEQ = 512
DEPTH = 2

N_MEM = 256
A_HEADS = 8
A_HEAD_DIM = 64
A_WIDTH = A_HEADS * A_HEAD_DIM
KV_RANK = 128
IDX_HEADS = 8
IDX_DIM = 32
TOPK_MAX = 256
Q_BLOCK = 128
POOL_WINDOWS = (2, 4, 8, 16)
N_POOL_GROUPS = 4
POOL_GROUP = 64
POOL_WIDTH = N_POOL_GROUPS * POOL_GROUP
C_HEADS = 4
C_HEAD_DIM = 64
C_WIDTH = C_HEADS * C_HEAD_DIM
N_BRANCH = 3
REL_BUCKETS = 32
REL_MAX_DIST = 128
D_FF = 2816
EPS = 1e-6
NEG = -1e30

IN_SPLITS = (A_WIDTH, KV_RANK, IDX_HEADS * IDX_DIM, IDX_DIM, IDX_HEADS,
             POOL_WIDTH, C_WIDTH, N_BRANCH * D_MODEL)
IN_WIDTH = sum(IN_SPLITS)

kernel_name = "hybrid_dsa_pool_memattn_macaron"

def _split_points(sizes):
    pts, acc = [], 0
    for s in sizes[:-1]:
        acc += s
        pts.append(acc)
    return pts

def rmsnorm(x, g):
    xf = x.astype(jnp.float32)
    y = xf * lax.rsqrt(jnp.mean(xf * xf, axis=-1, keepdims=True) + EPS)
    return (y * g.astype(jnp.float32)).astype(x.dtype)

def swiglu(x, w_in, w_out):
    a, b = jnp.split(x @ w_in, 2, axis=-1)
    return (jax.nn.silu(a) * b) @ w_out

def t5_bucket(dist):
    max_exact = REL_BUCKETS // 2
    n = jnp.maximum(dist, 0)
    nf = jnp.maximum(n, 1).astype(jnp.float32)
    large = max_exact + (jnp.log(nf / max_exact) / math.log(REL_MAX_DIST / max_exact)
                         * (REL_BUCKETS - max_exact)).astype(jnp.int32)
    large = jnp.minimum(large, REL_BUCKETS - 1)
    return jnp.where(n < max_exact, n, large)

def dsa_attention(q, c_kv, iq, ik, iw, w_uk, w_uv, rel_bias):
    B, S = q.shape[0], q.shape[1]
    k_sel = min(TOPK_MAX, S // 4)
    n_blk = S // Q_BLOCK
    q_lat = jnp.einsum('bshd,rhd->bshr', q, w_uk)
    key_pos = jnp.arange(S)
    scale = A_HEAD_DIM ** -0.5
    idx_scale = IDX_DIM ** -0.5
    w_scale = IDX_HEADS ** -0.5

    def block(i):
        start = i * Q_BLOCK
        qp = start + jnp.arange(Q_BLOCK)
        iq_b = lax.dynamic_slice_in_dim(iq, start, Q_BLOCK, axis=1)
        iw_b = lax.dynamic_slice_in_dim(iw, start, Q_BLOCK, axis=1)
        ql_b = lax.dynamic_slice_in_dim(q_lat, start, Q_BLOCK, axis=1)
        dots = jax.nn.relu(jnp.einsum('bqhd,bkd->bqhk', iq_b, ik) * idx_scale)
        score = jnp.einsum('bqh,bqhk->bqk', iw_b * w_scale, dots).astype(jnp.float32)
        causal = key_pos[None, :] <= qp[:, None]
        score = jnp.where(causal[None], score, -jnp.inf)
        _, idx = lax.top_k(score, k_sel)
        valid = idx <= qp[None, :, None]
        c_sel = jax.vmap(lambda c, j: c[j])(c_kv, idx)
        logits = jnp.einsum('bqhr,bqkr->bqhk', ql_b, c_sel).astype(jnp.float32) * scale
        bias = rel_bias[t5_bucket(qp[None, :, None] - idx)]
        logits = logits + jnp.transpose(bias, (0, 1, 3, 2)).astype(jnp.float32)
        logits = jnp.where(valid[:, :, None, :], logits, NEG)
        p = jax.nn.softmax(logits, axis=-1).astype(c_sel.dtype)
        o_lat = jnp.einsum('bqhk,bqkr->bqhr', p, c_sel)
        return jnp.einsum('bqhr,rhd->bqhd', o_lat, w_uv)

    out = lax.map(block, jnp.arange(n_blk))
    return jnp.moveaxis(out, 0, 1).reshape(B, S, A_WIDTH)

def pool_mixer(z, w_pool, pool_scale):
    B, S, C = z.shape
    zf = z.astype(jnp.float32)
    cs = jnp.cumsum(zf, axis=1)
    wmax = max(POOL_WINDOWS)
    cs_pad = jnp.pad(cs, ((0, 0), (wmax, 0), (0, 0)))
    pos = jnp.arange(1, S + 1, dtype=jnp.float32)
    outs = []
    for g, w in enumerate(POOL_WINDOWS):
        lo, hi = g * POOL_GROUP, (g + 1) * POOL_GROUP
        win_sum = cs[:, :, lo:hi] - cs_pad[:, wmax - w: wmax - w + S, lo:hi]
        count = jnp.minimum(pos, float(w))[None, :, None]
        pooled = win_sum / count - zf[:, :, lo:hi]
        outs.append(jnp.einsum('bsc,cd->bsd', pooled.astype(z.dtype), w_pool[g]))
    return jnp.concatenate(outs, axis=-1) * pool_scale

def mem_attention(qc, mem_n, w_mem_kv):
    B, S = qc.shape[0], qc.shape[1]
    M = mem_n.shape[1]
    k, v = jnp.split(mem_n @ w_mem_kv, 2, axis=-1)
    q = qc.reshape(B, S, C_HEADS, C_HEAD_DIM)
    k = k.reshape(B, M, C_HEADS, C_HEAD_DIM)
    v = v.reshape(B, M, C_HEADS, C_HEAD_DIM)
    logits = jnp.einsum('bshd,bmhd->bhsm', q, k).astype(jnp.float32) * C_HEAD_DIM ** -0.5
    p = jax.nn.softmax(logits, axis=-1).astype(v.dtype)
    return jnp.einsum('bhsm,bmhd->bshd', p, v).reshape(B, S, C_WIDTH)

def setup_inputs(seed: int = 0) -> dict:
    key = jax.random.key(seed)
    ks = jax.random.split(key, 24)
    f32 = jnp.float32
    L = DEPTH

    def nrm(k, shape, fan_in):
        return jax.random.normal(k, shape, f32) * fan_in ** -0.5

    def gain(k, shape):
        return 1.0 + 0.05 * jax.random.normal(k, shape, f32)

    return {
        "x": jax.random.normal(ks[0], (BATCH, SEQ, D_MODEL), f32),
        "mem": jax.random.normal(ks[1], (BATCH, N_MEM, D_MODEL), f32),
        "rel_bias": 0.5 * jax.random.normal(ks[2], (REL_BUCKETS, A_HEADS), f32),
        "ffn1_norm": gain(ks[3], (L, D_MODEL)),
        "ffn1_w_in": nrm(ks[4], (L, D_MODEL, 2 * D_FF), D_MODEL),
        "ffn1_w_out": nrm(ks[5], (L, D_FF, D_MODEL), D_FF),
        "mix_norm": gain(ks[6], (L, D_MODEL)),
        "w_in": nrm(ks[7], (L, D_MODEL, IN_WIDTH), D_MODEL),
        "kv_norm": gain(ks[8], (L, KV_RANK)),
        "w_uk": nrm(ks[9], (L, KV_RANK, A_HEADS, A_HEAD_DIM), KV_RANK),
        "w_uv": nrm(ks[10], (L, KV_RANK, A_HEADS, A_HEAD_DIM), KV_RANK),
        "w_pool": nrm(ks[11], (L, N_POOL_GROUPS, POOL_GROUP, POOL_GROUP), POOL_GROUP),
        "pool_scale": gain(ks[12], (L, POOL_WIDTH)),
        "mem_norm": gain(ks[13], (L, D_MODEL)),
        "w_mem_kv": nrm(ks[14], (L, D_MODEL, 2 * C_WIDTH), D_MODEL),
        "w_branch_a": nrm(ks[15], (L, A_WIDTH, D_MODEL), A_WIDTH),
        "w_branch_b": nrm(ks[16], (L, POOL_WIDTH, D_MODEL), POOL_WIDTH),
        "w_branch_c": nrm(ks[17], (L, C_WIDTH, D_MODEL), C_WIDTH),
        "w_out": nrm(ks[18], (L, D_MODEL, D_MODEL), D_MODEL),
        "ffn2_norm": gain(ks[19], (L, D_MODEL)),
        "ffn2_w_in": nrm(ks[20], (L, D_MODEL, 2 * D_FF), D_MODEL),
        "ffn2_w_out": nrm(ks[21], (L, D_FF, D_MODEL), D_FF),
        "final_norm": gain(ks[22], (D_MODEL,)),
    }

def reference(x, mem, rel_bias, ffn1_norm, ffn1_w_in, ffn1_w_out, mix_norm, w_in, kv_norm,
              w_uk, w_uv, w_pool, pool_scale, mem_norm, w_mem_kv, w_branch_a, w_branch_b,
              w_branch_c, w_out, ffn2_norm, ffn2_w_in, ffn2_w_out, final_norm):
    B, S, D = x.shape
    split_pts = _split_points(IN_SPLITS)
    h = x
    for l in range(DEPTH):
        h = h + 0.5 * swiglu(rmsnorm(h, ffn1_norm[l]), ffn1_w_in[l], ffn1_w_out[l])

        u = rmsnorm(h, mix_norm[l])
        q_a, c_kv, iq, ik, iw, z_pool, q_c, gate_pre = jnp.split(u @ w_in[l], split_pts, axis=-1)
        q_a = q_a.reshape(B, S, A_HEADS, A_HEAD_DIM)
        c_kv = rmsnorm(c_kv, kv_norm[l])
        iq = iq.reshape(B, S, IDX_HEADS, IDX_DIM)

        y_a = dsa_attention(q_a, c_kv, iq, ik, iw, w_uk[l], w_uv[l], rel_bias)
        y_b = pool_mixer(z_pool, w_pool[l], pool_scale[l])
        y_c = mem_attention(q_c, rmsnorm(mem, mem_norm[l]), w_mem_kv[l])

        g = jax.nn.sigmoid(gate_pre).reshape(B, S, N_BRANCH, D)
        merged = (g[:, :, 0] * (y_a @ w_branch_a[l])
                  + g[:, :, 1] * (y_b @ w_branch_b[l])
                  + g[:, :, 2] * (y_c @ w_branch_c[l]))
        h = h + merged @ w_out[l]

        h = h + 0.5 * swiglu(rmsnorm(h, ffn2_norm[l]), ffn2_w_in[l], ffn2_w_out[l])
    return rmsnorm(h, final_norm)


_drawn_inputs = setup_inputs


def setup_inputs(seed=0):
    import zlib

    import numpy as np

    out = dict(_drawn_inputs(seed))
    spreads = {}
    factors = {'kv_norm': 4.947, 'mem_norm': 8.0}
    for name, (base, spread) in spreads.items():
        noise = np.random.default_rng([zlib.crc32(name.encode()), seed]).standard_normal(out[name].shape)
        drawn = base * np.exp(spread * noise) if base else spread * noise
        out[name] = __import__('jax').numpy.asarray(drawn.astype(out[name].dtype))
    for name, factor in factors.items():
        out[name] = (out[name] * factor).astype(out[name].dtype)
    return out
```

```python
import math
from contextlib import ExitStack

import numpy as np

import concourse.bass as bass
from concourse import mybir

F32 = mybir.dt.float32
F32R = mybir.dt.float32r
ALU = mybir.AluOpType
ACT = mybir.ActivationFunctionType
AX = mybir.AxisListType

P = 128
D = 1024
T = 512
L = 2
M = 256
KD = D // P
QB = T // P
H = 8
HD = 64
R = 128
IH = 8
ID = 32
CH = 4
TOPK = 128
FF = 2816
FC = FF // P
BUCKETS = 32
MAXDIST = 128
EPS = 1e-6
NEG = -1e30
PICKED = -3e38
WINDOWS = (2, 4, 8, 16)
WMAX = max(WINDOWS)

RAW_SLOTS, SPLIT_SLOTS, BANKS = 4, 2, 4
HALF = (12, 10)
U_FFN = 2 * sum(HALF) + 2 * 16
C_FFN = 2 * sum(HALF) + 2 * 8
U_MEM, C_MEM = U_FFN, C_FFN
U_IN, C_IN = U_MEM + 4, C_MEM + 4
N_IN = 20
U_GBC, C_GBC = U_IN + N_IN, C_IN + N_IN
U_BA, C_BA = U_GBC + 3 * KD, C_GBC + 4 * KD
U_WO, C_WO = U_BA + KD, C_BA + KD
U_FFN2, C_FFN2 = U_WO + KD, C_WO + KD
UNITS, CHUNKS = U_FFN2 + U_FFN, C_FFN2 + C_FFN
assert UNITS % RAW_SLOTS == 0 and CHUNKS % BANKS == 0

G_MIX, G_FFN2, G_NEXT, G_MEM, G_KV, G_POOL = 0, 8, 16, 24, 32, 33
W_POOL, W_UK, W_UV, N_PAR = 35, 163, 675, 1187
K_ID, K_ONE, K_CAUSAL, K_COUNT, K_GAIN, N_CONST = 0, 128, 256, 384, 416, 424

N_SCORES = 3 * IH
NBIAS = 384


def attention_steps():
    s = [("C", qb, hp) for qb in range(QB) for hp in range(2)] + [("B", 0, 0), ("B", 1, 0)]
    s += [("Q", 0, 0), ("Q", 0, 1)]
    late = None
    for qb in range(QB):
        a = [("A", qb, h) for h in range(H)]
        if late:
            a.insert(2, late)
        at = a.index(("A", qb, 3))
        if qb + 1 < QB:
            a.insert(at + 1, ("Q", qb + 1, 0))
            a.append(("Q", qb + 1, 1))
        at = a.index(("A", qb, 3))
        a.insert(at + 4, ("U", qb, 0))
        late = ("U", qb, 1)
        s += a
    return s + [("N", 0, 0)] * 3 + [late]


STEPS = attention_steps()
SOFTMAX = [i for i, s in enumerate(STEPS) if s[0] in "AC"]
N_SOFT = len(SOFTMAX)
KIND_INDEX = [sum(1 for t in STEPS[:i] if t[0] == s[0]) for i, s in enumerate(STEPS)]
S_USES = [("score", s) for s in range(N_SCORES)] + [("step", i) for i, s in enumerate(STEPS) if s[0] != "N"]
S_INDEX = {u: n for n, u in enumerate(S_USES)}
LAG = 3


def slot_plan():
    slots = [("in", i) for i in range(N_IN)]
    for f in range(KD):
        slots += [("in", N_IN + 2 * f), ("in", N_IN + 2 * f + 1), ("bc", f)]
    plan, at, scored, rounds = {}, 0, 0, 0
    for s in slots:
        scores, steps = [], []
        if s[0] == "in" and 4 <= s[1] < 12:
            scores = list(range(scored, scored + 3))
            scored += 3
        if s[0] == "bc" or s[1] >= 12:
            n = 2 if s[0] == "in" else 1
            steps = list(range(at, min(at + n, len(STEPS))))
            at += len(steps)
        picks = 2 if s[0] == "bc" or s[1] >= 8 else 0
        plan[s] = (scores, steps, picks)
    assert scored == N_SCORES
    return slots, plan, list(range(at, len(STEPS) + LAG))


SLOTS, PLAN, TAIL = slot_plan()


def head(n):
    return 2 * (n % 4) + n // 4


def bucket_of(n):
    exact = BUCKETS // 2
    nf = np.maximum(n, 1).astype(np.float32)
    large = exact + (np.log(nf / np.float32(exact)) / np.float32(math.log(MAXDIST / exact))
                     * np.float32(BUCKETS - exact)).astype(np.int32)
    return np.where(n < exact, n, np.minimum(large, BUCKETS - 1))


def constants():
    c = np.zeros((P, N_CONST), np.float32)
    c[:, K_ID:K_ID + P] = np.eye(P)
    c[:, K_ONE:K_ONE + P] = 1.0
    c[:, K_CAUSAL:K_CAUSAL + P] = np.where(np.arange(P)[None, :] <= np.arange(P)[:, None], 0.0, NEG)
    for g, w in enumerate(WINDOWS):
        rows = slice(64 * (g % 2), 64 * (g % 2) + 64)
        first = 1.0 / np.minimum(np.arange(1, WMAX + 1), w)
        c[rows, K_COUNT + WMAX * (g // 2):K_COUNT + WMAX * (g // 2) + WMAX] = first
    buckets = bucket_of(np.maximum(255 - np.arange(NBIAS), 0))
    hot = (np.arange(BUCKETS)[:, None] == buckets[None, :]).astype(np.float32)
    return c, hot


def trunk(nc, xT, memT, wA, wB0, wB1, wM, wR, par, const, hot, rel, out, bias_rows):
    ctx = ExitStack()
    with ctx:
        def sb(name, shape, dt=F32, scope=ctx):
            return scope.enter_context(nc.sbuf_tensor(name, shape, dt))

        def sem(name):
            return ctx.enter_context(nc.semaphore(name))

        h = sb("h", [P, KD, T])
        u1H, u1L = sb("u1H", [P, KD, T], F32R), sb("u1L", [P, KD, T], F32R)
        raw = sb("raw", [P, RAW_SLOTS, 8 * P])
        wH = sb("wH", [P, SPLIT_SLOTS, 8 * P], F32R)
        wL = sb("wL", [P, SPLIT_SLOTS, 8 * P], F32R)
        near_bias = sb("near_bias", [P, H, 2 * P])
        far_bias = sb("far_bias", [P, H])
        cst = sb("cst", [P, N_CONST])
        pr = sb("pr", [P, N_PAR])
        rms = sb("rms", [P, T])
        mem_rms = sb("mem_rms", [P, M])
        ssq = sb("ssq", [P, T])
        sq = sb("sq", [P, T])
        ta = sb("ta", [P, T])
        tb = sb("tb", [P, T])
        sg = sb("sg", [P, 2, T])
        iw = sb("iw", [P, QB, IH])
        top8 = sb("top8", [P, 8])
        nmax = sb("nmax", [P, 4, 2])
        rsum = sb("rsum", [P, 4, 2])
        rinv = sb("rinv", [P, 4, 2])
        with ExitStack() as ffn:
            u0H, u0L = sb("u0H", [P, KD, T], F32R, ffn), sb("u0L", [P, KD, T], F32R, ffn)
            hidH = sb("hidH", [P, HALF[0], T], F32R, ffn)
            hidL = sb("hidL", [P, HALF[0], T], F32R, ffn)
            mem = sb("mem", [P, KD, M], F32, ffn)
        with ExitStack() as mix:
            yH, yL = sb("yH", [P, KD, T], F32R, mix), sb("yL", [P, KD, T], F32R, mix)
            gate_a = sb("gate_a", [P, KD, T], F32, mix)
            qc = sb("qc", [P, 2, T], F32, mix)
            kc = sb("kc", [P, 2, M], F32, mix)
            vc = sb("vc", [P, 2, M], F32, mix)
            z = sb("z", [P, 2, T], F32, mix)
            za = sb("za", [P, 2, T], F32, mix)
            iq = sb("iq", [P, 2, T], F32, mix)
            q = sb("q", [P, QB, T], F32, mix)
            qlat = sb("qlat", [P, H, P], F32, mix)
            probs = sb("probs", [P, 3, T], F32, mix)
            ckv = sb("ckv", [P, T], F32, mix)
            relu = sb("relu", [P, 2, T], F32, mix)
            picks = [None] + [sb(f"picks{b}", [P, P * (b + 1)], F32, mix) for b in range(1, QB)]
        with ExitStack() as late:
            sb("hole0", [P, 2, KD, T], F32, late)
            sb("hole1", [P, KD, T], F32, late)
            part = sb("part", [P, KD, T], F32, late)
            gate_bc = sb("gate_bc", [P, 2, T], F32, late)
        mem_hi = yH[:, 0:4, :].rearrange("p a (b m) -> p (a b) m", m=M)
        mem_lo = yL[:, 0:4, :].rearrange("p a (b m) -> p (a b) m", m=M)
        c_tok = ssq[:, :].rearrange("p (b r) -> p b r", r=R)
        zb = relu
        olat = relu[:, 0, :]
        pt = sg
        misc = ta
        ik = sq
        iwT = probs[0:8, 1, :]
        ckv_sq = probs[:, 0, :]
        ckv_rms = probs[:, 2, :]
        ident = cst[:, K_ID:K_ID + P]
        ones = cst[:, K_ONE:K_ONE + P]
        causal = cst[:, K_CAUSAL:K_CAUSAL + P]

        rel_sb = q[0:BUCKETS, 1, 0:H]
        bias_table = gate_a[:, 0:6, :].rearrange("p a t -> p (a t)").rearrange("p (h n) -> p h n", n=NBIAS)

        def masks(qb):
            return causal if qb == 0 else picks[qb][:, :]

        def gain(at, k):
            return pr[:, bass.ds(at + k, 1)]

        bank = [ctx.enter_context(nc.psum_tensor(f"bank{i}", [P, 512], F32)) for i in range(BANKS)]
        sbank = [ctx.enter_context(nc.psum_tensor(f"sbank{i}", [P, 512], F32)) for i in range(2)]
        tbank = ctx.enter_context(nc.psum_tensor("tbank", [P, 512], F32))
        obank = ctx.enter_context(nc.psum_tensor("obank", [P, 512], F32))

        const_loaded = sem("const_loaded")
        rel_loaded = sem("rel_loaded")
        x_loaded = sem("x_loaded")
        mem_loaded = sem("mem_loaded")
        par_loaded = sem("par_loaded")
        raw_landed = [sem(f"raw_landed{s}") for s in range(RAW_SLOTS)]
        rounded = sem("rounded")
        split_done = sem("split_done")
        unit_used = sem("unit_used")
        evacuated = sem("evacuated")
        sigmoid_ready = sem("sigmoid_ready")
        gated = sem("gated")
        hidden_high = sem("hidden_high")
        hidden_ready = sem("hidden_ready")
        u_high = sem("u_high")
        squared = sem("squared")
        u_ready = sem("u_ready")
        ssq_added = sem("ssq_added")
        norm_sum = sem("norm_sum")
        norm_var = sem("norm_var")
        norm_root = sem("norm_root")
        bias_full = sem("bias_full")
        bias_copied = sem("bias_copied")
        bias_stored = sem("bias_stored")
        bias_loaded = sem("bias_loaded")
        mem_squared = sem("mem_squared")
        mem_ssq = sem("mem_ssq")
        mem_normed = sem("mem_normed")
        mem_high = sem("mem_high")
        mem_ready = sem("mem_ready")
        ik_ready = sem("ik_ready")
        iw_full = sem("iw_full")
        iw_ready = sem("iw_ready")
        ckv_squared = sem("ckv_squared")
        ckv_ready = sem("ckv_ready")
        c_full = sem("c_full")
        c_ready = sem("c_ready")
        s_full = sem("s_full")
        relu_ready = sem("relu_ready")
        score_added = sem("score_added")
        pooled = sem("pooled")
        yb_high = sem("yb_high")
        yb_ready = sem("yb_ready")
        logits_read = sem("logits_read")
        logit_max = sem("logit_max")
        exp_done = sem("exp_done")
        sum_inverted = sem("sum_inverted")
        probs_ready = sem("probs_ready")
        t_full = sem("t_full")
        pt_ready = sem("pt_ready")
        v_full = sem("v_full")
        yc_high = sem("yc_high")
        yc_ready = sem("yc_ready")
        qlat_ready = sem("qlat_ready")
        olat_ready = sem("olat_ready")
        ya_high = sem("ya_high")
        ya_ready = sem("ya_ready")
        gate_exp = sem("gate_exp")
        merged_sum = sem("merged_sum")
        merged_high = sem("merged_high")
        merged_ready = sem("merged_ready")
        out_ready = sem("out_ready")
        out_stored = [sem(f"out_stored{s}") for s in range(2)]
        vector_step = sem("vector_step")
        scalar_step = sem("scalar_step")

        def unit_at(l, u):
            return l * UNITS + (u + 1 + SPLIT_SLOTS)

        def chunk_at(l, c):
            return l * CHUNKS + (c + 1 + BANKS)

        def apart(eng, *waits):
            waits = [(s, eng.to_reg(value)) for s, value in waits]
            eng.wait_ge(const_loaded, 16)
            for s, value in waits:
                eng.wait_ge(s, value)

        class Steps:

            def __init__(self, eng, s):
                self.eng, self.s, self.n = eng, s, 0

            def done(self, ins):
                self.n += 1
                ins.then_inc(self.s, 1)

            def wait(self):
                self.eng.wait_ge(self.s, self.n)

            def restart(self):
                if self.n:
                    self.wait()
                self.eng.sem_clear(self.s)
                self.n = 0

        block = ctx.enter_context(nc.Block())

        @block.sync
        def _(sp):
            sp.dma_start(cst[:, :], const).then_inc(const_loaded, 16)
            sp.dma_start(h[:, :, :], xT).then_inc(x_loaded, 16)
            sp.dma_start(q[0:BUCKETS, 0, 0:NBIAS], hot).then_inc(rel_loaded, 16)
            sp.dma_start(q[0:BUCKETS, 1, 0:H], rel).then_inc(rel_loaded, 16)
            sp.dma_start(far_bias[:, :], bass.AP(tensor=rel.tensor, offset=(BUCKETS - 1) * H, ap=[[0, P], [1, H]])
                         ).then_inc(bias_loaded, 16)
            sp.dma_start(mem[:, :, :], memT).then_inc(mem_loaded, 16)

            with sp.Fori(0, L) as l:
                def units(src, per_layer, first, count, cols, unit):
                    with sp.Fori(0, count // RAW_SLOTS) as j:
                        for s in range(RAW_SLOTS):
                            sp.wait_ge(split_done, l * UNITS + j * RAW_SLOTS + (unit + s + 1))
                            n = l * per_layer + j * RAW_SLOTS + (first + s)
                            sp.dma_start(raw[:, s, 0:cols],
                                         src[bass.ds(n, 1), :, :].rearrange("a p n -> p (a n)")
                                         ).then_inc(raw_landed[s], 16)

                def ffn_units(f, unit):
                    units(wA, 88, 44 * f, 24, 1024, unit)
                    if f == 0:
                        sp.dma_start(pr[:, :], par[bass.ds(l, 1), :, :].rearrange("a p n -> p (a n)")
                                     ).then_inc(par_loaded, 16)
                        sp.wait_ge(norm_root, 1)
                        sp.dma_start(mem[:, :, :], memT).then_inc(mem_loaded, 16)
                    units(wB0, 32, 16 * f, 16, 768, unit + 24)
                    units(wA, 88, 44 * f + 24, 20, 1024, unit + 40)
                    units(wB1, 32, 16 * f, 16, 640, unit + 60)

                ffn_units(0, 0)
                units(wM, 48, 0, 24, 1024, U_MEM)
                with sp.Fori(0, 2) as j:
                    for i in range(12):
                        f, kind = i // 3, i % 3
                        s = (U_GBC + i) % RAW_SLOTS
                        sp.wait_ge(split_done, l * UNITS + j * 12 + (U_GBC + i + 1))
                        if kind < 2:
                            src = wM[bass.ds(l * 48 + j * 8 + (24 + 2 * f + kind), 1), :, :]
                        else:
                            src = wR[bass.ds(l * 16 + j * 4 + f, 1), :, :]
                        sp.dma_start(raw[:, s, 0:1024 if kind < 2 else 512],
                                     src.rearrange("a p n -> p (a n)")).then_inc(raw_landed[s], 16)
                units(wR, 16, KD, KD, 512, U_BA)
                units(wM, 48, 40, KD, 1024, U_WO)
                ffn_units(1, U_FFN2)

            for k in range(KD):
                sp.wait_ge(out_ready, k + 1)
                sp.dma_start(out[k], sg[:, k % 2, :]).then_inc(out_stored[k % 2], 16)
            for s in range(2):
                sp.wait_ge(out_stored[s], 16 * KD // 2)

        @block.gpsimd
        def _(pool):
            for _s in range(RAW_SLOTS):
                pool.sem_inc(split_done, 1)

            def split(l, group, unit, slot, cols):
                w = slot % SPLIT_SLOTS
                pool.wait_ge(raw_landed[slot], (l * (UNITS // RAW_SLOTS) + group) * 16 + 16)
                apart(pool, (unit_used, unit + 1))
                pool.tensor_scalar(wH[:, w, 0:cols], raw[:, slot, 0:cols], 1.0, 0.0, ALU.mult, ALU.add
                                   ).then_inc(rounded, 1)
                pool.wait_ge(rounded, unit + 1)
                pool.tensor_tensor(wL[:, w, 0:cols], raw[:, slot, 0:cols], wH[:, w, 0:cols].bitcast(F32),
                                   ALU.subtract).then_inc(split_done, 1)

            with pool.Fori(0, L) as l:
                def units(first, count, cols):
                    with pool.Fori(0, count // RAW_SLOTS) as j:
                        for s in range(RAW_SLOTS):
                            split(l, j + first // RAW_SLOTS, l * UNITS + j * RAW_SLOTS + (first + s), s, cols)

                def ffn_units(first):
                    units(first, 24, 1024)
                    units(first + 24, 16, 768)
                    units(first + 40, 20, 1024)
                    units(first + 60, 16, 640)

                ffn_units(0)
                units(U_MEM, 24, 1024)
                with pool.Fori(0, 2) as j:
                    for i in range(12):
                        split(l, j * 3 + (U_GBC + i) // RAW_SLOTS, l * UNITS + j * 12 + (U_GBC + i),
                              (U_GBC + i) % RAW_SLOTS, 1024 if i % 3 < 2 else 512)
                units(U_BA, KD, 512)
                units(U_WO, KD, 1024)
                ffn_units(U_FFN2)

        @block.tensor
        def _(pe):
            for _s in range(SPLIT_SLOTS):
                pe.sem_inc(unit_used, 1)

            def take_unit(unit):
                pe.wait_ge(split_done, unit + 1 + RAW_SLOTS)

            def free_bank(chunk):
                pe.wait_ge(evacuated, chunk + 1)

            def exact(dst, w, tiles, hi, lo, first=True, last=True, before=None):
                for i, (t, k) in enumerate(tiles):
                    if before:
                        before(k)
                    a, b = wH[:, w, t * P:(t + 1) * P], wL[:, w, t * P:(t + 1) * P]
                    pe.matmul(dst, a, hi[:, k, :], start=first and i == 0, stop=False)
                    pe.matmul(dst, b, hi[:, k, :], start=False, stop=False)
                    mm = pe.matmul(dst, a, lo[:, k, :], start=False, stop=last and i == len(tiles) - 1)
                return mm

            def sum_rows(src, n, cols=T):
                if n is not None:
                    pe.wait_ge(norm_var, n - 1)
                pe.matmul(obank[:, 0:cols], ones, src, start=True, stop=True).then_inc(norm_sum, 1)

            pe.wait_ge(const_loaded, 16)
            pe.wait_ge(rel_loaded, 32)
            for hd in range(H):
                if hd >= 2:
                    pe.wait_ge(bias_copied, hd - 1)
                pe.matmul(sbank[hd % 2][:, 0:NBIAS], bass.AP(tensor=rel_sb.tensor, offset=rel_sb.offset + hd,
                                                             ap=[rel_sb.ap[0], [0, P]]),
                          q[0:BUCKETS, 0, 0:NBIAS], start=True, stop=True).then_inc(bias_full, 1)
            pe.wait_ge(mem_ssq, KD)
            sum_rows(ta[:, 0:M], None, M)

            with pe.Fori(0, L) as l:
                def ffn(unit, chunk, u_from, hid_from, ssq_count, norm_n):
                    def hidden(j, u, c, first):
                        for i in range(4):
                            n, m = l * UNITS + j * 4 + (u + i), l * CHUNKS + j * 4 + (c + i)
                            take_unit(n)
                            free_bank(m)
                            ready = None
                            if first and i == 0:
                                def ready(k):
                                    pe.wait_ge(u_ready, l * 24 + (u_from + k + 1))
                            exact(bank[i][:, :], i % 2, [(k, k) for k in range(KD)], u0H, u0L,
                                  before=ready).then_inc(unit_used, 1)
                            if first and i == 0:
                                pe.wait_ge(ssq_added, l * 24 + ssq_count)
                                sum_rows(ssq[:, :], l * 4 + norm_n)

                    def outs(u, c, n_hid, hid):
                        half = n_hid // 2
                        with pe.Fori(0, 2) as j:
                            for i in range(4):
                                free_bank(l * CHUNKS + j * 4 + (c + i))
                                for part_ in range(2):
                                    take_unit(l * UNITS + j * 8 + (u + 2 * i + part_))
                                    tiles = [(t, t + half * part_) for t in range(half)]
                                    ready = None
                                    if i == 0:
                                        def ready(k):
                                            pe.wait_ge(hidden_ready, l * 44 + (hid + k + 1))
                                    exact(bank[i][:, :], part_, tiles, hidH, hidL, first=part_ == 0,
                                          last=part_ == 1, before=ready).then_inc(unit_used, 1)

                    hidden(0, unit, chunk, True)
                    with pe.Fori(1, HALF[0] // 2) as j:
                        hidden(j, unit, chunk, False)
                    outs(unit + 24, chunk + 24, HALF[0], hid_from)
                    with pe.Fori(0, HALF[1] // 2) as j:
                        hidden(j, unit + 40, chunk + 32, False)
                    outs(unit + 60, chunk + 52, HALF[1], hid_from + HALF[0])

                ffn(0, 0, 0, 0, 8, 2)

                for i in range(4):
                    take_unit(l * UNITS + (U_MEM + i))
                    if i < 3:
                        free_bank(l * CHUNKS + (C_MEM + i))
                    w = i % 2
                    if i < 2:
                        for k in range(KD):
                            pe.wait_ge(mem_ready, l * KD + (k + 1))
                            a, b = wH[:, w, k * P:(k + 1) * P], wL[:, w, k * P:(k + 1) * P]
                            pe.matmul(bank[i][:, 0:M], a, mem_hi[:, k, :], start=k == 0, stop=False)
                            pe.matmul(bank[i][:, 0:M], b, mem_hi[:, k, :], start=False, stop=False)
                            mm = pe.matmul(bank[i][:, 0:M], a, mem_lo[:, k, :], start=False, stop=k == KD - 1)
                    else:
                        if i == 2:
                            free_bank(l * CHUNKS + (C_MEM + 3))
                        for mb in range(2):
                            rows = slice(mb * P, (mb + 1) * P)
                            for t in range(4):
                                k = 4 * (i - 2) + t
                                a, b = wH[:, w, t * M:(t + 1) * M], wL[:, w, t * M:(t + 1) * M]
                                dst = bank[2 + mb][:, 0:M]
                                pe.matmul(dst, mem_hi[:, k, rows], a, start=k == 0, stop=False)
                                pe.matmul(dst, mem_hi[:, k, rows], b, start=False, stop=False)
                                mm = pe.matmul(dst, mem_lo[:, k, rows], a, start=False, stop=k == KD - 1)
                    mm.then_inc(unit_used, 1)
                    if i == 0:
                        pe.wait_ge(ssq_added, l * 24 + 16)
                        sum_rows(ssq[:, :], l * 4 + 3)

                def s_bank_free(use):
                    n = S_INDEX[use]
                    if n < 2:
                        return n % 2, ()
                    kind, i = S_USES[n - 2]
                    if kind == "score":
                        return n % 2, (relu_ready, l * N_SCORES + (i + 1))
                    step, at = STEPS[i][0], KIND_INDEX[i] + 1
                    return n % 2, {"A": lambda: (logits_read, l * 32 + at),
                                   "C": lambda: (exp_done, l * N_SOFT + (SOFTMAX.index(i) + 1)),
                                   "Q": lambda: (qlat_ready, l * 8 + at),
                                   "U": lambda: (ya_ready, l * 8 + at),
                                   "B": lambda: (yb_ready, l * 2 + at)}[step]()

                def score(s):
                    qb, hd = 1 + s // IH, s % IH
                    g = slice(ID * (hd % 4), ID * (hd % 4) + ID)
                    width = P * (qb + 1)
                    if s == 0:
                        pe.wait_ge(evacuated, chunk_at(l, C_IN + 3))
                    n, free = s_bank_free(("score", s))
                    if free:
                        pe.wait_ge(*free)
                    dst = sbank[n]
                    pe.matmul(dst[:, 0:width], iq[g, hd // 4, qb * P:(qb + 1) * P], ik[g, 0:width],
                              start=True, stop=True).then_inc(s_full, 1)

                def logits(i):
                    kind, a, b = STEPS[i]
                    if kind == "N":
                        return
                    n, free = s_bank_free(("step", i))
                    if kind != "B":
                        pe.wait_ge(*free)
                    dst = sbank[n]
                    if kind == "C":
                        if i == 0:
                            pe.wait_ge(evacuated, chunk_at(l, C_IN + 9))
                        rows = slice(64 * b, 64 * b + 64)
                        for j in range(2):
                            mm = pe.matmul(dst[:, j * M:(j + 1) * M], qc[rows, j, a * P:(a + 1) * P],
                                           kc[rows, j, :], start=True, stop=True)
                    elif kind == "B":
                        apart(pe, free, (pooled, l * 4 + 4))
                        for j in range(2):
                            rows = slice(64 * j, 64 * j + 64)
                            mm = pe.matmul(dst[rows, :], pr[rows, W_POOL + 64 * a:W_POOL + 64 * a + 64],
                                           (za, zb)[j][rows, a, :], start=True, stop=True)
                    elif kind == "Q":
                        rows = slice(64 * b, 64 * b + 64)
                        for j in range(4):
                            mm = pe.matmul(dst[:, j * P:(j + 1) * P], pr[rows, W_UK + P * j:W_UK + P * (j + 1)],
                                           q[rows, j, a * P:(a + 1) * P], start=True, stop=True)
                    elif kind == "A":
                        pe.wait_ge(qlat_ready, l * 8 + (2 * a + b // 4 + 1))
                        width = P * (a + 1)
                        mm = pe.matmul(dst[:, 0:width], qlat[:, b, :], ckv[:, 0:width], start=True, stop=True)
                    elif kind == "U":
                        pe.wait_ge(olat_ready, l * 8 + (2 * a + b + 1))
                        for j in range(4):
                            hd = head(4 * b + j)
                            mm = pe.matmul(dst[64 * b:64 * b + 64, j * P:(j + 1) * P],
                                           pr[:, W_UV + HD * hd:W_UV + HD * hd + HD],
                                           olat[:, j * P:(j + 1) * P], start=True, stop=True)
                    mm.then_inc(s_full, 1)

                def turn(i):
                    kind, a, b = STEPS[i]
                    m = SOFTMAX.index(i)
                    pe.wait_ge(probs_ready, l * N_SOFT + (m + 1))
                    if m:
                        pe.wait_ge(pt_ready, l * N_SOFT + m)
                    else:
                        pe.wait_ge(c_ready, l + 1)
                    n = 4 if kind == "C" else a + 1
                    for kb in range(n):
                        mm = pe.transpose(tbank[:, kb * P:(kb + 1) * P],
                                          probs[:, m % 3, kb * P:(kb + 1) * P], ident)
                    mm.then_inc(t_full, 1)

                def values(i):
                    kind, a, b = STEPS[i]
                    m = SOFTMAX.index(i)
                    pe.wait_ge(pt_ready, l * N_SOFT + (m + 1))
                    if kind == "C":
                        if m:
                            pe.wait_ge(yc_ready, l * 8 + m)
                        for j in range(2):
                            for mb in range(2):
                                mm = pe.matmul(obank[64 * b:64 * b + 64, j * P:(j + 1) * P],
                                               vc[:, mb, (2 * j + b) * HD:(2 * j + b + 1) * HD],
                                               pt[:, m % 2, (2 * j + mb) * P:(2 * j + mb + 1) * P],
                                               start=mb == 0, stop=mb == 1)
                    else:
                        if b % 4 == 0:
                            g = 2 * a + b // 4
                            if g:
                                pe.wait_ge(olat_ready, l * 8 + g)
                            else:
                                pe.wait_ge(yc_ready, l * 8 + 8)
                        region = slice((b % 4) * P, (b % 4) * P + P)
                        for kb in range(a + 1):
                            mm = pe.matmul(obank[:, region], c_tok[:, kb, :],
                                           pt[:, m % 2, kb * P:(kb + 1) * P], start=kb == 0, stop=kb == a)
                    mm.then_inc(v_full, 1)

                def step(i):
                    if i < len(STEPS):
                        logits(i)
                    if i >= 2 and i - 2 in SOFTMAX:
                        turn(i - 2)
                    if i >= 3 and i - 3 in SOFTMAX:
                        values(i - 3)

                for at in SLOTS:
                    kind, i = at
                    if kind == "in":
                        off = i if i < N_IN else N_IN + 3 * ((i - N_IN) // 2) + (i - N_IN) % 2
                        cof = i if i < N_IN else N_IN + 4 * ((i - N_IN) // 2) + (i - N_IN) % 2
                        take_unit(l * UNITS + (U_IN + off))
                        free_bank(l * CHUNKS + (C_IN + cof))
                        ready = None
                        if i == 0:
                            def ready(k):
                                pe.wait_ge(u_ready, l * 24 + (8 + k + 1))
                        exact(bank[(C_IN + cof) % BANKS][:, :], (U_IN + off) % 2,
                              [(k, k) for k in range(KD)], u1H, u1L, before=ready).then_inc(unit_used, 1)
                    else:
                        take_unit(l * UNITS + (U_GBC + 3 * i + 2))
                        w = (U_GBC + 3 * i + 2) % 2
                        c = C_GBC + 4 * i + 2
                        free_bank(l * CHUNKS + (c + 1))
                        if i == 0:
                            pe.wait_ge(yb_ready, l * 2 + 2)
                            pe.wait_ge(yc_ready, l * 8 + 8)
                        exact(bank[c % BANKS][:, :], w, [(0, 4), (1, 5)], yH, yL)
                        exact(bank[(c + 1) % BANKS][:, :], w, [(2, 6), (3, 7)], yH, yL).then_inc(unit_used, 1)
                    scores, steps, _ = PLAN[at]
                    if at == ("in", 2):
                        apart(pe, (ik_ready, l * 5 + 5))
                        for qb in range(QB):
                            mm = pe.transpose(tbank[:, qb * IH:(qb + 1) * IH], iwT[:, qb * P:(qb + 1) * P],
                                              cst[0:8, K_ID:K_ID + 8])
                        mm.then_inc(iw_full, 1)
                        pe.wait_ge(ckv_squared, l + 1)
                        sum_rows(ckv_sq, l * 4 + 4)
                    if at == ("in", 5):
                        pe.wait_ge(ckv_ready, l + 1)
                        pe.wait_ge(iw_ready, l + 1)
                        for kb in range(QB):
                            mm = pe.transpose(tbank[:, kb * P:(kb + 1) * P], ckv[:, kb * P:(kb + 1) * P], ident)
                        mm.then_inc(c_full, 1)
                    for s in scores:
                        score(s)
                    for s in steps:
                        step(s)
                for s in TAIL:
                    step(s)

                for f in range(KD):
                    take_unit(l * UNITS + (U_BA + f))
                    free_bank(l * CHUNKS + (C_BA + f))
                    if f == 0:
                        pe.wait_ge(ya_ready, l * 8 + 8)
                    exact(bank[(C_BA + f) % BANKS][:, :], (U_BA + f) % 2, [(k, k) for k in range(4)],
                          yH, yL).then_inc(unit_used, 1)
                for f in range(KD):
                    take_unit(l * UNITS + (U_WO + f))
                    free_bank(l * CHUNKS + (C_WO + f))
                    ready = None
                    if f == 0:
                        def ready(k):
                            pe.wait_ge(merged_ready, l * KD + (k + 1))
                    exact(bank[(C_WO + f) % BANKS][:, :], (U_WO + f) % 2, [(k, k) for k in range(KD)],
                          u1H, u1L, before=ready).then_inc(unit_used, 1)

                ffn(U_FFN2, C_FFN2, 16, sum(HALF), 24, 5)

            pe.wait_ge(ssq_added, L * 24 + 8)
            sum_rows(ssq[:, :], L * 4 + 2)

        @block.scalar
        def _(act):
            own = Steps(act, scalar_step)

            def root(n, dst, src):
                act.wait_ge(norm_var, n)
                act.activation(dst, src, ACT.Sqrt).then_inc(norm_root, 1)

            def produce(l, k, n, g, hi):
                act.activation(hi[:, k, :], h[:, k, :], ACT.Copy, scale=g).then_inc(u_high, 1)
                act.wait_ge(ssq_added, n)
                act.activation(sq[:, :], h[:, k, :], ACT.Square).then_inc(squared, 1)

            act.wait_ge(const_loaded, 16)
            act.wait_ge(x_loaded, 16)
            for k in range(KD):
                act.activation(u0H[:, k, :], h[:, k, :], ACT.Copy,
                               scale=cst[:, K_GAIN + k:K_GAIN + k + 1]).then_inc(u_high, 1)
                if k:
                    act.wait_ge(ssq_added, k)
                act.activation(sq[:, :], h[:, k, :], ACT.Square).then_inc(squared, 1)
            act.wait_ge(mem_loaded, 16)
            for k in range(KD):
                if k >= 1:
                    act.wait_ge(mem_ssq, k)
                act.activation(tb[:, 0:M], mem[:, k, :], ACT.Square).then_inc(mem_squared, 1)
            for hd in range(H):
                act.wait_ge(bias_full, hd + 1)
                act.activation(bias_table[:, hd, :], sbank[hd % 2][:, 0:NBIAS], ACT.Copy).then_inc(bias_copied, 1)
            act.wait_ge(bias_copied, H)
            act.dma_start(bias_rows, bias_table).then_inc(bias_stored, 16)
            act.wait_ge(bias_stored, 16)
            act.dma_start(near_bias[:, :, :], bass.AP(tensor=bias_rows.tensor, offset=P - 1,
                                                      ap=[[H * NBIAS - 1, P], [NBIAS, H], [1, 2 * P]])
                          ).then_inc(bias_loaded, 16)
            root(1, tb[:, 0:M], ta[:, 0:M])

            with act.Fori(0, L) as l:
                def ffn(chunk, hid_from, root_n, hi, g, n_from):
                    def hidden(j, c, hid):
                        for i in range(2):
                            act.wait_ge(evacuated, chunk_at(l, c + 2 * i) + j * 4)
                            act.activation(sg[:, 0, :], ta[:, :], ACT.Sigmoid).then_inc(sigmoid_ready, 1)
                            apart(act, (gated, l * 44 + j * 2 + (hid + i + 1)))
                            act.activation(hidH[:, bass.ds(j * 2 + i, 1), :].rearrange("p a t -> p (a t)"),
                                           sg[:, 1, :], ACT.Copy).then_inc(hidden_high, 1)

                    root(l * 4 + root_n, tb[:, :], ta[:, :])
                    with act.Fori(0, HALF[0] // 2) as j:
                        hidden(j, chunk, hid_from)
                    with act.Fori(0, HALF[1] // 2) as j:
                        hidden(j, chunk + 32, hid_from + HALF[0])

                def last_half(chunk, n_from, g, hi):
                    with act.Fori(0, KD) as k:
                        apart(act, (evacuated, chunk_at(l, chunk + 52) + k))
                        kk = bass.ds(k, 1)
                        row = lambda t: t[:, kk, :].rearrange("p a t -> p (a t)")
                        act.activation(row(hi), row(h), ACT.Copy, scale=gain(g, k)).then_inc(u_high, 1)
                        apart(act, (ssq_added, l * 24 + k + n_from))
                        act.activation(sq[:, :], row(h), ACT.Square).then_inc(squared, 1)

                ffn(0, 0, 2, u1H, G_MIX, 8)
                act.wait_ge(mem_normed, l + 1)
                for k in range(KD):
                    act.activation(mem_hi[:, k, :], mem[:, k, :], ACT.Copy,
                                   scale=pr[:, G_MEM + k:G_MEM + k + 1]).then_inc(mem_high, 1)
                last_half(0, 8, G_MIX, u1H)

                root(l * 4 + 3, tb[:, :], ta[:, :])

                def exps(i):
                    kind, a, b = STEPS[i]
                    if kind == "N":
                        return
                    n = S_INDEX[("step", i)]
                    src = sbank[n % 2]
                    if kind == "A":
                        m = SOFTMAX.index(i)
                        width = P * (a + 1)
                        p = probs[:, m % 3, 0:width]
                        act.wait_ge(logit_max, l * N_SOFT + (m + 1))
                        act.activation(p, p, ACT.Exp, bias=nmax[:, m % 4, 0:1],
                                       accum_out=rsum[:, m % 4, 0:1]).then_inc(exp_done, 1)
                    elif kind == "C":
                        m = SOFTMAX.index(i)
                        act.wait_ge(logit_max, l * N_SOFT + (m + 1))
                        if m >= 3:
                            act.wait_ge(t_full, l * N_SOFT + (m - 2))
                        for j in range(2):
                            e = act.activation(probs[:, m % 3, j * M:(j + 1) * M], src[:, j * M:(j + 1) * M],
                                               ACT.Exp, bias=nmax[:, m % 4, j:j + 1],
                                               accum_out=rsum[:, m % 4, j:j + 1])
                        e.then_inc(exp_done, 1)
                    elif kind == "Q":
                        act.wait_ge(s_full, l * len(S_USES) + (n + 1))
                        act.activation(qlat[:, 4 * b:4 * b + 4, :].rearrange("p a t -> p (a t)"), src[:, :],
                                       ACT.Copy, scale=HD ** -0.5).then_inc(qlat_ready, 1)
                    elif kind == "U":
                        act.wait_ge(s_full, l * len(S_USES) + (n + 1))
                        rows = slice(64 * b, 64 * b + 64)
                        act.activation(yH[rows, 0:4, a * P:(a + 1) * P],
                                       src[rows, :].rearrange("p (a t) -> p a t", t=P),
                                       ACT.Copy).then_inc(ya_high, 1)
                    elif kind == "B":
                        act.wait_ge(s_full, l * len(S_USES) + (n + 1))
                        act.activation(yH[:, 4 + a, :], src[:, :], ACT.Copy,
                                       scale=pr[:, G_POOL + a:G_POOL + a + 1]).then_inc(yb_high, 1)

                def normalise(i):
                    kind, a, b = STEPS[i]
                    m = SOFTMAX.index(i)
                    act.wait_ge(sum_inverted, l * N_SOFT + (m + 1))
                    parts = [(0, P * (a + 1))] if kind == "A" else [(0, M), (M, 2 * M)]
                    for j, (x, y) in enumerate(parts):
                        e = act.activation(probs[:, m % 3, x:y], probs[:, m % 3, x:y], ACT.Copy,
                                           scale=rinv[:, m % 4, j:j + 1])
                    e.then_inc(probs_ready, 1)

                def take_turned(i):
                    kind, a, b = STEPS[i]
                    m = SOFTMAX.index(i)
                    width = 4 * P if kind == "C" else P * (a + 1)
                    act.wait_ge(t_full, l * N_SOFT + (m + 1))
                    if m >= 2:
                        act.wait_ge(v_full, l * N_SOFT + (m - 1))
                    act.activation(pt[:, m % 2, 0:width], tbank[:, 0:width], ACT.Copy).then_inc(pt_ready, 1)

                def take_values(i):
                    kind, a, b = STEPS[i]
                    m = SOFTMAX.index(i)
                    if kind == "C":
                        act.wait_ge(v_full, l * N_SOFT + (m + 1))
                        rows = slice(64 * b, 64 * b + 64)
                        act.activation(yH[rows, 6:8, a * P:(a + 1) * P],
                                       obank[rows, 0:2 * P].rearrange("p (a t) -> p a t", t=P),
                                       ACT.Copy).then_inc(yc_high, 1)
                    elif b % 4 == 3:
                        act.wait_ge(v_full, l * N_SOFT + (m + 1))
                        act.activation(olat, obank[:, :], ACT.Copy).then_inc(olat_ready, 1)

                def step(i):
                    if i < len(STEPS):
                        exps(i)
                    if i >= 1 and i - 1 in SOFTMAX:
                        normalise(i - 1)
                    if i >= 2 and i - 2 in SOFTMAX:
                        take_turned(i - 2)
                    if i >= 3 and i - 3 in SOFTMAX:
                        take_values(i - 3)

                n_gates = 0
                for at in SLOTS:
                    kind, i = at
                    scores, steps, _ = PLAN[at]
                    if at == ("in", 0):
                        act.wait_ge(evacuated, chunk_at(l, C_IN))
                        for g in range(4):
                            act.activation(ik[ID * g:ID * g + ID, :], misc[0:ID, :], ACT.Copy).then_inc(ik_ready, 1)
                        act.activation(iwT, misc[ID:ID + IH, :], ACT.Copy).then_inc(ik_ready, 1)
                    if at == ("in", 1):
                        act.wait_ge(evacuated, chunk_at(l, C_IN + 1))
                        act.activation(ckv_sq, ckv[:, :], ACT.Square).then_inc(ckv_squared, 1)
                    if at == ("in", 3):
                        root(l * 4 + 4, tb[:, :], ta[:, :])
                    if kind == "in" and i >= 12:
                        cof = i if i < N_IN else N_IN + 4 * ((i - N_IN) // 2) + (i - N_IN) % 2
                        g = gate_a[:, i - 12, :] if i < N_IN else gate_bc[:, i % 2, :]
                        act.wait_ge(evacuated, chunk_at(l, C_IN + cof))
                        own.done(act.activation(g, g, ACT.Exp, scale=-1.0))
                        own.wait()
                        act.activation(g, g, ACT.Copy, bias=1.0).then_inc(gate_exp, 1)
                    if at == ("in", 5):
                        act.wait_ge(c_full, l + 1)
                        act.activation(c_tok.rearrange("p b r -> p (b r)"), tbank[:, :], ACT.Copy
                                       ).then_inc(c_ready, 1)
                    for s in scores:
                        qb = 1 + s // IH
                        width = P * (qb + 1)
                        act.wait_ge(s_full, l * len(S_USES) + (s + 1))
                        if s >= 2:
                            act.wait_ge(score_added, l * N_SCORES + (s - 1))
                        act.activation(relu[:, s % 2, 0:width], sbank[s % 2][:, 0:width], ACT.Relu,
                                       scale=ID ** -0.5).then_inc(relu_ready, 1)
                    for s in steps:
                        step(s)
                for s in TAIL:
                    step(s)

                for f in range(KD):
                    act.wait_ge(merged_sum, l * KD + (f + 1))
                    act.activation(u1H[:, f, :], (tb, sg)[0][:, :], ACT.Copy).then_inc(merged_high, 1)
                for k in range(KD):
                    act.wait_ge(evacuated, chunk_at(l, C_WO + k))
                    act.activation(u0H[:, k, :], h[:, k, :], ACT.Copy,
                                   scale=pr[:, G_FFN2 + k:G_FFN2 + k + 1]).then_inc(u_high, 1)
                    act.wait_ge(ssq_added, l * 24 + (16 + k))
                    act.activation(sq[:, :], h[:, k, :], ACT.Square).then_inc(squared, 1)
                ffn(C_FFN2, sum(HALF), 5, u0H, G_NEXT, 24)
                last_half(C_FFN2, 24, G_NEXT, u0H)
                own.restart()
            root(L * 4 + 2, tb[:, :], ta[:, :])

        @block.vector
        def _(dve):
            own = Steps(dve, vector_step)
            for _b in range(BANKS):
                dve.sem_inc(evacuated, 1)

            def inverse_rms(n, dst, count, width, v, s):
                v, s = v[:, 0:width], s[:, 0:width]
                dve.wait_ge(norm_sum, n)
                dve.tensor_scalar(v, obank[:, 0:width], 1.0 / count, EPS, ALU.mult, ALU.add).then_inc(norm_var, 1)
                dve.wait_ge(norm_root, n)
                own.done(dve.reciprocal(dst, s))
                own.wait()
                own.done(dve.tensor_tensor(s, dst, dst, ALU.mult))
                own.wait()
                own.done(dve.tensor_tensor(s, s, v, ALU.mult))
                own.wait()
                own.done(dve.tensor_scalar(s, s, -0.5, 1.5, ALU.mult, ALU.add))
                own.wait()
                own.done(dve.tensor_tensor(dst, dst, s, ALU.mult))
                own.wait()

            own.done(dve.memset(ssq[:, :], 0.0))
            own.done(dve.memset(ta[:, 0:M], 0.0))
            own.wait()
            dve.wait_ge(x_loaded, 16)
            dve.wait_ge(const_loaded, 16)
            for k in range(KD):
                dve.wait_ge(u_high, k + 1)
                dve.scalar_tensor_tensor(u0L[:, k, :], h[:, k, :], cst[:, K_GAIN + k:K_GAIN + k + 1],
                                         u0H[:, k, :].bitcast(F32), ALU.mult, ALU.subtract).then_inc(u_ready, 1)
                dve.wait_ge(squared, k + 1)
                if k:
                    dve.wait_ge(ssq_added, k)
                dve.tensor_tensor(ssq[:, :], ssq[:, :], sq[:, :], ALU.add).then_inc(ssq_added, 1)
            for k in range(KD):
                dve.wait_ge(mem_squared, k + 1)
                if k:
                    dve.wait_ge(mem_ssq, k)
                dve.tensor_tensor(ta[:, 0:M], ta[:, 0:M], tb[:, 0:M], ALU.add).then_inc(mem_ssq, 1)
            inverse_rms(1, mem_rms[:, :], D, M, ta, tb)
            own.restart()

            with dve.Fori(0, L) as l:
                def ffn(unit, chunk, hid_from, norm_n):
                    def hidden(j, u, c, hid):
                        for i in range(2):
                            n = l * 44 + j * 2 + (hid + i + 1)
                            dve.wait_ge(unit_used, unit_at(l, u + 2 * i) + j * 4)
                            dve.tensor_tensor(ta[:, :], bank[2 * i][:, :], rms[:, :], ALU.mult).then_inc(evacuated, 1)
                            dve.wait_ge(unit_used, unit_at(l, u + 2 * i + 1) + j * 4)
                            dve.tensor_tensor(tb[:, :], bank[2 * i + 1][:, :], rms[:, :], ALU.mult
                                              ).then_inc(evacuated, 1)
                            dve.wait_ge(evacuated, chunk_at(l, c + 2 * i + 1) + j * 4)
                            dve.wait_ge(sigmoid_ready, n)
                            own.done(dve.tensor_tensor(ta[:, :], ta[:, :], sg[:, 0, :], ALU.mult))
                            own.wait()
                            dve.tensor_tensor(sg[:, 1, :], ta[:, :], tb[:, :], ALU.mult).then_inc(gated, 1)
                            dve.wait_ge(hidden_high, n)
                            kk = bass.ds(j * 2 + i, 1)
                            dve.tensor_tensor(hidL[:, kk, :].rearrange("p a t -> p (a t)"), sg[:, 1, :],
                                              hidH[:, kk, :].rearrange("p a t -> p (a t)").bitcast(F32),
                                              ALU.subtract).then_inc(hidden_ready, 1)
                        own.restart()

                    inverse_rms(l * 4 + norm_n, rms[:, :], D, T, ta, tb)
                    own.restart()
                    with dve.Fori(0, HALF[0] // 2) as j:
                        hidden(j, unit, chunk, hid_from)
                    with dve.Fori(0, 2) as j:
                        for i in range(4):
                            dve.wait_ge(unit_used, unit_at(l, unit + 24 + 2 * i + 1) + j * 8)
                            row = h[:, bass.ds(j * 4 + i, 1), :].rearrange("p a t -> p (a t)")
                            dve.scalar_tensor_tensor(row, bank[i][:, :], 0.5, row, ALU.mult, ALU.add
                                                     ).then_inc(evacuated, 1)
                    with dve.Fori(0, HALF[1] // 2) as j:
                        hidden(j, unit + 40, chunk + 32, hid_from + HALF[0])
                    dve.wait_ge(evacuated, chunk_at(l, chunk + 51))
                    own.done(dve.memset(ssq[:, :], 0.0))

                def finish_h(k, ps, c, scale, n, g, hi, lo):
                    row = (lambda t: t[:, k, :]) if isinstance(k, int) else (
                        lambda t: t[:, bass.ds(k, 1), :].rearrange("p a t -> p (a t)"))
                    dve.scalar_tensor_tensor(row(h), ps, scale, row(h), ALU.mult, ALU.add).then_inc(evacuated, 1)
                    dve.wait_ge(evacuated, c)
                    dve.wait_ge(u_high, n)
                    dve.scalar_tensor_tensor(row(lo), row(h), gain(g, k), row(hi).bitcast(F32),
                                             ALU.mult, ALU.subtract).then_inc(u_ready, 1)
                    dve.wait_ge(squared, n)
                    dve.wait_ge(ssq_added, n - 1)
                    dve.tensor_tensor(ssq[:, :], ssq[:, :], sq[:, :], ALU.add).then_inc(ssq_added, 1)

                def last_half(unit, chunk, n_from, g, hi, lo):
                    own.restart()
                    with dve.Fori(0, 2) as j:
                        for i in range(4):
                            dve.wait_ge(unit_used, unit_at(l, unit + 60 + 2 * i + 1) + j * 8)
                            finish_h(j * 4 + i, bank[i][:, :], chunk_at(l, chunk + 52 + i) + j * 4, 0.5,
                                     l * 24 + j * 4 + (n_from + i + 1), g, hi, lo)

                ffn(0, 0, 0, 2)
                dve.wait_ge(mem_loaded, l * 16 + 32)
                dve.wait_ge(unit_used, unit_at(l, 59))
                for k in range(KD):
                    ins = dve.tensor_tensor(mem[:, k, :], mem[:, k, :], mem_rms[:, :], ALU.mult)
                    if k < KD - 1:
                        own.done(ins)
                    else:
                        ins.then_inc(mem_normed, 1)
                dve.wait_ge(par_loaded, l * 16 + 16)
                for k in range(KD):
                    dve.wait_ge(mem_high, l * KD + (k + 1))
                    dve.scalar_tensor_tensor(mem_lo[:, k, :], mem[:, k, :], pr[:, G_MEM + k:G_MEM + k + 1],
                                             mem_hi[:, k, :].bitcast(F32), ALU.mult, ALU.subtract
                                             ).then_inc(mem_ready, 1)
                last_half(0, 0, 8, G_MIX, u1H, u1L)

                def mem_kv(i):
                    dve.wait_ge(unit_used, unit_at(l, U_MEM + (i if i < 2 else 3)))
                    dst = kc[:, i, :] if i < 2 else vc[:, i - 2, :]
                    dve.tensor_copy(dst, bank[i][:, 0:M]).then_inc(evacuated, 1)

                dve.wait_ge(bias_loaded, 32)
                mem_kv(0)
                inverse_rms(l * 4 + 3, rms[:, :], D, T, ta, tb)
                for i in range(1, 4):
                    mem_kv(i)

                rounds_done = [0]

                def pick_round():
                    qb, n = 1 + rounds_done[0] // (TOPK // 8), rounds_done[0] % (TOPK // 8)
                    rounds_done[0] += 1
                    own.done(dve.max(top8[:, :], picks[qb][:, :]))
                    own.wait()
                    own.done(dve.match_replace(picks[qb][:, :], top8[:, :], picks[qb][:, :], PICKED))
                    own.wait()
                    if n == TOPK // 8 - 1:
                        own.done(dve.tensor_scalar(picks[qb][:, :], picks[qb][:, :], PICKED, NEG,
                                                   ALU.not_equal, ALU.mult))
                        own.wait()

                def add_score(s):
                    qb, hd = 1 + s // IH, s % IH
                    width = P * (qb + 1)
                    dve.wait_ge(relu_ready, l * N_SCORES + (s + 1))
                    w = iw[:, qb, hd:hd + 1]
                    if hd == 0:
                        dve.tensor_scalar(picks[qb][:, :], relu[:, s % 2, 0:width], w, None, ALU.mult
                                          ).then_inc(score_added, 1)
                    else:
                        dve.wait_ge(score_added, l * N_SCORES + s)
                        dve.scalar_tensor_tensor(picks[qb][:, :], relu[:, s % 2, 0:width], w, picks[qb][:, :],
                                                 ALU.mult, ALU.add).then_inc(score_added, 1)
                    if hd == IH - 1:
                        dve.wait_ge(score_added, l * N_SCORES + (s + 1))
                        last = picks[qb][:, qb * P:(qb + 1) * P]
                        own.done(dve.tensor_tensor(last, last, causal, ALU.add))
                        own.wait()

                def window_means():
                    dve.wait_ge(evacuated, chunk_at(l, C_IN + 11))

                    def widen(dst, src, by):
                        own.done(dve.tensor_tensor(dst[:, :, by:T], src[:, :, by:T], src[:, :, 0:T - by], ALU.add))
                        own.done(dve.tensor_copy(dst[:, :, 0:by], src[:, :, 0:by]))
                        own.wait()

                    widen(za, z, 1)
                    widen(zb, za, 2)
                    widen(za[:, 1:2, :], zb[:, 1:2, :], 4)
                    widen(zb[64:128, 1:2, :], za[64:128, 1:2, :], 8)
                    for g, w in enumerate(WINDOWS):
                        rows, c = slice(64 * (g % 2), 64 * (g % 2) + 64), g // 2
                        s = (za, zb)[g % 2][rows, c, :]
                        count = cst[rows, K_COUNT + WMAX * c:K_COUNT + WMAX * (c + 1)]
                        own.done(dve.scalar_tensor_tensor(s[:, WMAX:T], s[:, WMAX:T], 1.0 / w, z[rows, c, WMAX:T],
                                                          ALU.mult, ALU.subtract))
                        own.done(dve.tensor_tensor(s[:, 0:WMAX], s[:, 0:WMAX], count, ALU.mult))
                        own.wait()
                        dve.tensor_tensor(s[:, 0:WMAX], s[:, 0:WMAX], z[rows, c, 0:WMAX], ALU.subtract
                                          ).then_inc(pooled, 1)

                def logits(i):
                    kind, a, b = STEPS[i]
                    if kind in "NQ":
                        return
                    n = S_INDEX[("step", i)]
                    src = sbank[n % 2]
                    if kind == "A":
                        m = SOFTMAX.index(i)
                        if i == 0 or b == 0:
                            while a and rounds_done[0] < a * (TOPK // 8):
                                pick_round()
                        width, near = P * (a + 1), P * max(a - 1, 0)
                        p, mask = probs[:, m % 3, :], masks(a)
                        read = l * 32 + (KIND_INDEX[i] + 1)
                        dve.wait_ge(s_full, l * len(S_USES) + (n + 1))
                        if m >= 3:
                            dve.wait_ge(t_full, l * N_SOFT + (m - 2))
                        ins = dve.tensor_tensor(p[:, near:width], src[:, near:width],
                                                near_bias[:, head(b), 2 * P - (width - near):2 * P], ALU.add)
                        if near:
                            own.done(ins)
                            dve.scalar_tensor_tensor(p[:, 0:near], src[:, 0:near], far_bias[:, head(b):head(b) + 1],
                                                     mask[:, 0:near], ALU.add, ALU.add).then_inc(logits_read, 1)
                            own.wait()
                        else:
                            ins.then_inc(logits_read, 1)
                        dve.wait_ge(logits_read, read)
                        own.done(dve.tensor_tensor(p[:, near:width], p[:, near:width], mask[:, near:width], ALU.add))
                        own.wait()
                        dve.tensor_reduce(nmax[:, m % 4, 0:1], p[:, 0:width], AX.X, ALU.max, negate=True
                                          ).then_inc(logit_max, 1)
                    elif kind == "C":
                        m = SOFTMAX.index(i)
                        dve.wait_ge(s_full, l * len(S_USES) + (n + 1))
                        dve.tensor_reduce(nmax[:, m % 4, :], src[:, :].rearrange("p (a t) -> p a t", a=2), AX.X,
                                          ALU.max, negate=True).then_inc(logit_max, 1)
                    elif kind == "U":
                        dve.wait_ge(ya_high, l * 8 + (KIND_INDEX[i] + 1))
                        rows = slice(64 * b, 64 * b + 64)
                        dve.tensor_tensor(yL[rows, 0:4, a * P:(a + 1) * P],
                                          src[rows, :].rearrange("p (a t) -> p a t", t=P),
                                          yH[rows, 0:4, a * P:(a + 1) * P].bitcast(F32), ALU.subtract
                                          ).then_inc(ya_ready, 1)
                    elif kind == "B":
                        dve.wait_ge(yb_high, l * 2 + (a + 1))
                        dve.scalar_tensor_tensor(yL[:, 4 + a, :], src[:, :], pr[:, G_POOL + a:G_POOL + a + 1],
                                                 yH[:, 4 + a, :].bitcast(F32), ALU.mult, ALU.subtract
                                                 ).then_inc(yb_ready, 1)

                def invert(i):
                    m = SOFTMAX.index(i)
                    n = 1 if STEPS[i][0] == "A" else 2
                    dve.wait_ge(exp_done, l * N_SOFT + (m + 1))
                    dve.reciprocal(rinv[:, m % 4, 0:n], rsum[:, m % 4, 0:n]).then_inc(sum_inverted, 1)

                def low_values(i):
                    kind, a, b = STEPS[i]
                    m = SOFTMAX.index(i)
                    if kind == "C":
                        dve.wait_ge(yc_high, l * 8 + (m + 1))
                        rows = slice(64 * b, 64 * b + 64)
                        dve.tensor_tensor(yL[rows, 6:8, a * P:(a + 1) * P],
                                          obank[rows, 0:2 * P].rearrange("p (a t) -> p a t", t=P),
                                          yH[rows, 6:8, a * P:(a + 1) * P].bitcast(F32), ALU.subtract
                                          ).then_inc(yc_ready, 1)

                def step(i):
                    if i < len(STEPS):
                        logits(i)
                    if i >= 1 and i - 1 in SOFTMAX:
                        invert(i - 1)
                    if i >= 3 and i - 3 in SOFTMAX:
                        low_values(i - 3)

                for at in SLOTS:
                    kind, i = at
                    scores, steps, n_picks = PLAN[at]
                    if kind == "in":
                        off = i if i < N_IN else N_IN + 3 * ((i - N_IN) // 2) + (i - N_IN) % 2
                        cof = i if i < N_IN else N_IN + 4 * ((i - N_IN) // 2) + (i - N_IN) % 2
                        src = bank[(C_IN + cof) % BANKS][:, :]
                        dve.wait_ge(unit_used, unit_at(l, U_IN + off))
                        if i == 0:
                            dve.tensor_tensor(misc[0:40, :], src[0:40, :], rms[0:40, :], ALU.mult
                                              ).then_inc(evacuated, 1)
                        elif 8 <= i < 10:
                            dve.scalar_tensor_tensor(qc[:, i - 8, :], src, HD ** -0.5, rms[:, :], ALU.mult,
                                                     ALU.mult).then_inc(evacuated, 1)
                        else:
                            dst = (ckv[:, :] if i == 1 else iq[:, i - 2, :] if i < 4 else q[:, i - 4, :] if i < 8
                                   else z[:, i - 10, :] if i < 12 else gate_a[:, i - 12, :] if i < N_IN
                                   else gate_bc[:, i % 2, :])
                            dve.tensor_tensor(dst, src, rms[:, :], ALU.mult).then_inc(evacuated, 1)
                    else:
                        dve.wait_ge(unit_used, unit_at(l, U_GBC + 3 * i + 2))
                        c = C_GBC + 4 * i + 2
                        dve.tensor_tensor(ta[:, :], bank[c % BANKS][:, :], gate_bc[:, 0, :], ALU.mult
                                          ).then_inc(evacuated, 1)
                        dve.tensor_tensor(tb[:, :], bank[(c + 1) % BANKS][:, :], gate_bc[:, 1, :], ALU.mult
                                          ).then_inc(evacuated, 1)
                        dve.wait_ge(evacuated, chunk_at(l, c + 1))
                        own.done(dve.tensor_tensor(part[:, i, :], ta[:, :], tb[:, :], ALU.add))
                        own.wait()
                    if at == ("in", 3):
                        dve.wait_ge(iw_full, l + 1)
                        dve.tensor_scalar(iw[:, :, :].rearrange("p a b -> p (a b)"), tbank[:, 0:QB * IH],
                                          IH ** -0.5, None, ALU.mult).then_inc(iw_ready, 1)
                        dve.wait_ge(iw_ready, l + 1)
                        dve.wait_ge(ik_ready, l * 5 + 5)
                        inverse_rms(l * 4 + 4, ckv_rms, R, T, ta, tb)
                        dve.scalar_tensor_tensor(ckv[:, :], ckv[:, :], pr[:, G_KV:G_KV + 1], ckv_rms,
                                                 ALU.mult, ALU.mult).then_inc(ckv_ready, 1)
                    for s in scores:
                        add_score(s)
                    if at == ("in", 12):
                        window_means()
                    for s in steps:
                        step(s)
                    for _r in range(n_picks):
                        if rounds_done[0] < 3 * (TOPK // 8):
                            pick_round()
                    if kind == "in" and i >= 12:
                        g = gate_a[:, i - 12, :] if i < N_IN else gate_bc[:, i % 2, :]
                        dve.wait_ge(gate_exp, l * 24 + (i - 11))
                        own.done(dve.reciprocal(g, g))
                        own.wait()
                for s in TAIL:
                    step(s)

                def merged_low(f):
                    dve.wait_ge(merged_high, l * KD + (f + 1))
                    dve.tensor_tensor(u1L[:, f, :], tb[:, :], u1H[:, f, :].bitcast(F32), ALU.subtract
                                      ).then_inc(merged_ready, 1)

                for f in range(KD):
                    dve.wait_ge(unit_used, unit_at(l, U_BA + f))
                    if f:
                        dve.wait_ge(merged_sum, l * KD + f)
                    dve.tensor_tensor(ta[:, :], bank[(C_BA + f) % BANKS][:, :], gate_a[:, f, :], ALU.mult
                                      ).then_inc(evacuated, 1)
                    if f:
                        merged_low(f - 1)
                        dve.wait_ge(merged_ready, l * KD + f)
                    dve.wait_ge(evacuated, chunk_at(l, C_BA + f))
                    dve.tensor_tensor(tb[:, :], ta[:, :], part[:, f, :], ALU.add).then_inc(merged_sum, 1)
                merged_low(KD - 1)
                own.done(dve.memset(ssq[:, :], 0.0))
                own.restart()
                for k in range(KD):
                    dve.wait_ge(unit_used, unit_at(l, U_WO + k))
                    finish_h(k, bank[(C_WO + k) % BANKS][:, :], chunk_at(l, C_WO + k), 1.0,
                             l * 24 + (16 + k + 1), G_FFN2, u0H, u0L)

                ffn(U_FFN2, C_FFN2, sum(HALF), 5)
                last_half(U_FFN2, C_FFN2, 24, G_NEXT, u0H, u0L)

            inverse_rms(L * 4 + 2, rms[:, :], D, T, ta, tb)
            for k in range(KD):
                own.done(dve.tensor_tensor(ta[:, :], u0H[:, k, :].bitcast(F32), u0L[:, k, :].bitcast(F32), ALU.add))
                own.wait()
                if k >= 2:
                    dve.wait_ge(out_stored[k % 2], 16 * (k // 2))
                dve.tensor_tensor(sg[:, k % 2, :], ta[:, :], rms[:, :], ALU.mult).then_inc(out_ready, 1)
                dve.wait_ge(out_ready, k + 1)


def tiles(w):
    k, n = w.shape
    return w.reshape(k // P, P, n // P, P).transpose(2, 1, 0, 3)


def lay_out(i):
    a = {n: np.asarray(v) for n, v in i.items()}
    cat, flat = np.concatenate, lambda t: t.reshape(t.shape[0], P, -1)
    wA, wB0, wB1, wM, wR, par = [], [], [], [], [], []
    per_part = lambda g: g.reshape(-1, P).T
    for l in range(L):
        for f in ("ffn1", "ffn2"):
            t = flat(tiles(a[f + "_w_in"][l]))
            wA.append(t.reshape(2, FC, P, -1).transpose(1, 0, 2, 3).reshape(2 * FC, P, -1))
            t = tiles(a[f + "_w_out"][l])
            for dst, x, y in ((wB0, 0, HALF[0]), (wB1, HALF[0], FC)):
                half = t[:, :, x:y].reshape(KD, P, 2, -1).transpose(0, 2, 1, 3)
                dst.append(half.reshape(2 * KD, P, -1))
        w = a["w_in"][l]
        at = {"q": 0, "ckv": 512, "iq": 640, "misc": 896, "z": 936, "qc": 1192, "gate": 1448}
        cols = [at["misc"], at["ckv"], at["iq"], at["iq"] + P] + [at["q"] + P * c for c in range(4)]
        cols += [at["qc"], at["qc"] + P, at["z"], at["z"] + P] + [at["gate"] + P * f for f in range(KD)]
        for f in range(KD):
            cols += [at["gate"] + D + P * f, at["gate"] + 2 * D + P * f]
        kv = a["w_mem_kv"][l]
        wM.append(flat(tiles(kv[:, 0:M])))
        wM.append(flat(kv[:, M:].reshape(2, 4, P, M).transpose(0, 2, 1, 3)))
        wM.append(cat([flat(tiles(w[:, c:c + P])) for c in cols]))
        wM.append(flat(tiles(a["w_out"][l])))
        wR.append(flat(cat([tiles(a["w_branch_b"][l]), tiles(a["w_branch_c"][l])], axis=2)))
        wR.append(flat(tiles(a["w_branch_a"][l])))
        after = a["ffn1_norm"][l + 1] if l + 1 < L else a["final_norm"]
        par.append(cat([
            per_part(a["mix_norm"][l]), per_part(a["ffn2_norm"][l]), per_part(after), per_part(a["mem_norm"][l]),
            per_part(a["kv_norm"][l]), per_part(a["pool_scale"][l]),
            a["w_pool"][l].reshape(2, 2, 64, 64).transpose(1, 2, 0, 3).reshape(P, -1),
            a["w_uk"][l].transpose(1, 2, 0).reshape(4, P, R).transpose(1, 0, 2).reshape(P, -1),
            a["w_uv"][l].reshape(R, -1)], axis=1)[None])
    const, hot = constants()
    const[:, K_GAIN:K_GAIN + KD] = per_part(a["ffn1_norm"][0])
    token = lambda x: np.ascontiguousarray(x[0].T.reshape(KD, P, -1).transpose(1, 0, 2))
    arrays = {"xT": token(a["x"]), "memT": token(a["mem"]), "wA": cat(wA), "wB0": cat(wB0), "wB1": cat(wB1),
              "wM": cat(wM), "wR": cat(wR), "par": cat(par), "const": const, "hot": hot, "rel": a["rel_bias"]}
    return {n: np.ascontiguousarray(v) for n, v in arrays.items()}


def kernel(**inputs):
    import concourse.bacc as _bacc
    from concourse.bass_utils import run_bass_kernel_spmd as _run

    nc = _bacc.Bacc("TRN2", target_bir_lowering=False, num_devices=1)
    arrays = {f"in_{n}": v for n, v in lay_out(inputs).items()}
    args = [nc.dram_tensor(n, v.shape, F32, kind="ExternalInput").ap() for n, v in arrays.items()]
    out = nc.dram_tensor("outT", (KD, P, T), F32, kind="ExternalOutput").ap()
    bias_rows = nc.dram_tensor("bias_rows", (P, H, NBIAS), F32, kind="Internal").ap()
    trunk(nc, *args, out, bias_rows)
    r = _run(nc, [arrays], core_ids=[0])
    return np.ascontiguousarray(r.results[0]["outT"].reshape(D, T).T)[None]
```

```python
import math
from contextlib import ExitStack

import numpy as np

import concourse.bass as bass
from concourse import mybir

F32 = mybir.dt.float32
F32R = mybir.dt.float32r
ALU = mybir.AluOpType
ACT = mybir.ActivationFunctionType
AX = mybir.AxisListType

P = 128
D = 1024
T = 512
L = 2
M = 256
KD = D // P
QB = T // P
H = 8
HD = 64
R = 128
IH = 8
ID = 32
CH = 4
TOPK = 128
FF = 2816
FC = FF // P
BUCKETS = 32
MAXDIST = 128
EPS = 1e-6
NEG = -1e30
PICKED = -3e38
WINDOWS = (2, 4, 8, 16)
WMAX = max(WINDOWS)

RAW_SLOTS, SPLIT_SLOTS, BANKS = 4, 2, 4
HALF = (12, 10)
U_FFN = 2 * sum(HALF) + 2 * 16
C_FFN = 2 * sum(HALF) + 2 * 8
U_MEM, C_MEM = U_FFN, C_FFN
U_IN, C_IN = U_MEM + 4, C_MEM + 4
N_IN = 20
U_GBC, C_GBC = U_IN + N_IN, C_IN + N_IN
U_BA, C_BA = U_GBC + 3 * KD, C_GBC + 4 * KD
U_WO, C_WO = U_BA + KD, C_BA + KD
U_FFN2, C_FFN2 = U_WO + KD, C_WO + KD
UNITS, CHUNKS = U_FFN2 + U_FFN, C_FFN2 + C_FFN
assert UNITS % RAW_SLOTS == 0 and CHUNKS % BANKS == 0

G_MIX, G_FFN2, G_NEXT, G_MEM, G_KV, G_POOL = 0, 8, 16, 24, 32, 33
W_POOL, W_UK, W_UV, N_PAR = 35, 163, 675, 1187
K_ID, K_ONE, K_CAUSAL, K_COUNT, K_GAIN, N_CONST = 0, 128, 256, 384, 416, 424

N_SCORES = 3 * IH
NBIAS = 384


def attention_steps():
    s = [("C", qb, hp) for qb in range(QB) for hp in range(2)] + [("B", 0, 0), ("B", 1, 0)]
    s += [("Q", 0, 0), ("Q", 0, 1)]
    late = None
    for qb in range(QB):
        a = [("A", qb, h) for h in range(H)]
        if late:
            a.insert(2, late)
        at = a.index(("A", qb, 3))
        if qb + 1 < QB:
            a.insert(at + 1, ("Q", qb + 1, 0))
            a.append(("Q", qb + 1, 1))
        at = a.index(("A", qb, 3))
        a.insert(at + 4, ("U", qb, 0))
        late = ("U", qb, 1)
        s += a
    return s + [("N", 0, 0)] * 3 + [late]


STEPS = attention_steps()
SOFTMAX = [i for i, s in enumerate(STEPS) if s[0] in "AC"]
N_SOFT = len(SOFTMAX)
KIND_INDEX = [sum(1 for t in STEPS[:i] if t[0] == s[0]) for i, s in enumerate(STEPS)]
SCORE_SLOTS = range(4, 10)
FIRST_STEPS = 10
S_USES = [("score", s) for s in range(N_SCORES)] + [("step", i) for i, s in enumerate(STEPS) if s[0] != "N"]
S_INDEX = {u: n for n, u in enumerate(S_USES)}


def slot_plan():
    slots = [("in", i) for i in range(N_IN)]
    for f in range(KD):
        slots += [("in", N_IN + 2 * f), ("in", N_IN + 2 * f + 1), ("bc", f)]
    plan, at, scored = {}, 0, 0
    per_slot = N_SCORES // len(SCORE_SLOTS)
    for s in slots:
        scores, steps = [], []
        if s[0] == "in" and s[1] in SCORE_SLOTS:
            scores = list(range(scored, scored + per_slot))
            scored += per_slot
        if s[0] == "bc" or s[1] >= FIRST_STEPS:
            n = 2 if s[0] == "in" else 1
            steps = list(range(at, min(at + n, len(STEPS))))
            at += len(steps)
        picks = 3 if s[0] == "bc" or s[1] >= SCORE_SLOTS.start + IH // per_slot else 0
        plan[s] = (scores, steps, picks)
    assert scored == N_SCORES
    return slots, plan, [list(range(i, min(i + 2, len(STEPS)))) for i in range(at, len(STEPS), 2)] + [[]]


SLOTS, PLAN, TAIL = slot_plan()


def head(n):
    return 2 * (n % 4) + n // 4


def bucket_of(n):
    exact = BUCKETS // 2
    nf = np.maximum(n, 1).astype(np.float32)
    large = exact + (np.log(nf / np.float32(exact)) / np.float32(math.log(MAXDIST / exact))
                     * np.float32(BUCKETS - exact)).astype(np.int32)
    return np.where(n < exact, n, np.minimum(large, BUCKETS - 1))


def constants():
    c = np.zeros((P, N_CONST), np.float32)
    c[:, K_ID:K_ID + P] = np.eye(P)
    c[:, K_ONE:K_ONE + P] = 1.0
    c[:, K_CAUSAL:K_CAUSAL + P] = np.where(np.arange(P)[None, :] <= np.arange(P)[:, None], 0.0, NEG)
    for g, w in enumerate(WINDOWS):
        rows = slice(64 * (g % 2), 64 * (g % 2) + 64)
        first = 1.0 / np.minimum(np.arange(1, WMAX + 1), w)
        c[rows, K_COUNT + WMAX * (g // 2):K_COUNT + WMAX * (g // 2) + WMAX] = first
    buckets = bucket_of(np.maximum(255 - np.arange(NBIAS), 0))
    hot = (np.arange(BUCKETS)[:, None] == buckets[None, :]).astype(np.float32)
    return c, hot


def trunk(nc, xT, memT, wA, wB0, wB1, wM, wR, par, const, hot, rel, out, bias_rows):
    ctx = ExitStack()
    with ctx:
        def sb(name, shape, dt=F32, scope=ctx):
            return scope.enter_context(nc.sbuf_tensor(name, shape, dt))

        def sem(name):
            return ctx.enter_context(nc.semaphore(name))

        h = sb("h", [P, KD, T])
        u1H, u1L = sb("u1H", [P, KD, T], F32R), sb("u1L", [P, KD, T], F32R)
        raw = sb("raw", [P, RAW_SLOTS, 8 * P])
        wH = sb("wH", [P, SPLIT_SLOTS, 8 * P], F32R)
        wL = sb("wL", [P, SPLIT_SLOTS, 8 * P], F32R)
        near_bias = sb("near_bias", [P, H, 2 * P])
        far_bias = sb("far_bias", [P, H])
        cst = sb("cst", [P, N_CONST])
        pr = sb("pr", [P, N_PAR])
        rms = sb("rms", [P, T])
        mem_rms = sb("mem_rms", [P, M])
        ssq = sb("ssq", [P, T])
        sq = sb("sq", [P, T])
        ta = sb("ta", [P, T])
        tb = sb("tb", [P, T])
        sg = sb("sg", [P, 2, T])
        iw = sb("iw", [P, QB, IH])
        top8 = sb("top8", [P, 8])
        nmax = sb("nmax", [P, 4, 2])
        rsum = sb("rsum", [P, 4, 2])
        rinv = sb("rinv", [P, 4, 2])
        with ExitStack() as ffn:
            u0H, u0L = sb("u0H", [P, KD, T], F32R, ffn), sb("u0L", [P, KD, T], F32R, ffn)
            hidH = sb("hidH", [P, HALF[0], T], F32R, ffn)
            hidL = sb("hidL", [P, HALF[0], T], F32R, ffn)
            mem = sb("mem", [P, KD, M], F32, ffn)
        with ExitStack() as mix:
            yH, yL = sb("yH", [P, KD, T], F32R, mix), sb("yL", [P, KD, T], F32R, mix)
            gate_a = sb("gate_a", [P, KD, T], F32, mix)
            qc = sb("qc", [P, 2, T], F32, mix)
            kc = sb("kc", [P, 2, M], F32, mix)
            vc = sb("vc", [P, 2, M], F32, mix)
            z = sb("z", [P, 2, T], F32, mix)
            za = sb("za", [P, 2, T], F32, mix)
            iq = sb("iq", [P, 2, T], F32, mix)
            q = sb("q", [P, QB, T], F32, mix)
            qlat = sb("qlat", [P, H, P], F32, mix)
            probs = sb("probs", [P, 3, T], F32, mix)
            ckv = sb("ckv", [P, T], F32, mix)
            relu = sb("relu", [P, 2, T], F32, mix)
            picks = [None] + [sb(f"picks{b}", [P, P * (b + 1)], F32, mix) for b in range(1, QB)]
        with ExitStack() as late:
            sb("hole0", [P, 2, KD, T], F32, late)
            sb("hole1", [P, KD, T], F32, late)
            part = sb("part", [P, KD, T], F32, late)
            gate_bc = sb("gate_bc", [P, 2, T], F32, late)
        mem_hi = yH[:, 0:4, :].rearrange("p a (b m) -> p (a b) m", m=M)
        mem_lo = yL[:, 0:4, :].rearrange("p a (b m) -> p (a b) m", m=M)
        c_tok = ssq[:, :].rearrange("p (b r) -> p b r", r=R)
        zb = relu
        olat = relu[:, 0, :]
        pt = sg
        misc = ta
        ik = sq
        iwT = probs[0:8, 1, :]
        ckv_sq = probs[:, 0, :]
        ckv_rms = probs[:, 2, :]
        ident = cst[:, K_ID:K_ID + P]
        ones = cst[:, K_ONE:K_ONE + P]
        causal = cst[:, K_CAUSAL:K_CAUSAL + P]

        rel_sb = q[0:BUCKETS, 1, 0:H]
        bias_table = q[0:H, 2, 0:NBIAS]

        def masks(qb):
            return causal if qb == 0 else picks[qb][:, :]

        def gain(at, k):
            return pr[:, bass.ds(at + k, 1)]

        bank = [ctx.enter_context(nc.psum_tensor(f"bank{i}", [P, 512], F32)) for i in range(BANKS)]
        sbank = [ctx.enter_context(nc.psum_tensor(f"sbank{i}", [P, 512], F32)) for i in range(2)]
        tbank = ctx.enter_context(nc.psum_tensor("tbank", [P, 512], F32))
        obank = ctx.enter_context(nc.psum_tensor("obank", [P, 512], F32))

        const_loaded = sem("const_loaded")
        rel_loaded = sem("rel_loaded")
        x_loaded = [sem(f"x_loaded{i}") for i in range(4)]
        mem_loaded = sem("mem_loaded")
        par_loaded = sem("par_loaded")
        raw_landed = [sem(f"raw_landed{s}") for s in range(RAW_SLOTS)]
        rounded = sem("rounded")
        split_done = sem("split_done")
        unit_used = sem("unit_used")
        evacuated = sem("evacuated")
        sigmoid_ready = sem("sigmoid_ready")
        gated = sem("gated")
        hidden_high = sem("hidden_high")
        hidden_ready = sem("hidden_ready")
        u_high = sem("u_high")
        squared = sem("squared")
        u_ready = sem("u_ready")
        ssq_added = sem("ssq_added")
        norm_sum = sem("norm_sum")
        norm_var = sem("norm_var")
        norm_root = sem("norm_root")
        bias_full = sem("bias_full")
        bias_copied = sem("bias_copied")
        bias_stored = sem("bias_stored")
        bias_loaded = sem("bias_loaded")
        mem_squared = sem("mem_squared")
        mem_ssq = sem("mem_ssq")
        mem_normed = sem("mem_normed")
        mem_high = sem("mem_high")
        mem_ready = sem("mem_ready")
        ik_ready = sem("ik_ready")
        iw_full = sem("iw_full")
        iw_ready = sem("iw_ready")
        ckv_squared = sem("ckv_squared")
        ckv_ready = sem("ckv_ready")
        c_full = sem("c_full")
        c_ready = sem("c_ready")
        s_full = sem("s_full")
        relu_ready = sem("relu_ready")
        score_added = sem("score_added")
        pooled = sem("pooled")
        yb_high = sem("yb_high")
        yb_ready = sem("yb_ready")
        logits_read = sem("logits_read")
        logit_max = sem("logit_max")
        exp_done = sem("exp_done")
        sum_inverted = sem("sum_inverted")
        probs_ready = sem("probs_ready")
        t_full = sem("t_full")
        pt_ready = sem("pt_ready")
        v_full = sem("v_full")
        yc_high = sem("yc_high")
        yc_ready = sem("yc_ready")
        qlat_ready = sem("qlat_ready")
        olat_ready = sem("olat_ready")
        ya_high = sem("ya_high")
        ya_ready = sem("ya_ready")
        gate_exp = sem("gate_exp")
        gate_ready = sem("gate_ready")
        merged_sum = sem("merged_sum")
        merged_high = sem("merged_high")
        merged_ready = sem("merged_ready")
        out_ready = sem("out_ready")
        out_stored = [sem(f"out_stored{s}") for s in range(4)]
        vector_step = sem("vector_step")
        scalar_step = sem("scalar_step")

        def unit_at(l, u):
            return l * UNITS + (u + 1 + SPLIT_SLOTS)

        def chunk_at(l, c):
            return l * CHUNKS + (c + 1 + BANKS)

        def apart(eng, *waits):
            waits = [(s, eng.to_reg(value)) for s, value in waits]
            eng.wait_ge(const_loaded, 16)
            for s, value in waits:
                eng.wait_ge(s, value)

        class Steps:

            def __init__(self, eng, s):
                self.eng, self.s, self.n = eng, s, 0

            def done(self, ins):
                self.n += 1
                ins.then_inc(self.s, 1)

            def wait(self):
                self.eng.wait_ge(self.s, self.n)

            def restart(self):
                if self.n:
                    self.wait()
                self.eng.sem_clear(self.s)
                self.n = 0

        block = ctx.enter_context(nc.Block())

        @block.sync
        def _(sp):
            sp.dma_start(cst[:, :], const).then_inc(const_loaded, 16)
            sp.dma_start(q[0:BUCKETS, 0, 0:NBIAS], hot).then_inc(rel_loaded, 16)
            sp.dma_start(q[0:BUCKETS, 1, 0:H], rel).then_inc(rel_loaded, 16)
            sp.dma_start(far_bias[:, :], bass.AP(tensor=rel.tensor, offset=(BUCKETS - 1) * H, ap=[[0, P], [1, H]])
                         ).then_inc(bias_loaded, 16)

            with sp.Fori(0, L) as l:
                def units(src, per_layer, first, count, cols, unit):
                    with sp.Fori(0, count // RAW_SLOTS) as j:
                        for s in range(RAW_SLOTS):
                            sp.wait_ge(split_done, l * UNITS + j * RAW_SLOTS + (unit + s + 1))
                            n = l * per_layer + j * RAW_SLOTS + (first + s)
                            sp.dma_start(raw[:, s, 0:cols],
                                         src[bass.ds(n, 1), :, :].rearrange("a p n -> p (a n)")
                                         ).then_inc(raw_landed[s], 16)

                def ffn_units(f, unit):
                    units(wA, 88, 44 * f, 24, 1024, unit)
                    if f == 0:
                        sp.dma_start(pr[:, :], par[bass.ds(l, 1), :, :].rearrange("a p n -> p (a n)")
                                     ).then_inc(par_loaded, 16)
                        sp.dma_start(mem[:, :, :], memT).then_inc(mem_loaded, 16)
                    units(wB0, 32, 16 * f, 16, 768, unit + 24)
                    units(wA, 88, 44 * f + 24, 20, 1024, unit + 40)
                    units(wB1, 32, 16 * f, 16, 640, unit + 60)

                ffn_units(0, 0)
                units(wM, 48, 0, 24, 1024, U_MEM)
                with sp.Fori(0, 2) as j:
                    for i in range(12):
                        f, kind = i // 3, i % 3
                        s = (U_GBC + i) % RAW_SLOTS
                        sp.wait_ge(split_done, l * UNITS + j * 12 + (U_GBC + i + 1))
                        if kind < 2:
                            src = wM[bass.ds(l * 48 + j * 8 + (24 + 2 * f + kind), 1), :, :]
                        else:
                            src = wR[bass.ds(l * 16 + j * 4 + f, 1), :, :]
                        sp.dma_start(raw[:, s, 0:1024 if kind < 2 else 512],
                                     src.rearrange("a p n -> p (a n)")).then_inc(raw_landed[s], 16)
                units(wR, 16, KD, KD, 512, U_BA)
                units(wM, 48, 40, KD, 1024, U_WO)
                ffn_units(1, U_FFN2)

            for i in range(4):
                sp.wait_ge(out_ready, 2 * i + 2)
                sp.dma_start(out[:, 2 * i:2 * i + 2, :], gate_a[:, 2 * i:2 * i + 2, :]).then_inc(out_stored[i], 16)
            for i in range(4):
                sp.wait_ge(out_stored[i], 16)

        @block.gpsimd
        def _(pool):
            for _s in range(RAW_SLOTS):
                pool.sem_inc(split_done, 1)

            def split(l, group, unit, slot, cols):
                w = slot % SPLIT_SLOTS
                pool.wait_ge(raw_landed[slot], (l * (UNITS // RAW_SLOTS) + group) * 16 + 16)
                apart(pool, (unit_used, unit + 1))
                pool.tensor_scalar(wH[:, w, 0:cols], raw[:, slot, 0:cols], 1.0, 0.0, ALU.mult, ALU.add
                                   ).then_inc(rounded, 1)
                pool.wait_ge(rounded, unit + 1)
                pool.tensor_tensor(wL[:, w, 0:cols], raw[:, slot, 0:cols], wH[:, w, 0:cols].bitcast(F32),
                                   ALU.subtract).then_inc(split_done, 1)

            with pool.Fori(0, L) as l:
                def units(first, count, cols):
                    with pool.Fori(0, count // RAW_SLOTS) as j:
                        for s in range(RAW_SLOTS):
                            split(l, j + first // RAW_SLOTS, l * UNITS + j * RAW_SLOTS + (first + s), s, cols)

                def ffn_units(first):
                    units(first, 24, 1024)
                    units(first + 24, 16, 768)
                    units(first + 40, 20, 1024)
                    units(first + 60, 16, 640)

                ffn_units(0)
                units(U_MEM, 24, 1024)
                with pool.Fori(0, 2) as j:
                    for i in range(12):
                        split(l, j * 3 + (U_GBC + i) // RAW_SLOTS, l * UNITS + j * 12 + (U_GBC + i),
                              (U_GBC + i) % RAW_SLOTS, 1024 if i % 3 < 2 else 512)
                units(U_BA, KD, 512)
                units(U_WO, KD, 1024)
                ffn_units(U_FFN2)

        @block.tensor
        def _(pe):
            for _s in range(SPLIT_SLOTS):
                pe.sem_inc(unit_used, 1)
            pe.sem_inc(norm_var, 1)

            def take_unit(unit):
                pe.wait_ge(split_done, unit + 1 + RAW_SLOTS)

            def free_bank(chunk):
                pe.wait_ge(evacuated, chunk + 1)

            def exact(dst, w, tiles, hi, lo, first=True, last=True, before=None):
                for i, (t, k) in enumerate(tiles):
                    if before:
                        before(k)
                    a, b = wH[:, w, t * P:(t + 1) * P], wL[:, w, t * P:(t + 1) * P]
                    pe.matmul(dst, a, hi[:, k, :], start=first and i == 0, stop=False)
                    pe.matmul(dst, b, hi[:, k, :], start=False, stop=False)
                    mm = pe.matmul(dst, a, lo[:, k, :], start=False, stop=last and i == len(tiles) - 1)
                return mm

            def sum_rows(src, n, cols=T):
                pe.wait_ge(norm_var, n)
                pe.matmul(obank[:, 0:cols], ones, src, start=True, stop=True).then_inc(norm_sum, 1)

            pe.wait_ge(const_loaded, 16)
            pe.wait_ge(rel_loaded, 32)
            pe.matmul(sbank[0][0:H, 0:NBIAS], rel_sb, q[0:BUCKETS, 0, 0:NBIAS], start=True, stop=True
                      ).then_inc(bias_full, 1)

            with pe.Fori(0, L) as l:
                def ffn(unit, chunk, u_from, hid_from, ssq_count, norm_n):
                    def hidden(j, u, c, first):
                        for i in range(4):
                            n, m = l * UNITS + j * 4 + (u + i), l * CHUNKS + j * 4 + (c + i)
                            take_unit(n)
                            free_bank(m)
                            ready = None
                            if first and i == 0:
                                def ready(k):
                                    pe.wait_ge(u_ready, l * 24 + (u_from + k + 1))
                            exact(bank[i][:, :], i % 2, [(k, k) for k in range(KD)], u0H, u0L,
                                  before=ready).then_inc(unit_used, 1)
                            if first and i == 0:
                                pe.wait_ge(ssq_added, l * 24 + ssq_count)
                                sum_rows(ssq[:, :], l * 5 + norm_n)

                    def outs(u, c, n_hid, hid):
                        half = n_hid // 2
                        with pe.Fori(0, 2) as j:
                            for i in range(4):
                                free_bank(l * CHUNKS + j * 4 + (c + i))
                                for part_ in range(2):
                                    take_unit(l * UNITS + j * 8 + (u + 2 * i + part_))
                                    tiles = [(t, t + half * part_) for t in range(half)]
                                    ready = None
                                    if i == 0:
                                        def ready(k):
                                            pe.wait_ge(hidden_ready, l * 44 + (hid + k + 1))
                                    exact(bank[i][:, :], part_, tiles, hidH, hidL, first=part_ == 0,
                                          last=part_ == 1, before=ready).then_inc(unit_used, 1)

                    hidden(0, unit, chunk, True)
                    with pe.Fori(1, HALF[0] // 2) as j:
                        hidden(j, unit, chunk, False)
                    outs(unit + 24, chunk + 24, HALF[0], hid_from)
                    if unit == 0:
                        pe.wait_ge(mem_ssq, l * KD + KD)
                        sum_rows(ssq[:, 0:M], l * 5 + 2, M)
                    with pe.Fori(0, HALF[1] // 2) as j:
                        hidden(j, unit + 40, chunk + 32, False)
                    outs(unit + 60, chunk + 52, HALF[1], hid_from + HALF[0])

                ffn(0, 0, 0, 0, 8, 1)

                for i in range(4):
                    take_unit(l * UNITS + (U_MEM + i))
                    if i < 3:
                        free_bank(l * CHUNKS + (C_MEM + i))
                    w = i % 2
                    if i < 2:
                        for k in range(KD):
                            pe.wait_ge(mem_ready, l * KD + (k + 1))
                            a, b = wH[:, w, k * P:(k + 1) * P], wL[:, w, k * P:(k + 1) * P]
                            pe.matmul(bank[i][:, 0:M], a, mem_hi[:, k, :], start=k == 0, stop=False)
                            pe.matmul(bank[i][:, 0:M], b, mem_hi[:, k, :], start=False, stop=False)
                            mm = pe.matmul(bank[i][:, 0:M], a, mem_lo[:, k, :], start=False, stop=k == KD - 1)
                    else:
                        if i == 2:
                            free_bank(l * CHUNKS + (C_MEM + 3))
                        for mb in range(2):
                            rows = slice(mb * P, (mb + 1) * P)
                            for t in range(4):
                                k = 4 * (i - 2) + t
                                a, b = wH[:, w, t * M:(t + 1) * M], wL[:, w, t * M:(t + 1) * M]
                                dst = bank[2 + mb][:, 0:M]
                                pe.matmul(dst, mem_hi[:, k, rows], a, start=k == 0, stop=False)
                                pe.matmul(dst, mem_hi[:, k, rows], b, start=False, stop=False)
                                mm = pe.matmul(dst, mem_lo[:, k, rows], a, start=False, stop=k == KD - 1)
                    mm.then_inc(unit_used, 1)
                    if i == 0:
                        pe.wait_ge(ssq_added, l * 24 + 16)
                        sum_rows(ssq[:, :], l * 5 + 3)

                def s_bank_free(use):
                    n = S_INDEX[use]
                    if n < 2:
                        return n % 2, ()
                    kind, i = S_USES[n - 2]
                    if kind == "score":
                        return n % 2, (relu_ready, l * N_SCORES + (i + 1))
                    step, at = STEPS[i][0], KIND_INDEX[i] + 1
                    return n % 2, {"A": lambda: (logits_read, l * 32 + at),
                                   "C": lambda: (exp_done, l * N_SOFT + (SOFTMAX.index(i) + 1)),
                                   "Q": lambda: (qlat_ready, l * 8 + at),
                                   "U": lambda: (ya_ready, l * 8 + at),
                                   "B": lambda: (yb_ready, l * 2 + at)}[step]()

                def score(s):
                    qb, hd = 1 + s // IH, s % IH
                    g = slice(ID * (hd % 4), ID * (hd % 4) + ID)
                    width = P * (qb + 1)
                    if s == 0:
                        pe.wait_ge(evacuated, chunk_at(l, C_IN + 3))
                    n, free = s_bank_free(("score", s))
                    if free:
                        pe.wait_ge(*free)
                    dst = sbank[n]
                    pe.matmul(dst[:, 0:width], iq[g, hd // 4, qb * P:(qb + 1) * P], ik[g, 0:width],
                              start=True, stop=True).then_inc(s_full, 1)

                def logits(i):
                    kind, a, b = STEPS[i]
                    if kind == "N":
                        return
                    n, free = s_bank_free(("step", i))
                    if kind != "B":
                        pe.wait_ge(*free)
                    dst = sbank[n]
                    if kind == "C":
                        if i == 0:
                            pe.wait_ge(evacuated, chunk_at(l, C_IN + 9))
                        rows = slice(64 * b, 64 * b + 64)
                        for j in range(2):
                            mm = pe.matmul(dst[:, j * M:(j + 1) * M], qc[rows, j, a * P:(a + 1) * P],
                                           kc[rows, j, :], start=True, stop=True)
                    elif kind == "B":
                        apart(pe, free, (pooled, l * 4 + 4))
                        for j in range(2):
                            rows = slice(64 * j, 64 * j + 64)
                            mm = pe.matmul(dst[rows, :], pr[rows, W_POOL + 64 * a:W_POOL + 64 * a + 64],
                                           (za, zb)[j][rows, a, :], start=True, stop=True)
                    elif kind == "Q":
                        rows = slice(64 * b, 64 * b + 64)
                        for j in range(4):
                            mm = pe.matmul(dst[:, j * P:(j + 1) * P], pr[rows, W_UK + P * j:W_UK + P * (j + 1)],
                                           q[rows, j, a * P:(a + 1) * P], start=True, stop=True)
                    elif kind == "A":
                        pe.wait_ge(qlat_ready, l * 8 + (2 * a + b // 4 + 1))
                        width = P * (a + 1)
                        mm = pe.matmul(dst[:, 0:width], qlat[:, b, :], ckv[:, 0:width], start=True, stop=True)
                    elif kind == "U":
                        pe.wait_ge(olat_ready, l * 8 + (2 * a + b + 1))
                        for j in range(4):
                            hd = head(4 * b + j)
                            mm = pe.matmul(dst[64 * b:64 * b + 64, j * P:(j + 1) * P],
                                           pr[:, W_UV + HD * hd:W_UV + HD * hd + HD],
                                           olat[:, j * P:(j + 1) * P], start=True, stop=True)
                    mm.then_inc(s_full, 1)

                def turn(i):
                    kind, a, b = STEPS[i]
                    m = SOFTMAX.index(i)
                    pe.wait_ge(probs_ready, l * N_SOFT + (m + 1))
                    if m:
                        pe.wait_ge(pt_ready, l * N_SOFT + m)
                    else:
                        pe.wait_ge(c_ready, l + 1)
                    n = 4 if kind == "C" else a + 1
                    for kb in range(n):
                        mm = pe.transpose(tbank[:, kb * P:(kb + 1) * P],
                                          probs[:, m % 3, kb * P:(kb + 1) * P], ident)
                    mm.then_inc(t_full, 1)

                def values(i):
                    kind, a, b = STEPS[i]
                    m = SOFTMAX.index(i)
                    pe.wait_ge(pt_ready, l * N_SOFT + (m + 1))
                    if kind == "C":
                        if m:
                            pe.wait_ge(yc_ready, l * 8 + m)
                        for j in range(2):
                            for mb in range(2):
                                mm = pe.matmul(obank[64 * b:64 * b + 64, j * P:(j + 1) * P],
                                               vc[:, mb, (2 * j + b) * HD:(2 * j + b + 1) * HD],
                                               pt[:, m % 2, (2 * j + mb) * P:(2 * j + mb + 1) * P],
                                               start=mb == 0, stop=mb == 1)
                    else:
                        if b % 4 == 0:
                            g = 2 * a + b // 4
                            if g:
                                pe.wait_ge(olat_ready, l * 8 + g)
                            else:
                                pe.wait_ge(yc_ready, l * 8 + 8)
                        region = slice((b % 4) * P, (b % 4) * P + P)
                        for kb in range(a + 1):
                            mm = pe.matmul(obank[:, region], c_tok[:, kb, :],
                                           pt[:, m % 2, kb * P:(kb + 1) * P], start=kb == 0, stop=kb == a)
                    mm.then_inc(v_full, 1)

                def group(now, last):
                    last = [i for i in last if i in SOFTMAX]
                    for j in range(2):
                        if j < len(now):
                            logits(now[j])
                        if j < len(last):
                            turn(last[j])
                    for i in last:
                        values(i)

                last = []
                for at in SLOTS:
                    kind, i = at
                    if kind == "in":
                        off = i if i < N_IN else N_IN + 3 * ((i - N_IN) // 2) + (i - N_IN) % 2
                        cof = i if i < N_IN else N_IN + 4 * ((i - N_IN) // 2) + (i - N_IN) % 2
                        take_unit(l * UNITS + (U_IN + off))
                        free_bank(l * CHUNKS + (C_IN + cof))
                        ready = None
                        if i == 0:
                            def ready(k):
                                pe.wait_ge(u_ready, l * 24 + (8 + k + 1))
                        exact(bank[(C_IN + cof) % BANKS][:, :], (U_IN + off) % 2,
                              [(k, k) for k in range(KD)], u1H, u1L, before=ready).then_inc(unit_used, 1)
                    else:
                        take_unit(l * UNITS + (U_GBC + 3 * i + 2))
                        w = (U_GBC + 3 * i + 2) % 2
                        c = C_GBC + 4 * i + 2
                        free_bank(l * CHUNKS + (c + 1))
                        if i == 0:
                            pe.wait_ge(yb_ready, l * 2 + 2)
                            pe.wait_ge(yc_ready, l * 8 + 8)
                        exact(bank[c % BANKS][:, :], w, [(0, 4), (1, 5)], yH, yL)
                        exact(bank[(c + 1) % BANKS][:, :], w, [(2, 6), (3, 7)], yH, yL).then_inc(unit_used, 1)
                    scores, steps, _ = PLAN[at]
                    if at == ("in", 2):
                        apart(pe, (ik_ready, l * 5 + 5))
                        for qb in range(QB):
                            mm = pe.transpose(tbank[:, qb * IH:(qb + 1) * IH], iwT[:, qb * P:(qb + 1) * P],
                                              cst[0:8, K_ID:K_ID + 8])
                        mm.then_inc(iw_full, 1)
                        pe.wait_ge(ckv_squared, l + 1)
                        sum_rows(ckv_sq, l * 5 + 4)
                    if at == ("in", 5):
                        pe.wait_ge(ckv_ready, l + 1)
                        pe.wait_ge(iw_ready, l + 1)
                        for kb in range(QB):
                            mm = pe.transpose(tbank[:, kb * P:(kb + 1) * P], ckv[:, kb * P:(kb + 1) * P], ident)
                        mm.then_inc(c_full, 1)
                    for s in scores:
                        score(s)
                    if steps:
                        group(steps, last)
                        last = steps
                for steps in TAIL:
                    group(steps, last)
                    last = steps

                for f in range(KD):
                    take_unit(l * UNITS + (U_BA + f))
                    free_bank(l * CHUNKS + (C_BA + f))
                    if f == 0:
                        pe.wait_ge(ya_ready, l * 8 + 8)
                    exact(bank[(C_BA + f) % BANKS][:, :], (U_BA + f) % 2, [(k, k) for k in range(4)],
                          yH, yL).then_inc(unit_used, 1)
                for f in range(KD):
                    take_unit(l * UNITS + (U_WO + f))
                    free_bank(l * CHUNKS + (C_WO + f))
                    ready = None
                    if f == 0:
                        def ready(k):
                            pe.wait_ge(merged_ready, l * KD + (k + 1))
                    exact(bank[(C_WO + f) % BANKS][:, :], (U_WO + f) % 2, [(k, k) for k in range(KD)],
                          u1H, u1L, before=ready).then_inc(unit_used, 1)

                ffn(U_FFN2, C_FFN2, 16, sum(HALF), 24, 5)

            pe.wait_ge(ssq_added, L * 24 + 8)
            sum_rows(ssq[:, :], L * 5 + 1)

        @block.scalar
        def _(act):
            own = Steps(act, scalar_step)

            def root(n, dst, src):
                act.wait_ge(norm_var, n + 1)
                act.activation(dst, src, ACT.Sqrt).then_inc(norm_root, 1)

            def produce(l, k, n, g, hi):
                act.activation(hi[:, k, :], h[:, k, :], ACT.Copy, scale=g).then_inc(u_high, 1)
                act.wait_ge(ssq_added, n)
                act.activation(sq[:, :], h[:, k, :], ACT.Square).then_inc(squared, 1)

            for i in range(4):
                act.dma_start(h[:, 2 * i:2 * i + 2, :], xT[:, 2 * i:2 * i + 2, :]).then_inc(x_loaded[i], 16)
            act.wait_ge(const_loaded, 16)
            for k in range(KD):
                if k % 2 == 0:
                    act.wait_ge(x_loaded[k // 2], 16)
                act.activation(u0H[:, k, :], h[:, k, :], ACT.Copy,
                               scale=cst[:, K_GAIN + k:K_GAIN + k + 1]).then_inc(u_high, 1)
                if k:
                    act.wait_ge(ssq_added, k)
                act.activation(sq[:, :], h[:, k, :], ACT.Square).then_inc(squared, 1)
            act.wait_ge(bias_full, 1)
            act.activation(bias_table, sbank[0][0:H, 0:NBIAS], ACT.Copy).then_inc(bias_copied, 1)
            act.wait_ge(bias_copied, 1)
            act.dma_start(bias_rows, bass.AP(tensor=bias_table.tensor, offset=bias_table.offset,
                                             ap=[bias_table.ap[0], [0, P], [1, NBIAS]])).then_inc(bias_stored, 16)
            act.wait_ge(bias_stored, 16)
            act.dma_start(near_bias[:, :, :], bass.AP(tensor=bias_rows.tensor, offset=P - 1,
                                                      ap=[[NBIAS - 1, P], [P * NBIAS, H], [1, 2 * P]])
                          ).then_inc(bias_loaded, 16)

            with act.Fori(0, L) as l:
                def ffn(chunk, hid_from, root_n, hi, g, n_from):
                    def hidden(j, c, hid):
                        for i in range(2):
                            act.wait_ge(evacuated, chunk_at(l, c + 2 * i) + j * 4)
                            act.activation(sg[:, 0, :], ta[:, :], ACT.Sigmoid).then_inc(sigmoid_ready, 1)
                            apart(act, (gated, l * 44 + j * 2 + (hid + i + 1)))
                            act.activation(hidH[:, bass.ds(j * 2 + i, 1), :].rearrange("p a t -> p (a t)"),
                                           sg[:, 1, :], ACT.Copy).then_inc(hidden_high, 1)

                    root(l * 5 + root_n, tb[:, :], ta[:, :])
                    with act.Fori(0, HALF[0] // 2) as j:
                        hidden(j, chunk, hid_from)
                    if chunk == 0:
                        act.wait_ge(mem_loaded, l * 16 + 16)
                        for k in range(KD):
                            if k:
                                act.wait_ge(mem_ssq, l * KD + k)
                            act.activation(sq[:, 0:M], mem[:, k, :], ACT.Square).then_inc(mem_squared, 1)
                        root(l * 5 + 2, ssq[:, 0:M], sq[:, 0:M])
                    with act.Fori(0, HALF[1] // 2) as j:
                        hidden(j, chunk + 32, hid_from + HALF[0])

                def last_half(chunk, n_from, g, hi):
                    with act.Fori(0, KD) as k:
                        apart(act, (evacuated, chunk_at(l, chunk + 52) + k))
                        kk = bass.ds(k, 1)
                        row = lambda t: t[:, kk, :].rearrange("p a t -> p (a t)")
                        act.activation(row(hi), row(h), ACT.Copy, scale=gain(g, k)).then_inc(u_high, 1)
                        apart(act, (ssq_added, l * 24 + k + n_from))
                        act.activation(sq[:, :], row(h), ACT.Square).then_inc(squared, 1)

                ffn(0, 0, 1, u1H, G_MIX, 8)
                act.wait_ge(mem_normed, l + 1)
                for k in range(KD):
                    act.activation(mem_hi[:, k, :], mem[:, k, :], ACT.Copy,
                                   scale=pr[:, G_MEM + k:G_MEM + k + 1]).then_inc(mem_high, 1)
                last_half(0, 8, G_MIX, u1H)

                root(l * 5 + 3, tb[:, :], ta[:, :])

                def exps(i):
                    kind, a, b = STEPS[i]
                    if kind == "N":
                        return
                    n = S_INDEX[("step", i)]
                    src = sbank[n % 2]
                    if kind == "A":
                        m = SOFTMAX.index(i)
                        width = P * (a + 1)
                        p = probs[:, m % 3, 0:width]
                        act.wait_ge(logit_max, l * N_SOFT + (m + 1))
                        act.activation(p, p, ACT.Exp, bias=nmax[:, m % 4, 0:1],
                                       accum_out=rsum[:, m % 4, 0:1]).then_inc(exp_done, 1)
                    elif kind == "C":
                        m = SOFTMAX.index(i)
                        act.wait_ge(logit_max, l * N_SOFT + (m + 1))
                        if m >= 3:
                            act.wait_ge(t_full, l * N_SOFT + (m - 2))
                        for j in range(2):
                            e = act.activation(probs[:, m % 3, j * M:(j + 1) * M], src[:, j * M:(j + 1) * M],
                                               ACT.Exp, bias=nmax[:, m % 4, j:j + 1],
                                               accum_out=rsum[:, m % 4, j:j + 1])
                        e.then_inc(exp_done, 1)
                    elif kind == "Q":
                        act.wait_ge(s_full, l * len(S_USES) + (n + 1))
                        act.activation(qlat[:, 4 * b:4 * b + 4, :].rearrange("p a t -> p (a t)"), src[:, :],
                                       ACT.Copy, scale=HD ** -0.5).then_inc(qlat_ready, 1)
                    elif kind == "U":
                        act.wait_ge(s_full, l * len(S_USES) + (n + 1))
                        rows = slice(64 * b, 64 * b + 64)
                        act.activation(yH[rows, 0:4, a * P:(a + 1) * P],
                                       src[rows, :].rearrange("p (a t) -> p a t", t=P),
                                       ACT.Copy).then_inc(ya_high, 1)
                    elif kind == "B":
                        act.wait_ge(s_full, l * len(S_USES) + (n + 1))
                        act.activation(yH[:, 4 + a, :], src[:, :], ACT.Copy,
                                       scale=pr[:, G_POOL + a:G_POOL + a + 1]).then_inc(yb_high, 1)

                def normalise(i):
                    kind, a, b = STEPS[i]
                    m = SOFTMAX.index(i)
                    act.wait_ge(sum_inverted, l * N_SOFT + (m + 1))
                    parts = [(0, P * (a + 1))] if kind == "A" else [(0, M), (M, 2 * M)]
                    for j, (x, y) in enumerate(parts):
                        e = act.activation(probs[:, m % 3, x:y], probs[:, m % 3, x:y], ACT.Copy,
                                           scale=rinv[:, m % 4, j:j + 1])
                    e.then_inc(probs_ready, 1)

                def take_turned(i):
                    kind, a, b = STEPS[i]
                    m = SOFTMAX.index(i)
                    width = 4 * P if kind == "C" else P * (a + 1)
                    act.wait_ge(t_full, l * N_SOFT + (m + 1))
                    if m >= 2:
                        act.wait_ge(v_full, l * N_SOFT + (m - 1))
                    act.activation(pt[:, m % 2, 0:width], tbank[:, 0:width], ACT.Copy).then_inc(pt_ready, 1)

                def take_values(i):
                    kind, a, b = STEPS[i]
                    m = SOFTMAX.index(i)
                    if kind == "C":
                        act.wait_ge(v_full, l * N_SOFT + (m + 1))
                        rows = slice(64 * b, 64 * b + 64)
                        act.activation(yH[rows, 6:8, a * P:(a + 1) * P],
                                       obank[rows, 0:2 * P].rearrange("p (a t) -> p a t", t=P),
                                       ACT.Copy).then_inc(yc_high, 1)
                    elif b % 4 == 3:
                        act.wait_ge(v_full, l * N_SOFT + (m + 1))
                        act.activation(olat, obank[:, :], ACT.Copy).then_inc(olat_ready, 1)

                def group(now, last):
                    last = [i for i in last if i in SOFTMAX]
                    for i in last:
                        take_turned(i)
                    for i in now:
                        exps(i)
                    for i in last:
                        take_values(i)
                    for i in now:
                        if i in SOFTMAX:
                            normalise(i)

                last = []
                for at in SLOTS:
                    kind, i = at
                    scores, steps, _ = PLAN[at]
                    if at == ("in", 0):
                        act.wait_ge(evacuated, chunk_at(l, C_IN))
                        for g in range(4):
                            act.activation(ik[ID * g:ID * g + ID, :], misc[0:ID, :], ACT.Copy).then_inc(ik_ready, 1)
                        act.activation(iwT, misc[ID:ID + IH, :], ACT.Copy).then_inc(ik_ready, 1)
                    if at == ("in", 1):
                        act.wait_ge(evacuated, chunk_at(l, C_IN + 1))
                        act.activation(ckv_sq, ckv[:, :], ACT.Square).then_inc(ckv_squared, 1)
                    if at == ("in", 3):
                        root(l * 5 + 4, tb[:, :], ta[:, :])
                        act.preload_act_table_set("natural_log_exp_and_others")
                    if at == ("in", 5):
                        act.wait_ge(c_full, l + 1)
                        act.activation(c_tok.rearrange("p b r -> p (b r)"), tbank[:, :], ACT.Copy
                                       ).then_inc(c_ready, 1)
                    for s in scores:
                        qb = 1 + s // IH
                        width = P * (qb + 1)
                        act.wait_ge(s_full, l * len(S_USES) + (s + 1))
                        if s >= 2:
                            act.wait_ge(score_added, l * N_SCORES + (s - 1))
                        act.activation(relu[:, s % 2, 0:width], sbank[s % 2][:, 0:width], ACT.Relu,
                                       scale=ID ** -0.5).then_inc(relu_ready, 1)
                    if steps:
                        group(steps, last)
                        last = steps
                    if kind == "in" and i >= N_IN:
                        cof = N_IN + 4 * ((i - N_IN) // 2) + (i - N_IN) % 2
                        g = gate_bc[:, i % 2, :]
                        act.wait_ge(evacuated, chunk_at(l, C_IN + cof))
                        own.done(act.activation(g, g, ACT.Exp, scale=-1.0))
                        own.wait()
                        own.done(act.activation(g, g, ACT.Ln, bias=cst[:, K_ONE:K_ONE + 1]))
                        own.wait()
                        act.activation(g, g, ACT.Exp, scale=-1.0).then_inc(gate_exp, 1)
                for steps in TAIL:
                    group(steps, last)
                    last = steps

                for f in range(KD):
                    act.activation(gate_a[:, f, :], gate_a[:, f, :], ACT.Sigmoid).then_inc(gate_ready, 1)
                for f in range(KD):
                    act.wait_ge(merged_sum, l * KD + (f + 1))
                    act.activation(u1H[:, f, :], (tb, sg)[0][:, :], ACT.Copy).then_inc(merged_high, 1)
                for k in range(KD):
                    act.wait_ge(evacuated, chunk_at(l, C_WO + k))
                    act.activation(u0H[:, k, :], h[:, k, :], ACT.Copy,
                                   scale=pr[:, G_FFN2 + k:G_FFN2 + k + 1]).then_inc(u_high, 1)
                    act.wait_ge(ssq_added, l * 24 + (16 + k))
                    act.activation(sq[:, :], h[:, k, :], ACT.Square).then_inc(squared, 1)
                ffn(C_FFN2, sum(HALF), 5, u0H, G_NEXT, 24)
                last_half(C_FFN2, 24, G_NEXT, u0H)
                own.restart()
            root(L * 5 + 1, tb[:, :], ta[:, :])

        @block.vector
        def _(dve):
            own = Steps(dve, vector_step)
            for _b in range(BANKS):
                dve.sem_inc(evacuated, 1)

            def inverse_rms(n, dst, count, width, v, s):
                v, s = v[:, 0:width], s[:, 0:width]
                dve.wait_ge(norm_sum, n)
                dve.tensor_scalar(v, obank[:, 0:width], 1.0 / count, EPS, ALU.mult, ALU.add).then_inc(norm_var, 1)
                dve.wait_ge(norm_root, n)
                own.done(dve.reciprocal(dst, s))
                own.wait()
                own.done(dve.tensor_tensor(s, dst, dst, ALU.mult))
                own.wait()
                own.done(dve.tensor_tensor(s, s, v, ALU.mult))
                own.wait()
                own.done(dve.tensor_scalar(s, s, -0.5, 1.5, ALU.mult, ALU.add))
                own.wait()
                own.done(dve.tensor_tensor(dst, dst, s, ALU.mult))
                own.wait()

            own.done(dve.memset(ssq[:, :], 0.0))
            own.wait()
            dve.wait_ge(const_loaded, 16)
            for k in range(KD):
                if k % 2 == 0:
                    dve.wait_ge(x_loaded[k // 2], 16)
                dve.wait_ge(u_high, k + 1)
                dve.scalar_tensor_tensor(u0L[:, k, :], h[:, k, :], cst[:, K_GAIN + k:K_GAIN + k + 1],
                                         u0H[:, k, :].bitcast(F32), ALU.mult, ALU.subtract).then_inc(u_ready, 1)
                dve.wait_ge(squared, k + 1)
                if k:
                    dve.wait_ge(ssq_added, k)
                dve.tensor_tensor(ssq[:, :], ssq[:, :], sq[:, :], ALU.add).then_inc(ssq_added, 1)
            own.restart()

            with dve.Fori(0, L) as l:
                def ffn(unit, chunk, hid_from, norm_n):
                    def hidden(j, u, c, hid):
                        for i in range(2):
                            n = l * 44 + j * 2 + (hid + i + 1)
                            dve.wait_ge(unit_used, unit_at(l, u + 2 * i) + j * 4)
                            dve.tensor_tensor(ta[:, :], bank[2 * i][:, :], rms[:, :], ALU.mult).then_inc(evacuated, 1)
                            dve.wait_ge(unit_used, unit_at(l, u + 2 * i + 1) + j * 4)
                            dve.tensor_tensor(tb[:, :], bank[2 * i + 1][:, :], rms[:, :], ALU.mult
                                              ).then_inc(evacuated, 1)
                            dve.wait_ge(evacuated, chunk_at(l, c + 2 * i + 1) + j * 4)
                            dve.wait_ge(sigmoid_ready, n)
                            own.done(dve.tensor_tensor(ta[:, :], ta[:, :], sg[:, 0, :], ALU.mult))
                            own.wait()
                            dve.tensor_tensor(sg[:, 1, :], ta[:, :], tb[:, :], ALU.mult).then_inc(gated, 1)
                            dve.wait_ge(hidden_high, n)
                            kk = bass.ds(j * 2 + i, 1)
                            dve.tensor_tensor(hidL[:, kk, :].rearrange("p a t -> p (a t)"), sg[:, 1, :],
                                              hidH[:, kk, :].rearrange("p a t -> p (a t)").bitcast(F32),
                                              ALU.subtract).then_inc(hidden_ready, 1)
                        own.restart()

                    inverse_rms(l * 5 + norm_n, rms[:, :], D, T, ta, tb)
                    own.restart()
                    with dve.Fori(0, HALF[0] // 2) as j:
                        hidden(j, unit, chunk, hid_from)
                    if unit == 0:
                        own.done(dve.memset(ssq[:, 0:M], 0.0))
                        own.wait()
                        for k in range(KD):
                            dve.wait_ge(mem_squared, l * KD + (k + 1))
                            if k:
                                dve.wait_ge(mem_ssq, l * KD + k)
                            dve.tensor_tensor(ssq[:, 0:M], ssq[:, 0:M], sq[:, 0:M], ALU.add).then_inc(mem_ssq, 1)
                    with dve.Fori(0, 2) as j:
                        for i in range(4):
                            dve.wait_ge(unit_used, unit_at(l, unit + 24 + 2 * i + 1) + j * 8)
                            row = h[:, bass.ds(j * 4 + i, 1), :].rearrange("p a t -> p (a t)")
                            dve.scalar_tensor_tensor(row, bank[i][:, :], 0.5, row, ALU.mult, ALU.add
                                                     ).then_inc(evacuated, 1)
                    if unit == 0:
                        inverse_rms(l * 5 + 2, mem_rms[:, :], D, M, sq, ssq)
                        own.restart()
                    with dve.Fori(0, HALF[1] // 2) as j:
                        hidden(j, unit + 40, chunk + 32, hid_from + HALF[0])
                    dve.wait_ge(evacuated, chunk_at(l, chunk + 51))
                    own.done(dve.memset(ssq[:, :], 0.0))

                def finish_h(k, ps, c, scale, n, g, hi, lo):
                    row = (lambda t: t[:, k, :]) if isinstance(k, int) else (
                        lambda t: t[:, bass.ds(k, 1), :].rearrange("p a t -> p (a t)"))
                    dve.scalar_tensor_tensor(row(h), ps, scale, row(h), ALU.mult, ALU.add).then_inc(evacuated, 1)
                    dve.wait_ge(evacuated, c)
                    dve.wait_ge(u_high, n)
                    dve.scalar_tensor_tensor(row(lo), row(h), gain(g, k), row(hi).bitcast(F32),
                                             ALU.mult, ALU.subtract).then_inc(u_ready, 1)
                    dve.wait_ge(squared, n)
                    dve.wait_ge(ssq_added, n - 1)
                    dve.tensor_tensor(ssq[:, :], ssq[:, :], sq[:, :], ALU.add).then_inc(ssq_added, 1)

                def last_half(unit, chunk, n_from, g, hi, lo):
                    own.restart()
                    with dve.Fori(0, 2) as j:
                        for i in range(4):
                            dve.wait_ge(unit_used, unit_at(l, unit + 60 + 2 * i + 1) + j * 8)
                            finish_h(j * 4 + i, bank[i][:, :], chunk_at(l, chunk + 52 + i) + j * 4, 0.5,
                                     l * 24 + j * 4 + (n_from + i + 1), g, hi, lo)

                ffn(0, 0, 0, 1)
                dve.wait_ge(mem_loaded, l * 16 + 16)
                dve.wait_ge(unit_used, unit_at(l, 59))
                for k in range(KD):
                    ins = dve.tensor_tensor(mem[:, k, :], mem[:, k, :], mem_rms[:, :], ALU.mult)
                    if k < KD - 1:
                        own.done(ins)
                    else:
                        ins.then_inc(mem_normed, 1)
                dve.wait_ge(par_loaded, l * 16 + 16)
                for k in range(KD):
                    dve.wait_ge(mem_high, l * KD + (k + 1))
                    dve.scalar_tensor_tensor(mem_lo[:, k, :], mem[:, k, :], pr[:, G_MEM + k:G_MEM + k + 1],
                                             mem_hi[:, k, :].bitcast(F32), ALU.mult, ALU.subtract
                                             ).then_inc(mem_ready, 1)
                last_half(0, 0, 8, G_MIX, u1H, u1L)

                def mem_kv(i):
                    dve.wait_ge(unit_used, unit_at(l, U_MEM + (i if i < 2 else 3)))
                    dst = kc[:, i, :] if i < 2 else vc[:, i - 2, :]
                    dve.tensor_copy(dst, bank[i][:, 0:M]).then_inc(evacuated, 1)

                dve.wait_ge(bias_loaded, 32)
                mem_kv(0)
                inverse_rms(l * 5 + 3, rms[:, :], D, T, ta, tb)
                for i in range(1, 4):
                    mem_kv(i)

                rounds_done = [0]

                def pick_round():
                    qb, n = 1 + rounds_done[0] // (TOPK // 8), rounds_done[0] % (TOPK // 8)
                    rounds_done[0] += 1
                    own.done(dve.max(top8[:, :], picks[qb][:, :]))
                    own.wait()
                    own.done(dve.match_replace(picks[qb][:, :], top8[:, :], picks[qb][:, :], PICKED))
                    own.wait()
                    if n == TOPK // 8 - 1:
                        own.done(dve.tensor_scalar(picks[qb][:, :], picks[qb][:, :], PICKED, NEG,
                                                   ALU.not_equal, ALU.mult))
                        own.wait()

                def add_score(s):
                    qb, hd = 1 + s // IH, s % IH
                    width = P * (qb + 1)
                    dve.wait_ge(relu_ready, l * N_SCORES + (s + 1))
                    w = iw[:, qb, hd:hd + 1]
                    if hd == 0:
                        dve.tensor_scalar(picks[qb][:, :], relu[:, s % 2, 0:width], w, None, ALU.mult
                                          ).then_inc(score_added, 1)
                    else:
                        dve.wait_ge(score_added, l * N_SCORES + s)
                        dve.scalar_tensor_tensor(picks[qb][:, :], relu[:, s % 2, 0:width], w, picks[qb][:, :],
                                                 ALU.mult, ALU.add).then_inc(score_added, 1)
                    if hd == IH - 1:
                        dve.wait_ge(score_added, l * N_SCORES + (s + 1))
                        last = picks[qb][:, qb * P:(qb + 1) * P]
                        own.done(dve.tensor_tensor(last, last, causal, ALU.add))
                        own.wait()

                def window_means():
                    dve.wait_ge(evacuated, chunk_at(l, C_IN + 11))

                    def widen(dst, src, by):
                        own.done(dve.tensor_tensor(dst[:, :, by:T], src[:, :, by:T], src[:, :, 0:T - by], ALU.add))
                        own.done(dve.tensor_copy(dst[:, :, 0:by], src[:, :, 0:by]))
                        own.wait()

                    widen(za, z, 1)
                    widen(zb, za, 2)
                    widen(za[:, 1:2, :], zb[:, 1:2, :], 4)
                    widen(zb[64:128, 1:2, :], za[64:128, 1:2, :], 8)
                    for g, w in enumerate(WINDOWS):
                        rows, c = slice(64 * (g % 2), 64 * (g % 2) + 64), g // 2
                        s = (za, zb)[g % 2][rows, c, :]
                        count = cst[rows, K_COUNT + WMAX * c:K_COUNT + WMAX * (c + 1)]
                        own.done(dve.scalar_tensor_tensor(s[:, WMAX:T], s[:, WMAX:T], 1.0 / w, z[rows, c, WMAX:T],
                                                          ALU.mult, ALU.subtract))
                        own.done(dve.tensor_tensor(s[:, 0:WMAX], s[:, 0:WMAX], count, ALU.mult))
                        own.wait()
                        dve.tensor_tensor(s[:, 0:WMAX], s[:, 0:WMAX], z[rows, c, 0:WMAX], ALU.subtract
                                          ).then_inc(pooled, 1)

                def logits(i):
                    kind, a, b = STEPS[i]
                    if kind in "NQ":
                        return
                    n = S_INDEX[("step", i)]
                    src = sbank[n % 2]
                    if kind == "A":
                        m = SOFTMAX.index(i)
                        if i == 0 or b == 0:
                            while a and rounds_done[0] < a * (TOPK // 8):
                                pick_round()
                        width, near = P * (a + 1), P * max(a - 1, 0)
                        p, mask = probs[:, m % 3, :], masks(a)
                        read = l * 32 + (KIND_INDEX[i] + 1)
                        dve.wait_ge(s_full, l * len(S_USES) + (n + 1))
                        if m >= 3:
                            dve.wait_ge(t_full, l * N_SOFT + (m - 2))
                        ins = dve.tensor_tensor(p[:, near:width], src[:, near:width],
                                                near_bias[:, head(b), 2 * P - (width - near):2 * P], ALU.add)
                        if near:
                            own.done(ins)
                            dve.scalar_tensor_tensor(p[:, 0:near], src[:, 0:near], far_bias[:, head(b):head(b) + 1],
                                                     mask[:, 0:near], ALU.add, ALU.add).then_inc(logits_read, 1)
                            own.wait()
                        else:
                            ins.then_inc(logits_read, 1)
                        dve.wait_ge(logits_read, read)
                        own.done(dve.tensor_tensor(p[:, near:width], p[:, near:width], mask[:, near:width], ALU.add))
                        own.wait()
                        dve.tensor_reduce(nmax[:, m % 4, 0:1], p[:, 0:width], AX.X, ALU.max, negate=True
                                          ).then_inc(logit_max, 1)
                    elif kind == "C":
                        m = SOFTMAX.index(i)
                        dve.wait_ge(s_full, l * len(S_USES) + (n + 1))
                        dve.tensor_reduce(nmax[:, m % 4, :], src[:, :].rearrange("p (a t) -> p a t", a=2), AX.X,
                                          ALU.max, negate=True).then_inc(logit_max, 1)
                    elif kind == "U":
                        dve.wait_ge(ya_high, l * 8 + (KIND_INDEX[i] + 1))
                        rows = slice(64 * b, 64 * b + 64)
                        dve.tensor_tensor(yL[rows, 0:4, a * P:(a + 1) * P],
                                          src[rows, :].rearrange("p (a t) -> p a t", t=P),
                                          yH[rows, 0:4, a * P:(a + 1) * P].bitcast(F32), ALU.subtract
                                          ).then_inc(ya_ready, 1)
                    elif kind == "B":
                        dve.wait_ge(yb_high, l * 2 + (a + 1))
                        dve.scalar_tensor_tensor(yL[:, 4 + a, :], src[:, :], pr[:, G_POOL + a:G_POOL + a + 1],
                                                 yH[:, 4 + a, :].bitcast(F32), ALU.mult, ALU.subtract
                                                 ).then_inc(yb_ready, 1)

                def invert(i):
                    m = SOFTMAX.index(i)
                    n = 1 if STEPS[i][0] == "A" else 2
                    dve.wait_ge(exp_done, l * N_SOFT + (m + 1))
                    dve.reciprocal(rinv[:, m % 4, 0:n], rsum[:, m % 4, 0:n]).then_inc(sum_inverted, 1)

                def low_values(i):
                    kind, a, b = STEPS[i]
                    m = SOFTMAX.index(i)
                    if kind == "C":
                        dve.wait_ge(yc_high, l * 8 + (m + 1))
                        rows = slice(64 * b, 64 * b + 64)
                        dve.tensor_tensor(yL[rows, 6:8, a * P:(a + 1) * P],
                                          obank[rows, 0:2 * P].rearrange("p (a t) -> p a t", t=P),
                                          yH[rows, 6:8, a * P:(a + 1) * P].bitcast(F32), ALU.subtract
                                          ).then_inc(yc_ready, 1)

                def group(now, last):
                    for i in now:
                        logits(i)
                    for i in last:
                        if i in SOFTMAX:
                            low_values(i)
                    for i in now:
                        if i in SOFTMAX:
                            invert(i)

                last = []
                for at in SLOTS:
                    kind, i = at
                    scores, steps, n_picks = PLAN[at]
                    if kind == "in":
                        off = i if i < N_IN else N_IN + 3 * ((i - N_IN) // 2) + (i - N_IN) % 2
                        cof = i if i < N_IN else N_IN + 4 * ((i - N_IN) // 2) + (i - N_IN) % 2
                        src = bank[(C_IN + cof) % BANKS][:, :]
                        dve.wait_ge(unit_used, unit_at(l, U_IN + off))
                        if i == 0:
                            dve.tensor_tensor(misc[0:40, :], src[0:40, :], rms[0:40, :], ALU.mult
                                              ).then_inc(evacuated, 1)
                        elif 8 <= i < 10:
                            dve.scalar_tensor_tensor(qc[:, i - 8, :], src, HD ** -0.5, rms[:, :], ALU.mult,
                                                     ALU.mult).then_inc(evacuated, 1)
                        else:
                            dst = (ckv[:, :] if i == 1 else iq[:, i - 2, :] if i < 4 else q[:, i - 4, :] if i < 8
                                   else z[:, i - 10, :] if i < 12 else gate_a[:, i - 12, :] if i < N_IN
                                   else gate_bc[:, i % 2, :])
                            dve.tensor_tensor(dst, src, rms[:, :], ALU.mult).then_inc(evacuated, 1)
                    else:
                        dve.wait_ge(unit_used, unit_at(l, U_GBC + 3 * i + 2))
                        c = C_GBC + 4 * i + 2
                        dve.wait_ge(gate_exp, l * 16 + (2 * i + 2))
                        dve.tensor_tensor(ta[:, :], bank[c % BANKS][:, :], gate_bc[:, 0, :], ALU.mult
                                          ).then_inc(evacuated, 1)
                        dve.tensor_tensor(tb[:, :], bank[(c + 1) % BANKS][:, :], gate_bc[:, 1, :], ALU.mult
                                          ).then_inc(evacuated, 1)
                        dve.wait_ge(evacuated, chunk_at(l, c + 1))
                        own.done(dve.tensor_tensor(part[:, i, :], ta[:, :], tb[:, :], ALU.add))
                        own.wait()
                    if at == ("in", 3):
                        dve.wait_ge(iw_full, l + 1)
                        dve.tensor_scalar(iw[:, :, :].rearrange("p a b -> p (a b)"), tbank[:, 0:QB * IH],
                                          IH ** -0.5, None, ALU.mult).then_inc(iw_ready, 1)
                        dve.wait_ge(iw_ready, l + 1)
                        dve.wait_ge(ik_ready, l * 5 + 5)
                        inverse_rms(l * 5 + 4, ckv_rms, R, T, ta, tb)
                        dve.scalar_tensor_tensor(ckv[:, :], ckv[:, :], pr[:, G_KV:G_KV + 1], ckv_rms,
                                                 ALU.mult, ALU.mult).then_inc(ckv_ready, 1)
                    for s in scores:
                        add_score(s)
                    if steps:
                        group(steps, last)
                        last = steps
                    if at == ("in", 12):
                        window_means()
                    for _r in range(n_picks):
                        if rounds_done[0] < 3 * (TOPK // 8):
                            pick_round()
                for steps in TAIL:
                    group(steps, last)
                    last = steps

                def merged_low(f):
                    dve.wait_ge(merged_high, l * KD + (f + 1))
                    dve.tensor_tensor(u1L[:, f, :], tb[:, :], u1H[:, f, :].bitcast(F32), ALU.subtract
                                      ).then_inc(merged_ready, 1)

                for f in range(KD):
                    dve.wait_ge(unit_used, unit_at(l, U_BA + f))
                    if f:
                        dve.wait_ge(merged_sum, l * KD + f)
                    dve.wait_ge(gate_ready, l * KD + (f + 1))
                    dve.tensor_tensor(ta[:, :], bank[(C_BA + f) % BANKS][:, :], gate_a[:, f, :], ALU.mult
                                      ).then_inc(evacuated, 1)
                    if f:
                        merged_low(f - 1)
                        dve.wait_ge(merged_ready, l * KD + f)
                    dve.wait_ge(evacuated, chunk_at(l, C_BA + f))
                    dve.tensor_tensor(tb[:, :], ta[:, :], part[:, f, :], ALU.add).then_inc(merged_sum, 1)
                merged_low(KD - 1)
                own.done(dve.memset(ssq[:, :], 0.0))
                own.restart()
                for k in range(KD):
                    dve.wait_ge(unit_used, unit_at(l, U_WO + k))
                    finish_h(k, bank[(C_WO + k) % BANKS][:, :], chunk_at(l, C_WO + k), 1.0,
                             l * 24 + (16 + k + 1), G_FFN2, u0H, u0L)

                ffn(U_FFN2, C_FFN2, sum(HALF), 5)
                last_half(U_FFN2, C_FFN2, 24, G_NEXT, u0H, u0L)

            inverse_rms(L * 5 + 1, rms[:, :], D, T, ta, tb)
            for k in range(KD):
                dve.scalar_tensor_tensor(gate_a[:, k, :], h[:, k, :], gain(G_NEXT, k), rms[:, :],
                                         ALU.mult, ALU.mult).then_inc(out_ready, 1)


def tiles(w):
    k, n = w.shape
    return w.reshape(k // P, P, n // P, P).transpose(2, 1, 0, 3)


def lay_out(i):
    a = {n: np.asarray(v) for n, v in i.items()}
    cat, flat = np.concatenate, lambda t: t.reshape(t.shape[0], P, -1)
    wA, wB0, wB1, wM, wR, par = [], [], [], [], [], []
    per_part = lambda g: g.reshape(-1, P).T
    for l in range(L):
        for f in ("ffn1", "ffn2"):
            t = flat(tiles(a[f + "_w_in"][l]))
            wA.append(t.reshape(2, FC, P, -1).transpose(1, 0, 2, 3).reshape(2 * FC, P, -1))
            t = tiles(a[f + "_w_out"][l])
            for dst, x, y in ((wB0, 0, HALF[0]), (wB1, HALF[0], FC)):
                half = t[:, :, x:y].reshape(KD, P, 2, -1).transpose(0, 2, 1, 3)
                dst.append(half.reshape(2 * KD, P, -1))
        w = a["w_in"][l]
        at = {"q": 0, "ckv": 512, "iq": 640, "misc": 896, "z": 936, "qc": 1192, "gate": 1448}
        cols = [at["misc"], at["ckv"], at["iq"], at["iq"] + P] + [at["q"] + P * c for c in range(4)]
        cols += [at["qc"], at["qc"] + P, at["z"], at["z"] + P] + [at["gate"] + P * f for f in range(KD)]
        for f in range(KD):
            cols += [at["gate"] + D + P * f, at["gate"] + 2 * D + P * f]
        kv = a["w_mem_kv"][l]
        wM.append(flat(tiles(kv[:, 0:M])))
        wM.append(flat(kv[:, M:].reshape(2, 4, P, M).transpose(0, 2, 1, 3)))
        wM.append(cat([flat(tiles(w[:, c:c + P])) for c in cols]))
        wM.append(flat(tiles(a["w_out"][l])))
        wR.append(flat(cat([tiles(a["w_branch_b"][l]), tiles(a["w_branch_c"][l])], axis=2)))
        wR.append(flat(tiles(a["w_branch_a"][l])))
        after = a["ffn1_norm"][l + 1] if l + 1 < L else a["final_norm"]
        par.append(cat([
            per_part(a["mix_norm"][l]), per_part(a["ffn2_norm"][l]), per_part(after), per_part(a["mem_norm"][l]),
            per_part(a["kv_norm"][l]), per_part(a["pool_scale"][l]),
            a["w_pool"][l].reshape(2, 2, 64, 64).transpose(1, 2, 0, 3).reshape(P, -1),
            a["w_uk"][l].transpose(1, 2, 0).reshape(4, P, R).transpose(1, 0, 2).reshape(P, -1),
            a["w_uv"][l].reshape(R, -1)], axis=1)[None])
    const, hot = constants()
    const[:, K_GAIN:K_GAIN + KD] = per_part(a["ffn1_norm"][0])
    token = lambda x: np.ascontiguousarray(x[0].T.reshape(KD, P, -1).transpose(1, 0, 2))
    arrays = {"xT": token(a["x"]), "memT": token(a["mem"]), "wA": cat(wA), "wB0": cat(wB0), "wB1": cat(wB1),
              "wM": cat(wM), "wR": cat(wR), "par": cat(par), "const": const, "hot": hot, "rel": a["rel_bias"]}
    return {n: np.ascontiguousarray(v) for n, v in arrays.items()}


def kernel(**inputs):
    import concourse.bacc as _bacc
    from concourse.bass_utils import run_bass_kernel_spmd as _run

    nc = _bacc.Bacc("TRN2", target_bir_lowering=False, num_devices=1)
    arrays = {f"in_{n}": v for n, v in lay_out(inputs).items()}
    args = [nc.dram_tensor(n, v.shape, F32, kind="ExternalInput").ap() for n, v in arrays.items()]
    out = nc.dram_tensor("outT", (P, KD, T), F32, kind="ExternalOutput").ap()
    bias_rows = nc.dram_tensor("bias_rows", (H, P, NBIAS), F32, kind="Internal").ap()
    trunk(nc, *args, out, bias_rows)
    r = _run(nc, [arrays], core_ids=[0])
    return np.ascontiguousarray(r.results[0]["outT"].transpose(2, 1, 0).reshape(T, D))[None]
```

```python
import math
from contextlib import ExitStack

import numpy as np

import concourse.bass as bass
from concourse import mybir

F32 = mybir.dt.float32
F32R = mybir.dt.float32r
ALU = mybir.AluOpType
ACT = mybir.ActivationFunctionType
AX = mybir.AxisListType

P = 128
D = 1024
T = 512
L = 2
M = 256
KD = D // P
QB = T // P
H = 8
HD = 64
R = 128
IH = 8
ID = 32
CH = 4
TOPK = 128
FF = 2816
FC = FF // P
BUCKETS = 32
MAXDIST = 128
EPS = 1e-6
NEG = -1e30
PICKED = -3e38
WINDOWS = (2, 4, 8, 16)
WMAX = max(WINDOWS)

RAW_SLOTS, SPLIT_SLOTS, BANKS = 4, 2, 4
HALF = (12, 10)
U_FFN = 2 * sum(HALF) + 2 * 16
C_FFN = 2 * sum(HALF) + 2 * 8
U_MEM, C_MEM = U_FFN, C_FFN
U_IN, C_IN = U_MEM + 4, C_MEM + 4
N_IN = 20
U_GBC, C_GBC = U_IN + N_IN, C_IN + N_IN
U_BA, C_BA = U_GBC + 3 * KD, C_GBC + 4 * KD
U_WO, C_WO = U_BA + KD, C_BA + KD
U_FFN2, C_FFN2 = U_WO + KD, C_WO + KD
UNITS, CHUNKS = U_FFN2 + U_FFN, C_FFN2 + C_FFN
assert UNITS % RAW_SLOTS == 0 and CHUNKS % BANKS == 0

G_MIX, G_FFN2, G_NEXT, G_MEM, G_KV, G_POOL = 0, 8, 16, 24, 32, 33
W_POOL, W_UK, W_UV, N_PAR = 35, 163, 675, 1187
K_ID, K_ONE, K_CAUSAL, K_COUNT, K_GAIN, N_CONST = 0, 128, 256, 384, 416, 424

N_SCORES = 3 * IH
NBIAS = 384


def attention_steps():
    s = [("C", qb, hp) for qb in range(QB) for hp in range(2)]
    s += [("Q", 0, 0), ("Q", 0, 1)]
    late = None
    for qb in range(QB):
        a = [("A", qb, h) for h in range(H)]
        if late:
            a.insert(2, late)
        at = a.index(("A", qb, 3))
        if qb + 1 < QB:
            a.insert(at + 1, ("Q", qb + 1, 0))
            a.append(("Q", qb + 1, 1))
        at = a.index(("A", qb, 3))
        a.insert(at + 4, ("U", qb, 0))
        late = ("U", qb, 1)
        if qb == 0:
            a += [("B", 0, 0), ("B", 1, 0)]
        s += a
    return s + [("N", 0, 0)] * 3 + [late]


STEPS = attention_steps()
SOFTMAX = [i for i, s in enumerate(STEPS) if s[0] in "AC"]
N_SOFT = len(SOFTMAX)
KIND_INDEX = [sum(1 for t in STEPS[:i] if t[0] == s[0]) for i, s in enumerate(STEPS)]
SCORE_SLOTS = range(6, 12)
SCORES_AFTER = (1, 2, 6, 7)
FIRST_STEPS = 6
MID = 4


MEANS_AT = {("in", 11 + piece): piece for piece in range(5)}


def slot_plan():
    slots = [("in", i) for i in range(N_IN)]
    for f in range(KD):
        slots += [("in", N_IN + 2 * f), ("in", N_IN + 2 * f + 1), ("bc", f)]
    plan, at, scored = {}, 0, 0
    per_slot = N_SCORES // len(SCORE_SLOTS)
    for s in slots:
        scores, mid, end = [], [], []
        if s[0] == "in" and s[1] in SCORE_SLOTS:
            scores = list(range(scored, scored + per_slot))
            scored += per_slot
        if s[0] == "in" and s[1] >= FIRST_STEPS:
            mid = list(range(at, min(at + 1, len(STEPS))))
            at += len(mid)
        if s[0] == "bc" or s[1] >= FIRST_STEPS:
            end = list(range(at, min(at + 1, len(STEPS))))
            at += len(end)
        if s[0] == "bc":
            picks = (0, int(s[1] >= 2))
        elif s[1] >= SCORE_SLOTS.start + IH // per_slot:
            picks = (1, 1) if s[1] >= N_IN + 2 else (1, 2)
        else:
            picks = (0, 0)
        if s in MEANS_AT:
            picks = (0, 1)
        elif sum(picks) == 3 and s[1] < min(MEANS_AT)[1]:
            picks = (2, 2)
        plan[s] = (mid, end, scores, picks)
    assert scored == N_SCORES and at == len(STEPS)
    return slots, plan


SLOTS, PLAN = slot_plan()
S_USES = []
for _slot in SLOTS:
    _mid, _end, _scores, _ = PLAN[_slot]
    S_USES += [("score", i) for i in _scores[0:2]] + [("step", i) for i in _mid]
    S_USES += [("score", i) for i in _scores[2:4]] + [("step", i) for i in _end]
S_USES = [u for u in S_USES if u[0] == "score" or STEPS[u[1]][0] != "N"]
S_INDEX = {u: n for n, u in enumerate(S_USES)}


def head(n):
    return 2 * (n % 4) + n // 4


def bucket_of(n):
    exact = BUCKETS // 2
    nf = np.maximum(n, 1).astype(np.float32)
    large = exact + (np.log(nf / np.float32(exact)) / np.float32(math.log(MAXDIST / exact))
                     * np.float32(BUCKETS - exact)).astype(np.int32)
    return np.where(n < exact, n, np.minimum(large, BUCKETS - 1))


def constants():
    c = np.zeros((P, N_CONST), np.float32)
    c[:, K_ID:K_ID + P] = np.eye(P)
    c[:, K_ONE:K_ONE + P] = 1.0
    c[:, K_CAUSAL:K_CAUSAL + P] = np.where(np.arange(P)[None, :] <= np.arange(P)[:, None], 0.0, NEG)
    for g, w in enumerate(WINDOWS):
        rows = slice(64 * (g % 2), 64 * (g % 2) + 64)
        first = 1.0 / np.minimum(np.arange(1, WMAX + 1), w)
        c[rows, K_COUNT + WMAX * (g // 2):K_COUNT + WMAX * (g // 2) + WMAX] = first
    buckets = bucket_of(np.maximum(255 - np.arange(NBIAS), 0))
    hot = (np.arange(BUCKETS)[:, None] == buckets[None, :]).astype(np.float32)
    return c, hot


def trunk(nc, xT, memT, wA, wB0, wB1, wM, wR, par, const, hot, rel, out, bias_rows):
    ctx = ExitStack()
    with ctx:
        def sb(name, shape, dt=F32, scope=ctx):
            return scope.enter_context(nc.sbuf_tensor(name, shape, dt))

        def sem(name):
            return ctx.enter_context(nc.semaphore(name))

        h = sb("h", [P, KD, T])
        u1H, u1L = sb("u1H", [P, KD, T], F32R), sb("u1L", [P, KD, T], F32R)
        raw = sb("raw", [P, RAW_SLOTS, 8 * P])
        wH = sb("wH", [P, SPLIT_SLOTS, 8 * P], F32R)
        wL = sb("wL", [P, SPLIT_SLOTS, 8 * P], F32R)
        near_bias = sb("near_bias", [P, H, 2 * P])
        far_bias = sb("far_bias", [P, H])
        cst = sb("cst", [P, N_CONST])
        pr = sb("pr", [P, N_PAR])
        rms = sb("rms", [P, T])
        mem_rms = sb("mem_rms", [P, M])
        ssq = sb("ssq", [P, T])
        sq = sb("sq", [P, T])
        ta = sb("ta", [P, T])
        tb = sb("tb", [P, T])
        sg = sb("sg", [P, 2, T])
        iw = sb("iw", [P, QB, IH])
        norm = sb("norm", [P, 3, QB])
        top8 = sb("top8", [P, 8])
        nmax = sb("nmax", [P, 4, 2])
        rsum = sb("rsum", [P, 4, 2])
        rinv = sb("rinv", [P, 4, 2])
        with ExitStack() as ffn:
            u0H, u0L = sb("u0H", [P, KD, T], F32R, ffn), sb("u0L", [P, KD, T], F32R, ffn)
            hidH = sb("hidH", [P, HALF[0], T], F32R, ffn)
            hidL = sb("hidL", [P, HALF[0], T], F32R, ffn)
            mem = sb("mem", [P, KD, M], F32, ffn)
        with ExitStack() as mix:
            yH, yL = sb("yH", [P, KD, T], F32R, mix), sb("yL", [P, KD, T], F32R, mix)
            gate_a = sb("gate_a", [P, KD, T], F32, mix)
            qc = sb("qc", [P, 2, T], F32, mix)
            kc = sb("kc", [P, 2, M], F32, mix)
            vc = sb("vc", [P, 2, M], F32, mix)
            z = sb("z", [P, 2, T], F32, mix)
            za = sb("za", [P, 2, T], F32, mix)
            iq = sb("iq", [P, 2, T], F32, mix)
            q = sb("q", [P, QB, T], F32, mix)
            qlat = sb("qlat", [P, H, P], F32, mix)
            probs = sb("probs", [P, 3, T], F32, mix)
            ckv = sb("ckv", [P, T], F32, mix)
            relu = sb("relu", [P, 2, T], F32, mix)
            picks = [None] + [sb(f"picks{b}", [P, P * (b + 1)], F32, mix) for b in range(1, QB)]
        with ExitStack() as index:
            sb("hole2", [P, 2, KD, T], F32, index)
            iq_stack = sb("iq_stack", [P, IH, T - P], F32R, index)
            ik_stack = sb("ik_stack", [P, T], F32R, index)
            sb("hole3", [P, T], F32, index)
            sb("hole4", [P, 2, T], F32, index)
            sb("hole5", [P, 2, M], F32, index)
            sb("hole6", [P, 2, M], F32, index)
            iqH = sb("iqH", [P, 2, T - P], F32R, index)
        with ExitStack() as late:
            sb("hole0", [P, 2, KD, T], F32, late)
            sb("hole1", [P, KD, T], F32, late)
            part = sb("part", [P, KD, T], F32, late)
            gate_bc = sb("gate_bc", [P, 2, T], F32, late)
        mem_hi = yH[:, 0:4, :].rearrange("p a (b m) -> p (a b) m", m=M)
        mem_lo = yL[:, 0:4, :].rearrange("p a (b m) -> p (a b) m", m=M)
        c_tok = ssq[:, :].rearrange("p (b r) -> p b r", r=R)
        zb = gate_bc
        olat = relu[:, 0, :]
        pt = sg
        misc = ta
        iwT = probs[0:8, 1, :]
        ckv_sq = probs[:, 0, :]
        ckv_rms = probs[:, 2, :]
        ident = cst[:, K_ID:K_ID + P]
        ones = cst[:, K_ONE:K_ONE + P]
        causal = cst[:, K_CAUSAL:K_CAUSAL + P]

        rel_sb = q[0:BUCKETS, 1, 0:H]
        bias_table = q[0:H, 2, 0:NBIAS]

        def masks(qb):
            return causal if qb == 0 else picks[qb][:, :]

        def gain(at, k):
            return pr[:, bass.ds(at + k, 1)]

        bank = [ctx.enter_context(nc.psum_tensor(f"bank{i}", [P, 512], F32)) for i in range(BANKS)]
        sbank = [ctx.enter_context(nc.psum_tensor(f"sbank{i}", [P, 512], F32)) for i in range(2)]
        tbank = ctx.enter_context(nc.psum_tensor("tbank", [P, 512], F32))
        obank = ctx.enter_context(nc.psum_tensor("obank", [P, 512], F32))

        const_loaded = sem("const_loaded")
        rel_loaded = sem("rel_loaded")
        x_loaded = [sem(f"x_loaded{i}") for i in range(4)]
        mem_loaded = sem("mem_loaded")
        par_loaded = sem("par_loaded")
        raw_landed = [sem(f"raw_landed{s}") for s in range(RAW_SLOTS)]
        rounded = sem("rounded")
        split_done = sem("split_done")
        unit_used = sem("unit_used")
        evacuated = sem("evacuated")
        sigmoid_ready = sem("sigmoid_ready")
        gated = sem("gated")
        hidden_high = sem("hidden_high")
        hidden_ready = sem("hidden_ready")
        u_high = sem("u_high")
        squared = sem("squared")
        u_ready = sem("u_ready")
        ssq_added = sem("ssq_added")
        norm_sum = sem("norm_sum")
        norm_var = sem("norm_var")
        norm_root = sem("norm_root")
        norm_diag = sem("norm_diag")
        norm_spread = sem("norm_spread")
        norm_taken = sem("norm_taken")
        bias_full = sem("bias_full")
        bias_copied = sem("bias_copied")
        bias_stored = sem("bias_stored")
        bias_loaded = sem("bias_loaded")
        far_loaded = sem("far_loaded")
        mem_squared = sem("mem_squared")
        mem_ssq = sem("mem_ssq")
        mem_normed = sem("mem_normed")
        mem_high = sem("mem_high")
        mem_ready = sem("mem_ready")
        ik_ready = sem("ik_ready")
        ik_low = sem("ik_low")
        iq_high = sem("iq_high")
        iq_stacked = sem("iq_stacked")
        iq_low = sem("iq_low")
        iw_full = sem("iw_full")
        iw_ready = sem("iw_ready")
        ckv_squared = sem("ckv_squared")
        ckv_ready = sem("ckv_ready")
        c_full = sem("c_full")
        c_ready = sem("c_ready")
        s_full = sem("s_full")
        relu_ready = sem("relu_ready")
        score_added = sem("score_added")
        pooled = sem("pooled")
        yb_high = sem("yb_high")
        yb_ready = sem("yb_ready")
        logits_read = sem("logits_read")
        logit_max = sem("logit_max")
        exp_done = sem("exp_done")
        sum_inverted = sem("sum_inverted")
        probs_ready = sem("probs_ready")
        t_full = sem("t_full")
        pt_ready = sem("pt_ready")
        v_full = sem("v_full")
        yc_high = sem("yc_high")
        yc_ready = sem("yc_ready")
        qlat_ready = sem("qlat_ready")
        olat_ready = sem("olat_ready")
        ya_high = sem("ya_high")
        ya_ready = sem("ya_ready")
        gate_exp = sem("gate_exp")
        gate_ready = sem("gate_ready")
        merged_sum = sem("merged_sum")
        merged_high = sem("merged_high")
        merged_ready = sem("merged_ready")
        out_ready = sem("out_ready")
        out_stored = [sem(f"out_stored{s}") for s in range(4)]
        vector_step = sem("vector_step")
        scalar_step = sem("scalar_step")

        def unit_at(l, u):
            return l * UNITS + (u + 1 + SPLIT_SLOTS)

        def chunk_at(l, c):
            return l * CHUNKS + (c + 1 + BANKS)

        def apart(eng, *waits):
            waits = [(s, eng.to_reg(value)) for s, value in waits]
            eng.wait_ge(const_loaded, 16)
            for s, value in waits:
                eng.wait_ge(s, value)

        class Steps:

            def __init__(self, eng, s):
                self.eng, self.s, self.n = eng, s, 0

            def done(self, ins):
                self.n += 1
                ins.then_inc(self.s, 1)

            def wait(self):
                self.eng.wait_ge(self.s, self.n)

            def restart(self):
                if self.n:
                    self.wait()
                self.eng.sem_clear(self.s)
                self.n = 0

        block = ctx.enter_context(nc.Block())

        @block.sync
        def _(sp):
            sp.dma_start(cst[:, :], const).then_inc(const_loaded, 16)
            sp.dma_start(q[0:BUCKETS, 0, 0:NBIAS], hot).then_inc(rel_loaded, 16)
            sp.dma_start(q[0:BUCKETS, 1, 0:H], rel).then_inc(rel_loaded, 16)

            with sp.Fori(0, L) as l:
                def units(src, per_layer, first, count, cols, unit):
                    with sp.Fori(0, count // RAW_SLOTS) as j:
                        for s in range(RAW_SLOTS):
                            sp.wait_ge(split_done, l * UNITS + j * RAW_SLOTS + (unit + s + 1))
                            n = l * per_layer + j * RAW_SLOTS + (first + s)
                            sp.dma_start(raw[:, s, 0:cols],
                                         src[bass.ds(n, 1), :, :].rearrange("a p n -> p (a n)")
                                         ).then_inc(raw_landed[s], 16)

                def ffn_units(f, unit):
                    units(wA, 88, 44 * f, 24, 1024, unit)
                    if f == 0:
                        sp.dma_start(pr[:, :], par[bass.ds(l, 1), :, :].rearrange("a p n -> p (a n)")
                                     ).then_inc(par_loaded, 16)
                        sp.dma_start(mem[:, :, :], memT).then_inc(mem_loaded, 16)
                    units(wB0, 32, 16 * f, 16, 768, unit + 24)
                    units(wA, 88, 44 * f + 24, 20, 1024, unit + 40)
                    units(wB1, 32, 16 * f, 16, 640, unit + 60)

                ffn_units(0, 0)
                units(wM, 48, 0, 24, 1024, U_MEM)
                with sp.Fori(0, 2) as j:
                    for i in range(12):
                        f, kind = i // 3, i % 3
                        s = (U_GBC + i) % RAW_SLOTS
                        sp.wait_ge(split_done, l * UNITS + j * 12 + (U_GBC + i + 1))
                        if kind < 2:
                            src = wM[bass.ds(l * 48 + j * 8 + (24 + 2 * f + kind), 1), :, :]
                        else:
                            src = wR[bass.ds(l * 16 + j * 4 + f, 1), :, :]
                        sp.dma_start(raw[:, s, 0:1024 if kind < 2 else 512],
                                     src.rearrange("a p n -> p (a n)")).then_inc(raw_landed[s], 16)
                units(wR, 16, KD, KD, 512, U_BA)
                units(wM, 48, 40, KD, 1024, U_WO)
                ffn_units(1, U_FFN2)

            for i in range(4):
                sp.wait_ge(out_ready, 2 * i + 2)
                sp.dma_start(out[:, 2 * i:2 * i + 2, :], gate_a[:, 2 * i:2 * i + 2, :]).then_inc(out_stored[i], 16)
            for i in range(4):
                sp.wait_ge(out_stored[i], 16)

        @block.gpsimd
        def _(pool):
            for _s in range(RAW_SLOTS):
                pool.sem_inc(split_done, 1)

            def split(l, group, unit, slot, cols):
                w = slot % SPLIT_SLOTS
                pool.wait_ge(raw_landed[slot], (l * (UNITS // RAW_SLOTS) + group) * 16 + 16)
                apart(pool, (unit_used, unit + 1))
                pool.tensor_scalar(wH[:, w, 0:cols], raw[:, slot, 0:cols], 1.0, 0.0, ALU.mult, ALU.add
                                   ).then_inc(rounded, 1)
                pool.wait_ge(rounded, unit + 1)
                pool.tensor_tensor(wL[:, w, 0:cols], raw[:, slot, 0:cols], wH[:, w, 0:cols].bitcast(F32),
                                   ALU.subtract).then_inc(split_done, 1)

            with pool.Fori(0, L) as l:
                def units(first, count, cols):
                    with pool.Fori(0, count // RAW_SLOTS) as j:
                        for s in range(RAW_SLOTS):
                            split(l, j + first // RAW_SLOTS, l * UNITS + j * RAW_SLOTS + (first + s), s, cols)

                def ffn_units(first):
                    units(first, 24, 1024)
                    units(first + 24, 16, 768)
                    units(first + 40, 20, 1024)
                    units(first + 60, 16, 640)

                ffn_units(0)
                units(U_MEM, 24, 1024)
                with pool.Fori(0, 2) as j:
                    for i in range(12):
                        split(l, j * 3 + (U_GBC + i) // RAW_SLOTS, l * UNITS + j * 12 + (U_GBC + i),
                              (U_GBC + i) % RAW_SLOTS, 1024 if i % 3 < 2 else 512)
                units(U_BA, KD, 512)
                units(U_WO, KD, 1024)
                ffn_units(U_FFN2)

        @block.tensor
        def _(pe):
            for _s in range(SPLIT_SLOTS):
                pe.sem_inc(unit_used, 1)
            pe.sem_inc(norm_taken, 1)

            def take_unit(unit):
                pe.wait_ge(split_done, unit + 1 + RAW_SLOTS)

            def free_bank(chunk):
                pe.wait_ge(evacuated, chunk + 1)

            def exact(dst, w, tiles, hi, lo, first=True, last=True, before=None, within=None):
                for i, (t, k) in enumerate(tiles):
                    if before:
                        before(k)
                    a, b = wH[:, w, t * P:(t + 1) * P], wL[:, w, t * P:(t + 1) * P]
                    pe.matmul(dst, a, hi[:, k, :], start=first and i == 0, stop=False)
                    pe.matmul(dst, b, hi[:, k, :], start=False, stop=False)
                    mm = pe.matmul(dst, a, lo[:, k, :], start=False, stop=last and i == len(tiles) - 1)
                    if within and i in within:
                        within[i]()
                return mm

            def sum_rows(src, n, cols=T):
                pe.wait_ge(norm_taken, n)
                for b in range(cols // P):
                    mm = pe.matmul(obank[:, b:b + 1], src[:, b * P:(b + 1) * P], ones[:, 0:1], start=True, stop=True)
                mm.then_inc(norm_sum, 1)

            def spread(diag, n, cols=T):
                pe.wait_ge(norm_diag, n)
                pe.matmul(obank[:, 0:cols], ones, diag[:, 0:cols], start=True, stop=True).then_inc(norm_spread, 1)

            pe.wait_ge(const_loaded, 16)
            pe.wait_ge(rel_loaded, 32)
            pe.matmul(sbank[0][0:H, 0:NBIAS], rel_sb, q[0:BUCKETS, 0, 0:NBIAS], start=True, stop=True
                      ).then_inc(bias_full, 1)

            with pe.Fori(0, L) as l:
                def ffn(unit, chunk, u_from, hid_from, ssq_count, norm_n):
                    def hidden(j, u, c, first):
                        for i in range(4):
                            n, m = l * UNITS + j * 4 + (u + i), l * CHUNKS + j * 4 + (c + i)
                            take_unit(n)
                            free_bank(m)
                            ready = None
                            if first and i == 0:
                                def ready(k):
                                    pe.wait_ge(u_ready, l * 24 + (u_from + k + 1))
                            within = {3: lambda: spread(tb, l * 5 + norm_n)} if first and i == 2 else None
                            exact(bank[i][:, :], i % 2, [(k, k) for k in range(KD)], u0H, u0L,
                                  before=ready, within=within).then_inc(unit_used, 1)
                            if first and i == 0:
                                pe.wait_ge(ssq_added, l * 24 + ssq_count)
                                sum_rows(ssq[:, :], l * 5 + norm_n)

                    def outs(u, c, n_hid, hid):
                        half = n_hid // 2
                        with pe.Fori(0, 2) as j:
                            for i in range(4):
                                free_bank(l * CHUNKS + j * 4 + (c + i))
                                for part_ in range(2):
                                    take_unit(l * UNITS + j * 8 + (u + 2 * i + part_))
                                    tiles = [(t, t + half * part_) for t in range(half)]
                                    ready = None
                                    if i == 0:
                                        def ready(k):
                                            pe.wait_ge(hidden_ready, l * 44 + (hid + k + 1))
                                    exact(bank[i][:, :], part_, tiles, hidH, hidL, first=part_ == 0,
                                          last=part_ == 1, before=ready).then_inc(unit_used, 1)

                    hidden(0, unit, chunk, True)
                    with pe.Fori(1, HALF[0] // 2) as j:
                        hidden(j, unit, chunk, False)
                    outs(unit + 24, chunk + 24, HALF[0], hid_from)
                    if unit == 0:
                        pe.wait_ge(mem_ssq, l * KD + KD)
                        sum_rows(ssq[:, 0:M], l * 5 + 2, M)
                    with pe.Fori(0, HALF[1] // 2) as j:
                        hidden(j, unit + 40, chunk + 32, False)
                    if unit == 0:
                        spread(ssq, l * 5 + 2, M)
                    outs(unit + 60, chunk + 52, HALF[1], hid_from + HALF[0])

                ffn(0, 0, 0, 0, 8, 1)

                for i in range(4):
                    take_unit(l * UNITS + (U_MEM + i))
                    if i < 3:
                        free_bank(l * CHUNKS + (C_MEM + i))
                    w = i % 2
                    if i < 2:
                        for k in range(KD):
                            pe.wait_ge(mem_ready, l * KD + (k + 1))
                            a, b = wH[:, w, k * P:(k + 1) * P], wL[:, w, k * P:(k + 1) * P]
                            pe.matmul(bank[i][:, 0:M], a, mem_hi[:, k, :], start=k == 0, stop=False)
                            pe.matmul(bank[i][:, 0:M], b, mem_hi[:, k, :], start=False, stop=False)
                            mm = pe.matmul(bank[i][:, 0:M], a, mem_lo[:, k, :], start=False, stop=k == KD - 1)
                    else:
                        if i == 2:
                            free_bank(l * CHUNKS + (C_MEM + 3))
                        for mb in range(2):
                            rows = slice(mb * P, (mb + 1) * P)
                            for t in range(4):
                                k = 4 * (i - 2) + t
                                a, b = wH[:, w, t * M:(t + 1) * M], wL[:, w, t * M:(t + 1) * M]
                                dst = bank[2 + mb][:, 0:M]
                                pe.matmul(dst, mem_hi[:, k, rows], a, start=k == 0, stop=False)
                                pe.matmul(dst, mem_hi[:, k, rows], b, start=False, stop=False)
                                mm = pe.matmul(dst, mem_lo[:, k, rows], a, start=False, stop=k == KD - 1)
                    mm.then_inc(unit_used, 1)
                    if i == 0:
                        pe.wait_ge(ssq_added, l * 24 + 16)
                        sum_rows(ssq[:, :], l * 5 + 3)
                    if i == 1:
                        spread(tb, l * 5 + 3)

                def s_bank_free(use):
                    n = S_INDEX[use]
                    if n < 2:
                        return n % 2, ()
                    kind, i = S_USES[n - 2]
                    if kind == "score":
                        return n % 2, (relu_ready, l * N_SCORES + (i + 1))
                    step, at = STEPS[i][0], KIND_INDEX[i] + 1
                    return n % 2, {"A": lambda: (logits_read, l * 32 + at),
                                   "C": lambda: (exp_done, l * N_SOFT + (SOFTMAX.index(i) + 1)),
                                   "Q": lambda: (qlat_ready, l * 8 + at),
                                   "U": lambda: (ya_ready, l * 8 + at),
                                   "B": lambda: (yb_ready, l * 2 + at)}[step]()

                def score(s):
                    qb, hd = 1 + s // IH, s % IH
                    width = P * (qb + 1)
                    if s == 0:
                        pe.wait_ge(ik_low, l + 1)
                        pe.wait_ge(iq_stacked, l * 8 + 8)
                        pe.wait_ge(iq_low, l * 16 + 16)
                    n, free = s_bank_free(("score", s))
                    if free:
                        pe.wait_ge(*free)
                    dst = sbank[n]
                    pe.matmul(dst[:, 0:width], iq_stack[0:3 * ID, hd, (qb - 1) * P:qb * P],
                              ik_stack[0:3 * ID, 0:width], start=True, stop=True).then_inc(s_full, 1)

                def logits(i):
                    kind, a, b = STEPS[i]
                    if kind == "N":
                        return
                    n, free = s_bank_free(("step", i))
                    if kind != "B":
                        pe.wait_ge(*free)
                    dst = sbank[n]
                    if kind == "C":
                        if i == 0:
                            pe.wait_ge(evacuated, chunk_at(l, C_IN + 5))
                        rows = slice(64 * b, 64 * b + 64)
                        for j in range(2):
                            mm = pe.matmul(dst[:, j * M:(j + 1) * M], qc[rows, j, a * P:(a + 1) * P],
                                           kc[rows, j, :], start=True, stop=True)
                    elif kind == "B":
                        apart(pe, free, (pooled, l * 4 + 4))
                        for j in range(2):
                            rows = slice(64 * j, 64 * j + 64)
                            mm = pe.matmul(dst[rows, :], pr[rows, W_POOL + 64 * a:W_POOL + 64 * a + 64],
                                           (za, zb)[j][rows, a, :], start=True, stop=True)
                    elif kind == "Q":
                        if a == 0 and b == 0:
                            pe.wait_ge(evacuated, chunk_at(l, C_IN + 9))
                        rows = slice(64 * b, 64 * b + 64)
                        for j in range(4):
                            mm = pe.matmul(dst[:, j * P:(j + 1) * P], pr[rows, W_UK + P * j:W_UK + P * (j + 1)],
                                           q[rows, j, a * P:(a + 1) * P], start=True, stop=True)
                    elif kind == "A":
                        pe.wait_ge(qlat_ready, l * 8 + (2 * a + b // 4 + 1))
                        width = P * (a + 1)
                        mm = pe.matmul(dst[:, 0:width], qlat[:, b, :], ckv[:, 0:width], start=True, stop=True)
                    elif kind == "U":
                        pe.wait_ge(olat_ready, l * 8 + (2 * a + b + 1))
                        for j in range(4):
                            hd = head(4 * b + j)
                            mm = pe.matmul(dst[64 * b:64 * b + 64, j * P:(j + 1) * P],
                                           pr[:, W_UV + HD * hd:W_UV + HD * hd + HD],
                                           olat[:, j * P:(j + 1) * P], start=True, stop=True)
                    mm.then_inc(s_full, 1)

                def turn(i):
                    kind, a, b = STEPS[i]
                    m = SOFTMAX.index(i)
                    pe.wait_ge(probs_ready, l * N_SOFT + (m + 1))
                    if m:
                        pe.wait_ge(pt_ready, l * N_SOFT + m)
                    else:
                        pe.wait_ge(c_ready, l + 1)
                    n = 4 if kind == "C" else a + 1
                    for kb in range(n):
                        mm = pe.transpose(tbank[:, kb * P:(kb + 1) * P],
                                          probs[:, m % 3, kb * P:(kb + 1) * P], ident)
                    mm.then_inc(t_full, 1)

                def values(i):
                    kind, a, b = STEPS[i]
                    m = SOFTMAX.index(i)
                    pe.wait_ge(pt_ready, l * N_SOFT + (m + 1))
                    if kind == "C":
                        if m:
                            pe.wait_ge(yc_ready, l * 8 + m)
                        for j in range(2):
                            for mb in range(2):
                                mm = pe.matmul(obank[64 * b:64 * b + 64, j * P:(j + 1) * P],
                                               vc[:, mb, (2 * j + b) * HD:(2 * j + b + 1) * HD],
                                               pt[:, m % 2, (2 * j + mb) * P:(2 * j + mb + 1) * P],
                                               start=mb == 0, stop=mb == 1)
                    else:
                        if b % 4 == 0:
                            g = 2 * a + b // 4
                            if g:
                                pe.wait_ge(olat_ready, l * 8 + g)
                            else:
                                pe.wait_ge(yc_ready, l * 8 + 8)
                        region = slice((b % 4) * P, (b % 4) * P + P)
                        for kb in range(a + 1):
                            mm = pe.matmul(obank[:, region], c_tok[:, kb, :],
                                           pt[:, m % 2, kb * P:(kb + 1) * P], start=kb == 0, stop=kb == a)
                    mm.then_inc(v_full, 1)

                def step(i):
                    if i >= 3 and i - 3 in SOFTMAX:
                        values(i - 3)
                    if i >= 2 and i - 2 in SOFTMAX:
                        turn(i - 2)
                    logits(i)

                def small_steps(mid, scores):
                    within = {MID: lambda: [step(i) for i in mid]}
                    for j, tile in enumerate(SCORES_AFTER):
                        within[tile] = lambda j=j: [score(s) for s in scores[j:j + 1]]
                    return within

                for at in SLOTS:
                    kind, i = at
                    mid, end, scores, _ = PLAN[at]
                    if kind == "in":
                        off = i if i < N_IN else N_IN + 3 * ((i - N_IN) // 2) + (i - N_IN) % 2
                        cof = i if i < N_IN else N_IN + 4 * ((i - N_IN) // 2) + (i - N_IN) % 2
                        take_unit(l * UNITS + (U_IN + off))
                        free_bank(l * CHUNKS + (C_IN + cof))
                        ready = None
                        if i == 0:
                            def ready(k):
                                pe.wait_ge(u_ready, l * 24 + (8 + k + 1))
                        exact(bank[(C_IN + cof) % BANKS][:, :], (U_IN + off) % 2,
                              [(k, k) for k in range(KD)], u1H, u1L, before=ready,
                              within=small_steps(mid, scores)).then_inc(unit_used, 1)
                    else:
                        take_unit(l * UNITS + (U_GBC + 3 * i + 2))
                        w = (U_GBC + 3 * i + 2) % 2
                        c = C_GBC + 4 * i + 2
                        free_bank(l * CHUNKS + (c + 1))
                        if i == 0:
                            pe.wait_ge(yb_ready, l * 2 + 2)
                            pe.wait_ge(yc_ready, l * 8 + 8)
                        exact(bank[c % BANKS][:, :], w, [(0, 4), (1, 5)], yH, yL)
                        exact(bank[(c + 1) % BANKS][:, :], w, [(2, 6), (3, 7)], yH, yL).then_inc(unit_used, 1)
                    if at == ("in", 2):
                        apart(pe, (ik_ready, l * 3 + 3))
                        for qb in range(QB):
                            mm = pe.transpose(tbank[:, qb * IH:(qb + 1) * IH], iwT[:, qb * P:(qb + 1) * P],
                                              cst[0:8, K_ID:K_ID + 8])
                        mm.then_inc(iw_full, 1)
                        pe.wait_ge(ckv_squared, l + 1)
                        sum_rows(ckv_sq, l * 5 + 4)
                    if at == ("in", 3):
                        spread(tb, l * 5 + 4)
                    if at == ("in", 5):
                        pe.wait_ge(ckv_ready, l + 1)
                        pe.wait_ge(iw_ready, l + 1)
                        for kb in range(QB):
                            mm = pe.transpose(tbank[:, kb * P:(kb + 1) * P], ckv[:, kb * P:(kb + 1) * P], ident)
                        mm.then_inc(c_full, 1)
                    for i in end:
                        step(i)

                for f in range(KD):
                    take_unit(l * UNITS + (U_BA + f))
                    free_bank(l * CHUNKS + (C_BA + f))
                    if f == 0:
                        pe.wait_ge(ya_ready, l * 8 + 8)
                    exact(bank[(C_BA + f) % BANKS][:, :], (U_BA + f) % 2, [(k, k) for k in range(4)],
                          yH, yL).then_inc(unit_used, 1)
                for f in range(KD):
                    take_unit(l * UNITS + (U_WO + f))
                    free_bank(l * CHUNKS + (C_WO + f))
                    ready = None
                    if f == 0:
                        def ready(k):
                            pe.wait_ge(merged_ready, l * KD + (k + 1))
                    exact(bank[(C_WO + f) % BANKS][:, :], (U_WO + f) % 2, [(k, k) for k in range(KD)],
                          u1H, u1L, before=ready).then_inc(unit_used, 1)

                ffn(U_FFN2, C_FFN2, 16, sum(HALF), 24, 5)

            pe.wait_ge(ssq_added, L * 24 + 8)
            sum_rows(ssq[:, :], L * 5 + 1)
            spread(tb, L * 5 + 1)

        @block.scalar
        def _(act):
            own = Steps(act, scalar_step)

            def root(n, blocks=QB):
                act.wait_ge(norm_var, n)
                act.activation(norm[:, 1, 0:blocks], norm[:, 0, 0:blocks], ACT.Sqrt).then_inc(norm_root, 1)

            for i in range(4):
                if i == 2:
                    act.wait_ge(const_loaded, 16)
                act.dma_start(h[:, 2 * i:2 * i + 2, :], xT[:, 2 * i:2 * i + 2, :]).then_inc(x_loaded[i], 16)
            for k in range(KD):
                if k % 2 == 0:
                    act.wait_ge(x_loaded[k // 2], 16)
                act.activation(u0H[:, k, :], h[:, k, :], ACT.Copy,
                               scale=cst[:, K_GAIN + k:K_GAIN + k + 1]).then_inc(u_high, 1)
                if k:
                    act.wait_ge(ssq_added, k)
                act.activation(sq[:, :], h[:, k, :], ACT.Square).then_inc(squared, 1)
            act.dma_start(far_bias[:, :], bass.AP(tensor=rel.tensor, offset=(BUCKETS - 1) * H,
                                                  ap=[[0, P], [1, H]])).then_inc(far_loaded, 16)
            act.wait_ge(bias_full, 1)
            act.activation(bias_table, sbank[0][0:H, 0:NBIAS], ACT.Copy).then_inc(bias_copied, 1)
            act.wait_ge(bias_copied, 1)
            act.dma_start(bias_rows, bass.AP(tensor=bias_table.tensor, offset=bias_table.offset,
                                             ap=[bias_table.ap[0], [0, P], [1, NBIAS]])).then_inc(bias_stored, 16)
            act.wait_ge(bias_stored, 16)
            act.dma_start(near_bias[:, :, :], bass.AP(tensor=bias_rows.tensor, offset=P - 1,
                                                      ap=[[NBIAS - 1, P], [P * NBIAS, H], [1, 2 * P]])
                          ).then_inc(bias_loaded, 16)

            with act.Fori(0, L) as l:
                def ffn(chunk, hid_from, root_n, hi, g, n_from):
                    def hidden(j, c, hid):
                        for i in range(2):
                            act.wait_ge(evacuated, chunk_at(l, c + 2 * i) + j * 4)
                            act.activation(sg[:, 0, :], ta[:, :], ACT.Sigmoid).then_inc(sigmoid_ready, 1)
                            apart(act, (gated, l * 44 + j * 2 + (hid + i + 1)))
                            act.activation(hidH[:, bass.ds(j * 2 + i, 1), :].rearrange("p a t -> p (a t)"),
                                           sg[:, 1, :], ACT.Copy).then_inc(hidden_high, 1)

                    root(l * 5 + root_n)
                    with act.Fori(0, HALF[0] // 2) as j:
                        hidden(j, chunk, hid_from)
                    if chunk == 0:
                        act.wait_ge(mem_loaded, l * 16 + 16)
                        for k in range(KD):
                            if k:
                                act.wait_ge(mem_ssq, l * KD + k)
                            act.activation(sq[:, 0:M], mem[:, k, :], ACT.Square).then_inc(mem_squared, 1)
                        root(l * 5 + 2, M // P)
                    with act.Fori(0, HALF[1] // 2) as j:
                        hidden(j, chunk + 32, hid_from + HALF[0])

                def last_half(chunk, n_from, g, hi):
                    with act.Fori(0, KD) as k:
                        apart(act, (evacuated, chunk_at(l, chunk + 52) + k))
                        kk = bass.ds(k, 1)
                        row = lambda t: t[:, kk, :].rearrange("p a t -> p (a t)")
                        act.activation(row(hi), row(h), ACT.Copy, scale=gain(g, k)).then_inc(u_high, 1)
                        apart(act, (ssq_added, l * 24 + k + n_from))
                        act.activation(sq[:, :], row(h), ACT.Square).then_inc(squared, 1)

                ffn(0, 0, 1, u1H, G_MIX, 8)
                act.wait_ge(mem_normed, l + 1)
                for k in range(KD):
                    act.activation(mem_hi[:, k, :], mem[:, k, :], ACT.Copy,
                                   scale=pr[:, G_MEM + k:G_MEM + k + 1]).then_inc(mem_high, 1)
                last_half(0, 8, G_MIX, u1H)

                root(l * 5 + 3)

                def exps(i):
                    kind, a, b = STEPS[i]
                    if kind == "N":
                        return
                    n = S_INDEX[("step", i)]
                    src = sbank[n % 2]
                    if kind == "A":
                        m = SOFTMAX.index(i)
                        width = P * (a + 1)
                        p = probs[:, m % 3, 0:width]
                        act.wait_ge(logit_max, l * N_SOFT + (m + 1))
                        act.activation(p, p, ACT.Exp, bias=nmax[:, m % 4, 0:1],
                                       accum_out=rsum[:, m % 4, 0:1]).then_inc(exp_done, 1)
                    elif kind == "C":
                        m = SOFTMAX.index(i)
                        act.wait_ge(logit_max, l * N_SOFT + (m + 1))
                        if m >= 3:
                            act.wait_ge(t_full, l * N_SOFT + (m - 2))
                        for j in range(2):
                            e = act.activation(probs[:, m % 3, j * M:(j + 1) * M], src[:, j * M:(j + 1) * M],
                                               ACT.Exp, bias=nmax[:, m % 4, j:j + 1],
                                               accum_out=rsum[:, m % 4, j:j + 1])
                        e.then_inc(exp_done, 1)
                    elif kind == "Q":
                        act.wait_ge(s_full, l * len(S_USES) + (n + 1))
                        act.activation(qlat[:, 4 * b:4 * b + 4, :].rearrange("p a t -> p (a t)"), src[:, :],
                                       ACT.Copy, scale=HD ** -0.5).then_inc(qlat_ready, 1)
                    elif kind == "U":
                        act.wait_ge(s_full, l * len(S_USES) + (n + 1))
                        rows = slice(64 * b, 64 * b + 64)
                        act.activation(yH[rows, 0:4, a * P:(a + 1) * P],
                                       src[rows, :].rearrange("p (a t) -> p a t", t=P),
                                       ACT.Copy).then_inc(ya_high, 1)
                    elif kind == "B":
                        act.wait_ge(s_full, l * len(S_USES) + (n + 1))
                        act.activation(yH[:, 4 + a, :], src[:, :], ACT.Copy,
                                       scale=pr[:, G_POOL + a:G_POOL + a + 1]).then_inc(yb_high, 1)

                def normalise(i):
                    kind, a, b = STEPS[i]
                    m = SOFTMAX.index(i)
                    act.wait_ge(sum_inverted, l * N_SOFT + (m + 1))
                    parts = [(0, P * (a + 1))] if kind == "A" else [(0, M), (M, 2 * M)]
                    for j, (x, y) in enumerate(parts):
                        e = act.activation(probs[:, m % 3, x:y], probs[:, m % 3, x:y], ACT.Copy,
                                           scale=rinv[:, m % 4, j:j + 1])
                    e.then_inc(probs_ready, 1)

                def take_turned(i):
                    kind, a, b = STEPS[i]
                    m = SOFTMAX.index(i)
                    width = 4 * P if kind == "C" else P * (a + 1)
                    act.wait_ge(t_full, l * N_SOFT + (m + 1))
                    if m >= 2:
                        act.wait_ge(v_full, l * N_SOFT + (m - 1))
                    act.activation(pt[:, m % 2, 0:width], tbank[:, 0:width], ACT.Copy).then_inc(pt_ready, 1)

                def take_values(i):
                    kind, a, b = STEPS[i]
                    m = SOFTMAX.index(i)
                    if kind == "C":
                        act.wait_ge(v_full, l * N_SOFT + (m + 1))
                        rows = slice(64 * b, 64 * b + 64)
                        act.activation(yH[rows, 6:8, a * P:(a + 1) * P],
                                       obank[rows, 0:2 * P].rearrange("p (a t) -> p a t", t=P),
                                       ACT.Copy).then_inc(yc_high, 1)
                    elif b % 4 == 3:
                        act.wait_ge(v_full, l * N_SOFT + (m + 1))
                        act.activation(olat, obank[:, :], ACT.Copy).then_inc(olat_ready, 1)

                def gate(at):
                    c = N_IN + 4 * ((at - N_IN) // 2) + (at - N_IN) % 2
                    g = gate_bc[:, at % 2, :]
                    act.wait_ge(evacuated, chunk_at(l, C_IN + c))
                    own.done(act.activation(g, g, ACT.Exp, scale=-1.0))
                    own.wait()
                    own.done(act.activation(g, g, ACT.Ln, bias=cst[:, K_ONE:K_ONE + 1]))
                    own.wait()
                    act.activation(g, g, ACT.Exp, scale=-1.0).then_inc(gate_exp, 1)

                def step(i, gate_at=None):
                    if i >= 3 and i - 3 in SOFTMAX:
                        take_values(i - 3)
                    if i >= 2 and i - 2 in SOFTMAX:
                        take_turned(i - 2)
                    if gate_at is not None:
                        gate(gate_at)
                    exps(i)
                    if i in SOFTMAX:
                        normalise(i)

                def relus(scores):
                    for s in scores:
                        qb = 1 + s // IH
                        width = P * (qb + 1)
                        n = S_INDEX[("score", s)]
                        act.wait_ge(s_full, l * len(S_USES) + (n + 1))
                        if s >= 2:
                            act.wait_ge(score_added, l * N_SCORES + (s - 1))
                        act.activation(relu[:, s % 2, 0:width], sbank[n % 2][:, 0:width], ACT.Relu,
                                       scale=ID ** -0.5).then_inc(relu_ready, 1)

                for at in SLOTS:
                    kind, i = at
                    mid, end, scores, _ = PLAN[at]
                    relus(scores[0:2])
                    for n in mid:
                        step(n)
                    relus(scores[2:4])
                    if at == ("in", 0):
                        act.wait_ge(evacuated, chunk_at(l, C_IN))
                        for g in range(2):
                            act.activation(ik_stack[ID * g:ID * g + ID, :], misc[0:ID, :], ACT.Copy
                                           ).then_inc(ik_ready, 1)
                        act.activation(iwT, misc[ID:ID + IH, :], ACT.Copy).then_inc(ik_ready, 1)
                    if at == ("in", 1):
                        act.wait_ge(evacuated, chunk_at(l, C_IN + 1))
                        act.activation(ckv_sq, ckv[:, :], ACT.Square).then_inc(ckv_squared, 1)
                    if at == ("in", 2):
                        root(l * 5 + 4)
                        act.preload_act_table_set("natural_log_exp_and_others")
                    if at in (("in", 2), ("in", 3)):
                        c = i - 2
                        act.wait_ge(evacuated, chunk_at(l, C_IN + i))
                        act.activation(iqH[:, c, :], iq[:, c, P:T], ACT.Copy).then_inc(iq_high, 1)
                        act.wait_ge(iq_high, l * 2 + (c + 1))
                        for j in range(4):
                            act.activation(iq_stack[0:ID, 4 * c + j, :], iqH[ID * j:ID * j + ID, c, :], ACT.Copy
                                           ).then_inc(iq_stacked, 1)
                    if at == ("in", 5):
                        act.wait_ge(c_full, l + 1)
                        act.activation(c_tok.rearrange("p b r -> p (b r)"), tbank[:, :], ACT.Copy
                                       ).then_inc(c_ready, 1)
                    gate_at = i if kind == "in" and i >= N_IN else None
                    for n in end:
                        step(n, gate_at)
                    if gate_at is not None and not end:
                        gate(gate_at)

                for f in range(KD):
                    act.activation(gate_a[:, f, :], gate_a[:, f, :], ACT.Sigmoid).then_inc(gate_ready, 1)
                for f in range(KD):
                    act.wait_ge(merged_sum, l * KD + (f + 1))
                    act.activation(u1H[:, f, :], (tb, sg)[0][:, :], ACT.Copy).then_inc(merged_high, 1)
                for k in range(KD):
                    act.wait_ge(evacuated, chunk_at(l, C_WO + k))
                    act.activation(u0H[:, k, :], h[:, k, :], ACT.Copy,
                                   scale=pr[:, G_FFN2 + k:G_FFN2 + k + 1]).then_inc(u_high, 1)
                    act.wait_ge(ssq_added, l * 24 + (16 + k))
                    act.activation(sq[:, :], h[:, k, :], ACT.Square).then_inc(squared, 1)
                ffn(C_FFN2, sum(HALF), 5, u0H, G_NEXT, 24)
                last_half(C_FFN2, 24, G_NEXT, u0H)
                own.restart()
            root(L * 5 + 1)

        @block.vector
        def _(dve):
            own = Steps(dve, vector_step)
            for _b in range(BANKS):
                dve.sem_inc(evacuated, 1)

            def inverse_rms(n, diag, count, blocks=QB):
                v, s, r = (norm[:, i, 0:blocks] for i in range(3))
                dve.wait_ge(norm_sum, n)
                dve.tensor_scalar(v, obank[:, 0:blocks], 1.0 / count, EPS, ALU.mult, ALU.add).then_inc(norm_var, 1)
                dve.wait_ge(norm_root, n)
                own.done(dve.reciprocal(r, s))
                own.wait()
                own.done(dve.tensor_tensor(s, r, r, ALU.mult))
                own.wait()
                own.done(dve.tensor_tensor(s, s, v, ALU.mult))
                own.wait()
                own.done(dve.tensor_scalar(s, s, -0.5, 1.5, ALU.mult, ALU.add))
                own.wait()
                own.done(dve.tensor_tensor(r, r, s, ALU.mult))
                own.wait()
                for b in range(blocks):
                    if b == blocks - 1:
                        own.wait()
                    ins = dve.tensor_scalar(diag[:, b * P:(b + 1) * P], ident, r[:, b:b + 1], None, ALU.mult)
                    if b < blocks - 1:
                        own.done(ins)
                    else:
                        ins.then_inc(norm_diag, 1)

            def take_rms(n, dst, cols=T):
                dve.wait_ge(norm_spread, n)
                own.done(dve.tensor_copy(dst, obank[:, 0:cols]))
                own.wait()
                dve.sem_inc(norm_taken, 1)

            own.done(dve.memset(ssq[:, :], 0.0))
            own.wait()
            dve.wait_ge(const_loaded, 16)
            for k in range(KD):
                if k % 2 == 0:
                    dve.wait_ge(x_loaded[k // 2], 16)
                dve.wait_ge(u_high, k + 1)
                dve.scalar_tensor_tensor(u0L[:, k, :], h[:, k, :], cst[:, K_GAIN + k:K_GAIN + k + 1],
                                         u0H[:, k, :].bitcast(F32), ALU.mult, ALU.subtract).then_inc(u_ready, 1)
                dve.wait_ge(squared, k + 1)
                if k:
                    dve.wait_ge(ssq_added, k)
                dve.tensor_tensor(ssq[:, :], ssq[:, :], sq[:, :], ALU.add).then_inc(ssq_added, 1)
            own.restart()

            with dve.Fori(0, L) as l:
                def ffn(unit, chunk, hid_from, norm_n):
                    def hidden(j, u, c, hid):
                        for i in range(2):
                            n = l * 44 + j * 2 + (hid + i + 1)
                            dve.wait_ge(unit_used, unit_at(l, u + 2 * i) + j * 4)
                            dve.tensor_tensor(ta[:, :], bank[2 * i][:, :], rms[:, :], ALU.mult).then_inc(evacuated, 1)
                            dve.wait_ge(unit_used, unit_at(l, u + 2 * i + 1) + j * 4)
                            dve.tensor_tensor(tb[:, :], bank[2 * i + 1][:, :], rms[:, :], ALU.mult
                                              ).then_inc(evacuated, 1)
                            dve.wait_ge(evacuated, chunk_at(l, c + 2 * i + 1) + j * 4)
                            dve.wait_ge(sigmoid_ready, n)
                            own.done(dve.tensor_tensor(ta[:, :], ta[:, :], sg[:, 0, :], ALU.mult))
                            own.wait()
                            dve.tensor_tensor(sg[:, 1, :], ta[:, :], tb[:, :], ALU.mult).then_inc(gated, 1)
                            dve.wait_ge(hidden_high, n)
                            kk = bass.ds(j * 2 + i, 1)
                            dve.tensor_tensor(hidL[:, kk, :].rearrange("p a t -> p (a t)"), sg[:, 1, :],
                                              hidH[:, kk, :].rearrange("p a t -> p (a t)").bitcast(F32),
                                              ALU.subtract).then_inc(hidden_ready, 1)
                        own.restart()

                    inverse_rms(l * 5 + norm_n, tb, D)
                    take_rms(l * 5 + norm_n, rms[:, :])
                    own.restart()
                    with dve.Fori(0, HALF[0] // 2) as j:
                        hidden(j, unit, chunk, hid_from)
                    if unit == 0:
                        own.done(dve.memset(ssq[:, 0:M], 0.0))
                        own.wait()
                        for k in range(KD):
                            dve.wait_ge(mem_squared, l * KD + (k + 1))
                            if k:
                                dve.wait_ge(mem_ssq, l * KD + k)
                            dve.tensor_tensor(ssq[:, 0:M], ssq[:, 0:M], sq[:, 0:M], ALU.add).then_inc(mem_ssq, 1)
                    with dve.Fori(0, 2) as j:
                        for i in range(4):
                            dve.wait_ge(unit_used, unit_at(l, unit + 24 + 2 * i + 1) + j * 8)
                            row = h[:, bass.ds(j * 4 + i, 1), :].rearrange("p a t -> p (a t)")
                            dve.scalar_tensor_tensor(row, bank[i][:, :], 0.5, row, ALU.mult, ALU.add
                                                     ).then_inc(evacuated, 1)
                    if unit == 0:
                        inverse_rms(l * 5 + 2, ssq, D, M // P)
                        own.restart()
                    with dve.Fori(0, HALF[1] // 2) as j:
                        hidden(j, unit + 40, chunk + 32, hid_from + HALF[0])
                    if unit == 0:
                        take_rms(l * 5 + 2, mem_rms[:, :], M)
                    dve.wait_ge(evacuated, chunk_at(l, chunk + 51))
                    own.done(dve.memset(ssq[:, :], 0.0))

                def finish_h(k, ps, c, scale, n, g, hi, lo):
                    row = (lambda t: t[:, k, :]) if isinstance(k, int) else (
                        lambda t: t[:, bass.ds(k, 1), :].rearrange("p a t -> p (a t)"))
                    dve.scalar_tensor_tensor(row(h), ps, scale, row(h), ALU.mult, ALU.add).then_inc(evacuated, 1)
                    dve.wait_ge(evacuated, c)
                    dve.wait_ge(u_high, n)
                    dve.scalar_tensor_tensor(row(lo), row(h), gain(g, k), row(hi).bitcast(F32),
                                             ALU.mult, ALU.subtract).then_inc(u_ready, 1)
                    dve.wait_ge(squared, n)
                    dve.wait_ge(ssq_added, n - 1)
                    dve.tensor_tensor(ssq[:, :], ssq[:, :], sq[:, :], ALU.add).then_inc(ssq_added, 1)

                def last_half(unit, chunk, n_from, g, hi, lo):
                    own.restart()
                    with dve.Fori(0, 2) as j:
                        for i in range(4):
                            dve.wait_ge(unit_used, unit_at(l, unit + 60 + 2 * i + 1) + j * 8)
                            finish_h(j * 4 + i, bank[i][:, :], chunk_at(l, chunk + 52 + i) + j * 4, 0.5,
                                     l * 24 + j * 4 + (n_from + i + 1), g, hi, lo)

                ffn(0, 0, 0, 1)
                dve.wait_ge(mem_loaded, l * 16 + 16)
                dve.wait_ge(unit_used, unit_at(l, 59))
                for k in range(KD):
                    ins = dve.tensor_tensor(mem[:, k, :], mem[:, k, :], mem_rms[:, :], ALU.mult)
                    if k < KD - 1:
                        own.done(ins)
                    else:
                        ins.then_inc(mem_normed, 1)
                dve.wait_ge(par_loaded, l * 16 + 16)
                for k in range(KD):
                    dve.wait_ge(mem_high, l * KD + (k + 1))
                    dve.scalar_tensor_tensor(mem_lo[:, k, :], mem[:, k, :], pr[:, G_MEM + k:G_MEM + k + 1],
                                             mem_hi[:, k, :].bitcast(F32), ALU.mult, ALU.subtract
                                             ).then_inc(mem_ready, 1)
                last_half(0, 0, 8, G_MIX, u1H, u1L)

                def mem_kv(i):
                    dve.wait_ge(unit_used, unit_at(l, U_MEM + (i if i < 2 else 3)))
                    dst = kc[:, i, :] if i < 2 else vc[:, i - 2, :]
                    dve.tensor_copy(dst, bank[i][:, 0:M]).then_inc(evacuated, 1)

                dve.wait_ge(bias_loaded, 16)
                dve.wait_ge(far_loaded, 16)
                mem_kv(0)
                inverse_rms(l * 5 + 3, tb, D)
                mem_kv(1)
                take_rms(l * 5 + 3, rms[:, :])
                for i in range(2, 4):
                    mem_kv(i)

                rounds_done = [0]

                def pick_round():
                    qb, n = 1 + rounds_done[0] // (TOPK // 8), rounds_done[0] % (TOPK // 8)
                    rounds_done[0] += 1
                    own.done(dve.max(top8[:, :], picks[qb][:, :]))
                    own.wait()
                    own.done(dve.match_replace(picks[qb][:, :], top8[:, :], picks[qb][:, :], PICKED))
                    own.wait()
                    if n == TOPK // 8 - 1:
                        own.done(dve.tensor_scalar(picks[qb][:, :], picks[qb][:, :], PICKED, NEG,
                                                   ALU.not_equal, ALU.mult))
                        own.wait()

                def pick_rounds(n):
                    for _r in range(n):
                        if rounds_done[0] < (QB - 1) * (TOPK // 8):
                            pick_round()

                def add_score(s):
                    qb, hd = 1 + s // IH, s % IH
                    width = P * (qb + 1)
                    dve.wait_ge(relu_ready, l * N_SCORES + (s + 1))
                    w = iw[:, qb, hd:hd + 1]
                    if hd == 0:
                        dve.tensor_scalar(picks[qb][:, :], relu[:, s % 2, 0:width], w, None, ALU.mult
                                          ).then_inc(score_added, 1)
                    else:
                        dve.wait_ge(score_added, l * N_SCORES + s)
                        dve.scalar_tensor_tensor(picks[qb][:, :], relu[:, s % 2, 0:width], w, picks[qb][:, :],
                                                 ALU.mult, ALU.add).then_inc(score_added, 1)
                    if hd == IH - 1:
                        dve.wait_ge(score_added, l * N_SCORES + (s + 1))
                        last = picks[qb][:, qb * P:(qb + 1) * P]
                        own.done(dve.tensor_tensor(last, last, causal, ALU.add))
                        own.wait()

                def window_means(piece):

                    def widen(dst, src, by):
                        own.done(dve.tensor_tensor(dst[:, :, by:T], src[:, :, by:T], src[:, :, 0:T - by], ALU.add))
                        own.done(dve.tensor_copy(dst[:, :, 0:by], src[:, :, 0:by]))
                        own.wait()

                    if piece == 0:
                        dve.wait_ge(evacuated, chunk_at(l, C_IN + 11))
                        widen(za, z, 1)
                    if piece == 1:
                        widen(zb, za, 2)
                    if piece == 2:
                        widen(za[:, 1:2, :], zb[:, 1:2, :], 4)
                        widen(zb[64:128, 1:2, :], za[64:128, 1:2, :], 8)
                    for g, w in enumerate(WINDOWS):
                        if piece != 3 + g // 2:
                            continue
                        rows, c = slice(64 * (g % 2), 64 * (g % 2) + 64), g // 2
                        s = (za, zb)[g % 2][rows, c, :]
                        count = cst[rows, K_COUNT + WMAX * c:K_COUNT + WMAX * (c + 1)]
                        own.done(dve.scalar_tensor_tensor(s[:, WMAX:T], s[:, WMAX:T], 1.0 / w, z[rows, c, WMAX:T],
                                                          ALU.mult, ALU.subtract))
                        own.done(dve.tensor_tensor(s[:, 0:WMAX], s[:, 0:WMAX], count, ALU.mult))
                        own.wait()
                        dve.tensor_tensor(s[:, 0:WMAX], s[:, 0:WMAX], z[rows, c, 0:WMAX], ALU.subtract
                                          ).then_inc(pooled, 1)

                def logits(i):
                    kind, a, b = STEPS[i]
                    if kind in "NQ":
                        return
                    n = S_INDEX[("step", i)]
                    src = sbank[n % 2]
                    if kind == "A":
                        m = SOFTMAX.index(i)
                        if i == 0 or b == 0:
                            while a and rounds_done[0] < a * (TOPK // 8):
                                pick_round()
                        width, near = P * (a + 1), P * max(a - 1, 0)
                        p, mask = probs[:, m % 3, :], masks(a)
                        read = l * 32 + (KIND_INDEX[i] + 1)
                        dve.wait_ge(s_full, l * len(S_USES) + (n + 1))
                        if m >= 3:
                            dve.wait_ge(t_full, l * N_SOFT + (m - 2))
                        ins = dve.tensor_tensor(p[:, near:width], src[:, near:width],
                                                near_bias[:, head(b), 2 * P - (width - near):2 * P], ALU.add)
                        if near:
                            own.done(ins)
                            dve.scalar_tensor_tensor(p[:, 0:near], src[:, 0:near], far_bias[:, head(b):head(b) + 1],
                                                     mask[:, 0:near], ALU.add, ALU.add).then_inc(logits_read, 1)
                            own.wait()
                        else:
                            ins.then_inc(logits_read, 1)
                        dve.wait_ge(logits_read, read)
                        own.done(dve.tensor_tensor(p[:, near:width], p[:, near:width], mask[:, near:width], ALU.add))
                        own.wait()
                        dve.tensor_reduce(nmax[:, m % 4, 0:1], p[:, 0:width], AX.X, ALU.max, negate=True
                                          ).then_inc(logit_max, 1)
                    elif kind == "C":
                        m = SOFTMAX.index(i)
                        dve.wait_ge(s_full, l * len(S_USES) + (n + 1))
                        dve.tensor_reduce(nmax[:, m % 4, :], src[:, :].rearrange("p (a t) -> p a t", a=2), AX.X,
                                          ALU.max, negate=True).then_inc(logit_max, 1)
                    elif kind == "U":
                        dve.wait_ge(ya_high, l * 8 + (KIND_INDEX[i] + 1))
                        rows = slice(64 * b, 64 * b + 64)
                        dve.tensor_tensor(yL[rows, 0:4, a * P:(a + 1) * P],
                                          src[rows, :].rearrange("p (a t) -> p a t", t=P),
                                          yH[rows, 0:4, a * P:(a + 1) * P].bitcast(F32), ALU.subtract
                                          ).then_inc(ya_ready, 1)
                    elif kind == "B":
                        dve.wait_ge(yb_high, l * 2 + (a + 1))
                        dve.scalar_tensor_tensor(yL[:, 4 + a, :], src[:, :], pr[:, G_POOL + a:G_POOL + a + 1],
                                                 yH[:, 4 + a, :].bitcast(F32), ALU.mult, ALU.subtract
                                                 ).then_inc(yb_ready, 1)

                def invert(i):
                    m = SOFTMAX.index(i)
                    n = 1 if STEPS[i][0] == "A" else 2
                    dve.wait_ge(exp_done, l * N_SOFT + (m + 1))
                    dve.reciprocal(rinv[:, m % 4, 0:n], rsum[:, m % 4, 0:n]).then_inc(sum_inverted, 1)

                def low_values(i):
                    kind, a, b = STEPS[i]
                    m = SOFTMAX.index(i)
                    if kind == "C":
                        dve.wait_ge(yc_high, l * 8 + (m + 1))
                        rows = slice(64 * b, 64 * b + 64)
                        dve.tensor_tensor(yL[rows, 6:8, a * P:(a + 1) * P],
                                          obank[rows, 0:2 * P].rearrange("p (a t) -> p a t", t=P),
                                          yH[rows, 6:8, a * P:(a + 1) * P].bitcast(F32), ALU.subtract
                                          ).then_inc(yc_ready, 1)

                def step(i, n_picks):
                    logits(i)
                    if i >= 3 and i - 3 in SOFTMAX:
                        low_values(i - 3)
                    pick_rounds(min(n_picks, 1))
                    if i in SOFTMAX:
                        invert(i)
                    pick_rounds(n_picks - 1)

                for at in SLOTS:
                    kind, i = at
                    mid, end, scores, n_picks = PLAN[at]
                    for n in scores[0:2]:
                        add_score(n)
                    for n in mid:
                        step(n, n_picks[0])
                    for n in scores[2:4]:
                        add_score(n)
                    if kind == "in":
                        off = i if i < N_IN else N_IN + 3 * ((i - N_IN) // 2) + (i - N_IN) % 2
                        cof = i if i < N_IN else N_IN + 4 * ((i - N_IN) // 2) + (i - N_IN) % 2
                        src = bank[(C_IN + cof) % BANKS][:, :]
                        dve.wait_ge(unit_used, unit_at(l, U_IN + off))
                        if i == 0:
                            dve.tensor_tensor(misc[0:40, :], src[0:40, :], rms[0:40, :], ALU.mult
                                              ).then_inc(evacuated, 1)
                        elif 4 <= i < 6:
                            dve.scalar_tensor_tensor(qc[:, i - 4, :], src, HD ** -0.5, rms[:, :], ALU.mult,
                                                     ALU.mult).then_inc(evacuated, 1)
                        else:
                            dst = (ckv[:, :] if i == 1 else iq[:, i - 2, :] if i < 4 else q[:, i - 6, :] if i < 10
                                   else z[:, i - 10, :] if i < 12 else gate_a[:, i - 12, :] if i < N_IN
                                   else gate_bc[:, i % 2, :])
                            dve.tensor_tensor(dst, src, rms[:, :], ALU.mult).then_inc(evacuated, 1)
                    else:
                        dve.wait_ge(unit_used, unit_at(l, U_GBC + 3 * i + 2))
                        c = C_GBC + 4 * i + 2
                        dve.wait_ge(gate_exp, l * 16 + (2 * i + 2))
                        dve.tensor_tensor(ta[:, :], bank[c % BANKS][:, :], gate_bc[:, 0, :], ALU.mult
                                          ).then_inc(evacuated, 1)
                        dve.tensor_tensor(tb[:, :], bank[(c + 1) % BANKS][:, :], gate_bc[:, 1, :], ALU.mult
                                          ).then_inc(evacuated, 1)
                    if at == ("in", 2):
                        dve.wait_ge(ik_ready, l * 3 + 3)
                        dve.tensor_tensor(ik_stack[2 * ID:3 * ID, :], misc[0:ID, :], ik_stack[0:ID, :].bitcast(F32),
                                          ALU.subtract).then_inc(ik_low, 1)
                        dve.wait_ge(iw_full, l + 1)
                        dve.tensor_scalar(iw[:, :, :].rearrange("p a b -> p (a b)"), tbank[:, 0:QB * IH],
                                          IH ** -0.5, None, ALU.mult).then_inc(iw_ready, 1)
                        dve.wait_ge(iw_ready, l + 1)
                        inverse_rms(l * 5 + 4, tb, R)
                    if at in (("in", 2), ("in", 3)):
                        c = i - 2
                        dve.wait_ge(iq_high, l * 2 + (c + 1))
                        for j in range(4):
                            rows = slice(ID * j, ID * j + ID)
                            dve.tensor_tensor(iq_stack[ID:2 * ID, 4 * c + j, :], iq[rows, c, P:T],
                                              iqH[rows, c, :].bitcast(F32), ALU.subtract).then_inc(iq_low, 1)
                            dve.tensor_copy(iq_stack[2 * ID:3 * ID, 4 * c + j, :], iqH[rows, c, :]
                                            ).then_inc(iq_low, 1)
                    if at == ("in", 3):
                        take_rms(l * 5 + 4, ckv_rms)
                        dve.scalar_tensor_tensor(ckv[:, :], ckv[:, :], pr[:, G_KV:G_KV + 1], ckv_rms,
                                                 ALU.mult, ALU.mult).then_inc(ckv_ready, 1)
                    for n in end:
                        step(n, n_picks[1])
                    if kind == "bc":
                        dve.wait_ge(evacuated, chunk_at(l, c + 1))
                        own.done(dve.tensor_tensor(part[:, i, :], ta[:, :], tb[:, :], ALU.add))
                        own.wait()
                    if at in MEANS_AT:
                        window_means(MEANS_AT[at])
                def merged_low(f):
                    dve.wait_ge(merged_high, l * KD + (f + 1))
                    dve.tensor_tensor(u1L[:, f, :], tb[:, :], u1H[:, f, :].bitcast(F32), ALU.subtract
                                      ).then_inc(merged_ready, 1)

                for f in range(KD):
                    dve.wait_ge(unit_used, unit_at(l, U_BA + f))
                    if f:
                        dve.wait_ge(merged_sum, l * KD + f)
                    dve.wait_ge(gate_ready, l * KD + (f + 1))
                    dve.tensor_tensor(ta[:, :], bank[(C_BA + f) % BANKS][:, :], gate_a[:, f, :], ALU.mult
                                      ).then_inc(evacuated, 1)
                    if f:
                        merged_low(f - 1)
                        dve.wait_ge(merged_ready, l * KD + f)
                    dve.wait_ge(evacuated, chunk_at(l, C_BA + f))
                    dve.tensor_tensor(tb[:, :], ta[:, :], part[:, f, :], ALU.add).then_inc(merged_sum, 1)
                merged_low(KD - 1)
                own.done(dve.memset(ssq[:, :], 0.0))
                own.restart()
                for k in range(KD):
                    dve.wait_ge(unit_used, unit_at(l, U_WO + k))
                    finish_h(k, bank[(C_WO + k) % BANKS][:, :], chunk_at(l, C_WO + k), 1.0,
                             l * 24 + (16 + k + 1), G_FFN2, u0H, u0L)

                ffn(U_FFN2, C_FFN2, sum(HALF), 5)
                last_half(U_FFN2, C_FFN2, 24, G_NEXT, u0H, u0L)

            inverse_rms(L * 5 + 1, tb, D)
            take_rms(L * 5 + 1, rms[:, :])
            for k in range(KD):
                dve.scalar_tensor_tensor(gate_a[:, k, :], h[:, k, :], gain(G_NEXT, k), rms[:, :],
                                         ALU.mult, ALU.mult).then_inc(out_ready, 1)


def tiles(w):
    k, n = w.shape
    return w.reshape(k // P, P, n // P, P).transpose(2, 1, 0, 3)


def lay_out(i):
    a = {n: np.asarray(v) for n, v in i.items()}
    cat, flat = np.concatenate, lambda t: t.reshape(t.shape[0], P, -1)
    wA, wB0, wB1, wM, wR, par = [], [], [], [], [], []
    per_part = lambda g: g.reshape(-1, P).T
    for l in range(L):
        for f in ("ffn1", "ffn2"):
            t = flat(tiles(a[f + "_w_in"][l]))
            wA.append(t.reshape(2, FC, P, -1).transpose(1, 0, 2, 3).reshape(2 * FC, P, -1))
            t = tiles(a[f + "_w_out"][l])
            for dst, x, y in ((wB0, 0, HALF[0]), (wB1, HALF[0], FC)):
                half = t[:, :, x:y].reshape(KD, P, 2, -1).transpose(0, 2, 1, 3)
                dst.append(half.reshape(2 * KD, P, -1))
        w = a["w_in"][l]
        at = {"q": 0, "ckv": 512, "iq": 640, "misc": 896, "z": 936, "qc": 1192, "gate": 1448}
        cols = [at["misc"], at["ckv"], at["iq"], at["iq"] + P, at["qc"], at["qc"] + P]
        cols += [at["q"] + P * c for c in range(4)] + [at["z"], at["z"] + P] + [at["gate"] + P * f for f in range(KD)]
        for f in range(KD):
            cols += [at["gate"] + D + P * f, at["gate"] + 2 * D + P * f]
        kv = a["w_mem_kv"][l]
        wM.append(flat(tiles(kv[:, 0:M])))
        wM.append(flat(kv[:, M:].reshape(2, 4, P, M).transpose(0, 2, 1, 3)))
        wM.append(cat([flat(tiles(w[:, c:c + P])) for c in cols]))
        wM.append(flat(tiles(a["w_out"][l])))
        wR.append(flat(cat([tiles(a["w_branch_b"][l]), tiles(a["w_branch_c"][l])], axis=2)))
        wR.append(flat(tiles(a["w_branch_a"][l])))
        after = a["ffn1_norm"][l + 1] if l + 1 < L else a["final_norm"]
        par.append(cat([
            per_part(a["mix_norm"][l]), per_part(a["ffn2_norm"][l]), per_part(after), per_part(a["mem_norm"][l]),
            per_part(a["kv_norm"][l]), per_part(a["pool_scale"][l]),
            a["w_pool"][l].reshape(2, 2, 64, 64).transpose(1, 2, 0, 3).reshape(P, -1),
            a["w_uk"][l].transpose(1, 2, 0).reshape(4, P, R).transpose(1, 0, 2).reshape(P, -1),
            a["w_uv"][l].reshape(R, -1)], axis=1)[None])
    const, hot = constants()
    const[:, K_GAIN:K_GAIN + KD] = per_part(a["ffn1_norm"][0])
    token = lambda x: np.ascontiguousarray(x[0].T.reshape(KD, P, -1).transpose(1, 0, 2))
    arrays = {"xT": token(a["x"]), "memT": token(a["mem"]), "wA": cat(wA), "wB0": cat(wB0), "wB1": cat(wB1),
              "wM": cat(wM), "wR": cat(wR), "par": cat(par), "const": const, "hot": hot, "rel": a["rel_bias"]}
    return {n: np.ascontiguousarray(v) for n, v in arrays.items()}


def kernel(**inputs):
    import concourse.bacc as _bacc
    from concourse.bass_utils import run_bass_kernel_spmd as _run

    nc = _bacc.Bacc("TRN2", target_bir_lowering=False, num_devices=1)
    arrays = {f"in_{n}": v for n, v in lay_out(inputs).items()}
    args = [nc.dram_tensor(n, v.shape, F32, kind="ExternalInput").ap() for n, v in arrays.items()]
    out = nc.dram_tensor("outT", (P, KD, T), F32, kind="ExternalOutput").ap()
    bias_rows = nc.dram_tensor("bias_rows", (H, P, NBIAS), F32, kind="Internal").ap()
    trunk(nc, *args, out, bias_rows)
    r = _run(nc, [arrays], core_ids=[0])
    return np.ascontiguousarray(r.results[0]["outT"].transpose(2, 1, 0).reshape(T, D))[None]
```
